# Optimizing a Trainium2 kernel written in Bass

```python
import math
import jax, jax.numpy as jnp
from jax import lax
import numpy as np

D_MODEL = 1024
BATCH = 1
SEQ = 256
DEPTH = 2

GRID_W = 64
CTX_LEN = 256
Q_BLOCK = 128
ROPE_BASE = 10000.0
NORM_EPS = 1e-6

H_A = 8
N_A = 64
RW = H_A * N_A
DECAY_LORA = 64
ICLR_LORA = 64
GATE_LORA = 128
GN_EPS = 64e-5
RWKV_COLS = 3 * RW + 2 * DECAY_LORA + 2 * ICLR_LORA + GATE_LORA

H_B = 4
DIFF_HD = 64
DIFF_QK = H_B * 2 * DIFF_HD
DIFF_V = H_B * 2 * DIFF_HD
DIFF_COLS = 2 * DIFF_QK + DIFF_V

H_C = 8
Q_LORA = 384
KV_LORA = 256
MLA_NOPE = 64
MLA_ROPE = 32
MLA_V = 64
MLA_COLS = Q_LORA + KV_LORA + MLA_ROPE

N_BRANCH = 3
BRANCH_W = RW
GATE_COLS = N_BRANCH * D_MODEL
N_IN = RWKV_COLS + DIFF_COLS + MLA_COLS + GATE_COLS
D_FF = -(-8 * D_MODEL // (3 * 256)) * 256

kernel_name = 'hybrid_rwkv7_diffattn_mla_prefix_dit_block'

def rms_norm(x, g):
    xf = x.astype(jnp.float32)
    return (xf * lax.rsqrt(jnp.mean(xf * xf, axis=-1, keepdims=True) + NORM_EPS)).astype(x.dtype) * g

def modulate(h, shift, scale):
    return h * (1 + scale) + shift

def split_cols(z, sizes):
    idx, acc = [], 0
    for s in sizes[:-1]:
        acc += s
        idx.append(acc)
    return jnp.split(z, idx, axis=-1)

def axial_rope_tables(rows, rot_dim, dtype):
    row = jnp.repeat(jnp.arange(rows, dtype=jnp.float32), GRID_W)
    col = jnp.tile(jnp.arange(GRID_W, dtype=jnp.float32), rows)
    n_freq = rot_dim // 4
    inv_freq = ROPE_BASE ** (-jnp.arange(n_freq, dtype=jnp.float32) / n_freq)
    ang = jnp.concatenate([row[:, None] * inv_freq, col[:, None] * inv_freq], axis=-1)
    return jnp.cos(ang).astype(dtype), jnp.sin(ang).astype(dtype)

def apply_rope(x, cos, sin):
    x1, x2 = jnp.split(x, 2, axis=-1)
    return jnp.concatenate([x1 * cos - x2 * sin, x2 * cos + x1 * sin], axis=-1)

def softmax_probs(q, k, scale):
    s = jnp.einsum('bhqd,bhkd->bhqk', q, k).astype(jnp.float32) * scale
    return jax.nn.softmax(s, axis=-1)

def sweep_query_blocks(fn, q):
    B, H, T = q.shape[:3]
    nb = T // Q_BLOCK
    qb = jnp.moveaxis(q.reshape((B, H, nb, Q_BLOCK) + q.shape[3:]), 2, 0)
    out = lax.map(fn, qb)
    return jnp.moveaxis(out, 0, 2).reshape(B, H, T, out.shape[-1])

def centred_token_shift(z, mu_prev, mu_next):
    prev = jnp.pad(z[:, :-1], ((0, 0), (1, 0), (0, 0)))
    nxt = jnp.pad(z[:, 1:], ((0, 0), (0, 1), (0, 0)))
    return z + mu_prev * (prev - z) + mu_next * (nxt - z)

def rwkv7_prepare(z, mu, w0, w2, a0, a2, g2, k_k, k_a):
    B, T, _ = z.shape
    z = centred_token_shift(z, mu[0], mu[1])
    r, k, v, wd_f, wd_b, ad_f, ad_b, gd = split_cols(
        z, [RW, RW, RW, DECAY_LORA, DECAY_LORA, ICLR_LORA, ICLR_LORA, GATE_LORA])
    heads = lambda t: t.reshape(B, T, H_A, N_A).astype(jnp.float32)
    kk = heads(k * k_k)
    kk = kk / jnp.maximum(jnp.sqrt(jnp.sum(kk * kk, axis=-1, keepdims=True)), 1e-12)
    dirs = []
    for d, (wd, ad) in enumerate(((wd_f, ad_f), (wd_b, ad_b))):
        w_log = -jax.nn.softplus(-(w0[d] + jnp.tanh(wd) @ w2[d]).astype(jnp.float32)) - 0.5
        decay = jnp.exp(-jnp.exp(w_log))
        a = jax.nn.sigmoid(a0[d] + ad @ a2[d])
        k_dir = k * (1 + (a - 1) * k_a)
        dirs.append((heads(decay), heads(k_dir), kk * heads(a)))
    g = jax.nn.sigmoid(gd) @ g2
    return heads(r), heads(v), kk, g, dirs

def wkv7_scan(state0, r, v, kk, decay, k, b, reverse, emit):
    xs = tuple(jnp.moveaxis(t, 1, 0) for t in (r, decay, k, v, -kk, b))

    def step(S, inp):
        r_t, w_t, k_t, v_t, a_t, b_t = inp
        sa = jnp.einsum('bhvk,bhk->bhv', S, a_t)
        S = S * w_t[:, :, None, :] + sa[..., None] * b_t[:, :, None, :] + v_t[..., None] * k_t[:, :, None, :]
        return S, (jnp.einsum('bhvk,bhk->bhv', S, r_t) if emit else None)

    state, ys = lax.scan(step, state0, xs, reverse=reverse)
    return state, (jnp.moveaxis(ys, 0, 1) if emit else None)

def rwkv7_readout(ys, r, v, dirs, g, r_k, ln_w, ln_b):
    B, T = r.shape[:2]
    y = ys[0] + ys[1]
    mean = jnp.mean(y, axis=-1, keepdims=True)
    var = jnp.mean(jnp.square(y - mean), axis=-1, keepdims=True)
    y = (y - mean) * lax.rsqrt(var + GN_EPS)
    rk = r_k.astype(jnp.float32)
    bonus = (jnp.sum(r * dirs[0][1] * rk, axis=-1, keepdims=True)
             + jnp.sum(r * dirs[1][1] * rk, axis=-1, keepdims=True)) * v
    y = y.reshape(B, T, RW) * ln_w + ln_b + bonus.reshape(B, T, RW)
    return y.astype(g.dtype) * g

def rwkv7_branch(z_lat, z_ctx, mu, w0, w2, a0, a2, g2, k_k, k_a, r_k, ln_w, ln_b, emit_ctx):
    p = (mu, w0, w2, a0, a2, g2, k_k, k_a)
    r_l, v_l, kk_l, g_l, dirs_l = rwkv7_prepare(z_lat, *p)
    r_c, v_c, kk_c, g_c, dirs_c = rwkv7_prepare(z_ctx, *p)
    state0 = jnp.zeros((z_lat.shape[0], H_A, N_A, N_A), jnp.float32)
    ys_l, ys_c = [], []
    for d, reverse in enumerate((False, True)):
        state_c, y_c = wkv7_scan(state0, r_c, v_c, kk_c, *dirs_c[d], reverse, emit_ctx)
        _, y_l = wkv7_scan(state_c, r_l, v_l, kk_l, *dirs_l[d], reverse, True)
        ys_l.append(y_l)
        ys_c.append(y_c)
    out_l = rwkv7_readout(ys_l, r_l, v_l, dirs_l, g_l, r_k, ln_w, ln_b)
    out_c = rwkv7_readout(ys_c, r_c, v_c, dirs_c, g_c, r_k, ln_w, ln_b) if emit_ctx else None
    return out_l, out_c

def diff_attention_branch(z_lat, z_ctx, lam_vecs, subln_g, layer_idx, rope, emit_ctx):
    lambda_init = 0.8 - 0.6 * math.exp(-0.3 * layer_idx)
    lv = lam_vecs.astype(jnp.float32)
    lam = jnp.exp(jnp.sum(lv[0] * lv[1])) - jnp.exp(jnp.sum(lv[2] * lv[3])) + lambda_init
    scale = DIFF_HD ** -0.5

    def qkv(z):
        B, T, _ = z.shape
        q, k, v = split_cols(z, [DIFF_QK, DIFF_QK, DIFF_V])
        return (q.reshape(B, T, H_B, 2, DIFF_HD), k.reshape(B, T, H_B, 2, DIFF_HD),
                v.reshape(B, T, H_B, 2 * DIFF_HD))

    q_l, k_l, v_l = qkv(z_lat)
    q_c, k_c, v_c = qkv(z_ctx)
    cos, sin = rope[0][None, :, None, None, :], rope[1][None, :, None, None, :]
    q_l = apply_rope(q_l, cos, sin)
    k_l = apply_rope(k_l, cos, sin)
    bh = lambda t: jnp.moveaxis(t, 2, 1)
    k_all = bh(jnp.concatenate([k_c, k_l], axis=1))
    v_all = bh(jnp.concatenate([v_c, v_l], axis=1))

    def attend(q, k, v):
        p1 = softmax_probs(q[..., 0, :], k[..., 0, :], scale)
        p2 = softmax_probs(q[..., 1, :], k[..., 1, :], scale)
        return jnp.einsum('bhqk,bhkd->bhqd', (p1 - lam * p2).astype(v.dtype), v)

    def finish(o):
        o = rms_norm(o, subln_g) * (1.0 - lambda_init)
        B, H, T, E = o.shape
        return jnp.moveaxis(o, 1, 2).reshape(B, T, H * E)

    out_l = finish(sweep_query_blocks(lambda qb: attend(qb, k_all, v_all), bh(q_l)))
    out_c = finish(attend(bh(q_c), bh(k_c), bh(v_c))) if emit_ctx else None
    return out_l, out_c

def mla_branch(z_lat, z_ctx, q_norm_g, kv_norm_g, w_uq, w_uk, w_uv, rope, emit_ctx):
    scale = (MLA_NOPE + MLA_ROPE) ** -0.5

    def project(z, rope_tables):
        B, T, _ = z.shape
        cq, ckv, k_rope = split_cols(z, [Q_LORA, KV_LORA, MLA_ROPE])
        q = (rms_norm(cq, q_norm_g) @ w_uq).reshape(B, T, H_C, MLA_NOPE + MLA_ROPE)
        ckv = rms_norm(ckv, kv_norm_g)
        k_nope = (ckv @ w_uk).reshape(B, T, H_C, MLA_NOPE)
        v = (ckv @ w_uv).reshape(B, T, H_C, MLA_V)
        q_nope, q_rope = jnp.split(q, [MLA_NOPE], axis=-1)
        if rope_tables is not None:
            cos, sin = rope_tables
            q_rope = apply_rope(q_rope, cos[None, :, None, :], sin[None, :, None, :])
            k_rope = apply_rope(k_rope, cos[None], sin[None])
        k = jnp.concatenate([k_nope, jnp.broadcast_to(k_rope[:, :, None, :], (B, T, H_C, MLA_ROPE))], axis=-1)
        q = jnp.concatenate([q_nope, q_rope], axis=-1)
        return jnp.moveaxis(q, 2, 1), jnp.moveaxis(k, 2, 1), jnp.moveaxis(v, 2, 1)

    q_l, k_l, v_l = project(z_lat, rope)
    q_c, k_c, v_c = project(z_ctx, None)
    k_all = jnp.concatenate([k_c, k_l], axis=2)
    v_all = jnp.concatenate([v_c, v_l], axis=2)

    def attend(q, k, v):
        return jnp.einsum('bhqk,bhkd->bhqd', softmax_probs(q, k, scale).astype(v.dtype), v)

    def finish(o):
        B, H, T, E = o.shape
        return jnp.moveaxis(o, 1, 2).reshape(B, T, H * E)

    out_l = finish(sweep_query_blocks(lambda qb: attend(qb, k_all, v_all), q_l))
    out_c = finish(attend(q_c, k_c, v_c)) if emit_ctx else None
    return out_l, out_c

def merge_branches(ys, gate_logits, w_branch, w_out):
    B, T, _ = gate_logits.shape
    y = jnp.stack(ys, axis=2)
    proj = jnp.einsum('btge,ged->btgd', y, w_branch)
    gates = jax.nn.sigmoid(gate_logits.reshape(B, T, N_BRANCH, D_MODEL))
    return jnp.sum(gates * proj, axis=2) @ w_out

def swiglu(h, w_gate, w_up, w_down):
    return (jax.nn.silu(h @ w_gate) * (h @ w_up)) @ w_down

def setup_inputs(seed: int = 0) -> dict:
    key = jax.random.key(seed)
    keys = jax.random.split(key, 40)
    counter = [0]

    def nk():
        k = keys[counter[0]]
        counter[0] += 1
        return k

    nrm = lambda shape, s: jax.random.normal(nk(), shape, jnp.float32) * s
    uni = lambda shape, lo, hi: jax.random.uniform(nk(), shape, jnp.float32, lo, hi)
    L, D = DEPTH, D_MODEL
    return {
        'x': nrm((BATCH, SEQ, D), 1.0),
        'c': nrm((BATCH, D), 1.0),
        'ctx': nrm((BATCH, CTX_LEN, D), 1.0),
        'c_ctx': nrm((D,), 1.0),
        'ada_w': nrm((L, D, 6 * D), D ** -0.5),
        'ada_b': nrm((L, 6 * D), 0.02),
        'norm1_g': 1.0 + nrm((L, D), 0.02),
        'norm2_g': 1.0 + nrm((L, D), 0.02),
        'w_in': nrm((L, D, N_IN), D ** -0.5),
        'rwkv_shift_mu': uni((L, 2, RWKV_COLS), 0.0, 0.5),
        'rwkv_w0': uni((L, 2, RW), -6.0, 1.0),
        'rwkv_w2': nrm((L, 2, DECAY_LORA, RW), 0.5 * DECAY_LORA ** -0.5),
        'rwkv_a0': nrm((L, 2, RW), 0.1),
        'rwkv_a2': nrm((L, 2, ICLR_LORA, RW), 0.5 * ICLR_LORA ** -0.5),
        'rwkv_g2': nrm((L, GATE_LORA, RW), GATE_LORA ** -0.5),
        'rwkv_k_k': 0.85 + nrm((L, RW), 0.02),
        'rwkv_k_a': 1.0 + nrm((L, RW), 0.02),
        'rwkv_r_k': -0.04 + nrm((L, H_A, N_A), 0.02),
        'rwkv_ln_w': 1.0 + nrm((L, RW), 0.02),
        'rwkv_ln_b': nrm((L, RW), 0.02),
        'diff_lambda': nrm((L, 4, DIFF_HD), 0.1),
        'diff_subln_g': 1.0 + nrm((L, 2 * DIFF_HD), 0.02),
        'mla_q_norm_g': 1.0 + nrm((L, Q_LORA), 0.02),
        'mla_kv_norm_g': 1.0 + nrm((L, KV_LORA), 0.02),
        'mla_w_uq': nrm((L, Q_LORA, H_C * (MLA_NOPE + MLA_ROPE)), Q_LORA ** -0.5),
        'mla_w_uk': nrm((L, KV_LORA, H_C * MLA_NOPE), KV_LORA ** -0.5),
        'mla_w_uv': nrm((L, KV_LORA, H_C * MLA_V), KV_LORA ** -0.5),
        'w_branch': nrm((L, N_BRANCH, BRANCH_W, D), BRANCH_W ** -0.5),
        'w_out': nrm((L, D, D), D ** -0.5),
        'ffn_w_gate': nrm((L, D, D_FF), D ** -0.5),
        'ffn_w_up': nrm((L, D, D_FF), D ** -0.5),
        'ffn_w_down': nrm((L, D_FF, D), D_FF ** -0.5),
        'final_norm_g': 1.0 + nrm((D,), 0.02),
    }

def reference(x, c, ctx, c_ctx, ada_w, ada_b, norm1_g, norm2_g, w_in, rwkv_shift_mu, rwkv_w0, rwkv_w2,
              rwkv_a0, rwkv_a2, rwkv_g2, rwkv_k_k, rwkv_k_a, rwkv_r_k, rwkv_ln_w, rwkv_ln_b, diff_lambda,
              diff_subln_g, mla_q_norm_g, mla_kv_norm_g, mla_w_uq, mla_w_uk, mla_w_uv, w_branch, w_out,
              ffn_w_gate, ffn_w_up, ffn_w_down, final_norm_g):
    B, T, D = x.shape
    rows = T // GRID_W
    rope_b = axial_rope_tables(rows, DIFF_HD, x.dtype)
    rope_c = axial_rope_tables(rows, MLA_ROPE, x.dtype)
    col_sizes = [RWKV_COLS, DIFF_COLS, MLA_COLS, GATE_COLS]
    sc = jax.nn.silu(c)
    scc = jax.nn.silu(c_ctx)
    x_lat, x_ctx = x, ctx
    for l in range(DEPTH):
        emit_ctx = l < DEPTH - 1
        sh1, s1, g1, sh2, s2, g2 = [m[:, None, :] for m in jnp.split(sc @ ada_w[l] + ada_b[l], 6, axis=-1)]
        csh1, cs1, cg1, csh2, cs2, cg2 = jnp.split(scc @ ada_w[l] + ada_b[l], 6, axis=-1)

        h_lat = modulate(rms_norm(x_lat, norm1_g[l]), sh1, s1)
        h_ctx = modulate(rms_norm(x_ctx, norm1_g[l]), csh1, cs1)
        za, zb, zc, zg = split_cols(h_lat @ w_in[l], col_sizes)
        za_c, zb_c, zc_c, zg_c = split_cols(h_ctx @ w_in[l], col_sizes)
        ya, ya_c = rwkv7_branch(za, za_c, rwkv_shift_mu[l], rwkv_w0[l], rwkv_w2[l], rwkv_a0[l], rwkv_a2[l],
                                rwkv_g2[l], rwkv_k_k[l], rwkv_k_a[l], rwkv_r_k[l], rwkv_ln_w[l], rwkv_ln_b[l],
                                emit_ctx)
        yb, yb_c = diff_attention_branch(zb, zb_c, diff_lambda[l], diff_subln_g[l], l, rope_b, emit_ctx)
        yc, yc_c = mla_branch(zc, zc_c, mla_q_norm_g[l], mla_kv_norm_g[l], mla_w_uq[l], mla_w_uk[l],
                              mla_w_uv[l], rope_c, emit_ctx)
        x_lat = x_lat + g1 * merge_branches((ya, yb, yc), zg, w_branch[l], w_out[l])

        h2 = modulate(rms_norm(x_lat, norm2_g[l]), sh2, s2)
        x_lat = x_lat + g2 * swiglu(h2, ffn_w_gate[l], ffn_w_up[l], ffn_w_down[l])

        if emit_ctx:
            x_ctx = x_ctx + cg1 * merge_branches((ya_c, yb_c, yc_c), zg_c, w_branch[l], w_out[l])
            h2c = modulate(rms_norm(x_ctx, norm2_g[l]), csh2, cs2)
            x_ctx = x_ctx + cg2 * swiglu(h2c, ffn_w_gate[l], ffn_w_up[l], ffn_w_down[l])
    return rms_norm(x_lat, final_norm_g)


_drawn_inputs = setup_inputs


def setup_inputs(seed=0):
    import zlib

    import numpy as np

    out = dict(_drawn_inputs(seed))
    spreads = {}
    factors = {'norm1_g': 4.845,
     'norm2_g': 2.922,
     'rwkv_w2': 2.91,
     'rwkv_a0': 6.861,
     'rwkv_ln_w': 8.0,
     'rwkv_ln_b': 8.0,
     'diff_subln_g': 8.0,
     'mla_q_norm_g': 8.0,
     'mla_kv_norm_g': 8.0,
     'final_norm_g': 2.718}
    for name, (base, spread) in spreads.items():
        noise = np.random.default_rng([zlib.crc32(name.encode()), seed]).standard_normal(out[name].shape)
        drawn = base * np.exp(spread * noise) if base else spread * noise
        out[name] = __import__('jax').numpy.asarray(drawn.astype(out[name].dtype))
    for name, factor in factors.items():
        out[name] = (out[name] * factor).astype(out[name].dtype)
    return out
```

```python
import math
from contextlib import ExitStack

import numpy as np
import concourse.bass as bass
from concourse import mybir

F32 = mybir.dt.float32
ALU = mybir.AluOpType
ACT = mybir.ActivationFunctionType
AX = mybir.AxisListType

P = 128
DEPTH, D, KT = 2, 1024, 8
T, HALF = 512, 256
C = 64
NCH = T // C
RW, RT = 512, 4
W_COLS = 7200
A0, B0, C0, G0 = 0, 1920, 1920 + 1536, 1920 + 1536 + 672
DFF, FT = 2816, 22
EPS = 1e-6
GN_EPS = 64e-5
DECAY = math.exp(-0.5)
NBANK = 8
NW, WSLOT = 4, 2048
LAT = slice(HALF, T)
DIFF_SCALE = 64 ** -0.5
MLA_SCALE = 96 ** -0.5

IDENT, MASK, ONES, BONES, PERM, PERM32, COSB, SINB, COSC, SINC, STARTS = (
    0, 128, 256, 384, 512, 640, 768, 1024, 1280, 1536, 1792)
NTAB = STARTS + NCH * (C + 1)
MU, N1, N2, W0, A0C, KKC, KAC, RKC, LNW, LNB, SUBG, QNG, KVG, NPAR = (
    0, 30, 38, 46, 54, 62, 66, 70, 74, 78, 82, 83, 86, 88)
ADAB, FING, CVEC, CCTX, NPAR2 = 0, 48, 56, 64, 72


def tables():
    t = np.zeros((P, NTAB), np.float32)
    i = np.arange(P)
    t[:, IDENT:IDENT + P] = np.eye(P)
    s, q = i[:, None] % 64, i[None, :]
    t[:, MASK:MASK + P] = np.where(q < 64, s < q, s <= q - 64)
    t[:, ONES:ONES + P] = 1
    t[:, BONES:BONES + P] = (i[:, None] // 64) == (i[None, :] // 64)
    for b in range(2):
        for j in range(32):
            t[64 * b + 32 + j, PERM + 64 * b + j] = -1
            t[64 * b + j, PERM + 64 * b + 32 + j] = 1
    for j in range(16):
        t[64 + 16 + j, PERM32 + j] = -1
        t[64 + j, PERM32 + 16 + j] = 1
    tok = np.arange(HALF)
    row, col = (tok // 64).astype(np.float32), (tok % 64).astype(np.float32)
    for rot, c0, s0 in ((64, COSB, SINB), (32, COSC, SINC)):
        n = rot // 4
        inv = (np.float32(10000.0) ** (-np.arange(n, dtype=np.float32) / np.float32(n))).astype(np.float32)
        ang = np.concatenate([row[:, None] * inv, col[:, None] * inv], -1).T
        cs, sn = np.cos(ang, dtype=np.float32), np.sin(ang, dtype=np.float32)
        if rot == 64:
            t[:, c0:c0 + HALF], t[:, s0:s0 + HALF] = np.tile(cs, (4, 1)), np.tile(sn, (4, 1))
        else:
            t[64:96, c0:c0 + HALF], t[64:96, s0:s0 + HALF] = np.tile(cs, (2, 1)), np.tile(sn, (2, 1))
    t[:, STARTS:].reshape(P, NCH, C + 1)[:, :, 0] = 1
    return t


class Plan:

    def __init__(self, known=None):
        self.known = known
        self.count, self.at, self.jobs, self.release = {}, {}, {}, {}

    def start(self, sem_of):
        self.sem_of = sem_of

    def mark(self, name, *key, by=1):
        self.count[name] = self.count.get(name, 0) + by
        self.at[(name, *key)] = self.count[name]
        return self.sem_of(name), by

    def dma(self, name, *key):
        return self.mark(name, *key, by=16)

    def when(self, name, *key):
        return self.sem_of(name), (self.known.at[(name, *key)] if self.known else 1)

    def job(self, *key):
        n = len(self.jobs)
        self.jobs[key] = n
        return n

    def index(self, *key):
        return self.known.jobs[key] if self.known else 0

    def full(self, *key):
        n = self.index(*key)
        return self.sem_of(f"psum_full{n % NBANK}"), n // NBANK + 1

    def drained(self, *key):
        n = self.index(*key)
        return self.sem_of(f"psum_drained{n % NBANK}"), n // NBANK + 1

    def released(self, n):
        key = self.known.release[n] if self.known else ("x",)
        return self.when(*key[1:]) if key[0] == "mark" else self.full(*key)

    def drain(self, *key):
        return self.sem_of(f"psum_drained{self.index(*key) % NBANK}"), 1


def weight_chunks(w, l):
    win = w["w_in"][l]

    def cols(m, a, n):
        return m[:, a:a + n].rearrange("(k p) n -> p k n", p=P)

    for j in range(24):
        yield ("ada", j), 8, 256, [(0, 256, 0, 8, cols(w["ada_w"][l], 256 * j, 256))]
    for j in range(6):
        yield ("B", j), 8, 256, [(0, 256, 0, 8, cols(win, B0 + 256 * j, 256))]
    for j, n in enumerate((256, 256, 160)):
        yield ("C", j), 8, n, [(0, n, 0, 8, cols(win, C0 + 256 * j, n))]
    for j in range(2):
        yield ("uq", j), 3, 384, [(0, 384, 0, 3, cols(w["mla_w_uq"][l], 384 * j, 384))]
    yield ("uk",), 2, 512, [(0, 512, 0, 2, cols(w["mla_w_uk"][l], 0, 512))]
    yield ("uv",), 2, 512, [(0, 512, 0, 2, cols(w["mla_w_uv"][l], 0, 512))]
    for j in range(8):
        n = 256 if j < 7 else 128
        yield ("A", j), 8, n, [(0, n, 0, 8, cols(win, A0 + 256 * j, n))]
    for d in range(8):
        yield ("G12", d), 8, 256, [(P * g, P * g + P, 0, 8, cols(win, G0 + D * (1 + g) + P * d, P))
                                   for g in range(2)]
        wb = w["w_branch"][l].rearrange("g e n -> (g e) n")
        yield ("W12", d), 8, P, [(0, P, 0, 8, cols(wb[RW:3 * RW], P * d, P))]
    for d in range(8):
        wb = w["w_branch"][l].rearrange("g e n -> (g e) n")
        yield ("GW0", d), 12, P, [(0, P, 0, 8, cols(win, G0 + P * d, P)),
                                  (0, P, 8, 12, cols(wb[0:RW], P * d, P))]
    for j in range(4):
        yield ("O", j), 8, 256, [(0, 256, 0, 8, cols(w["w_out"][l], 256 * j, 256))]
    for j in range(11):
        yield ("FG", j), 8, 256, [(0, 256, 0, 8, cols(w["ffn_w_gate"][l], 256 * j, 256))]
        yield ("FU", j), 8, 256, [(0, 256, 0, 8, cols(w["ffn_w_up"][l], 256 * j, 256))]
    for d in range(4):
        for kc, (k0, k1) in enumerate(((0, 8), (8, 16), (16, 22))):
            yield ("FD", d, kc), k1 - k0, 256, [
                (0, 256, 0, k1 - k0, cols(w["ffn_w_down"][l][P * k0:P * k1, :], 256 * d, 256))]


def attention_units(l):
    tiles = range(4) if l == 0 else range(2, 4)
    return ([("diff", h, q, 2 if q < 2 else 4) for h in range(4) for q in tiles]
            + [("mla", h, q, 2 if q < 2 else 4) for h in range(8) for q in tiles])


def build(nc, w, tab, out, plan, ctx):
    sems = {}

    def sem_of(name):
        if name not in sems:
            sems[name] = ctx.enter_context(nc.semaphore(name))
        return sems[name]

    plan.start(sem_of)
    mark, dma, when, full, drained, drain = plan.mark, plan.dma, plan.when, plan.full, plan.drained, plan.drain

    def sb(name, shape):
        return ctx.enter_context(nc.sbuf_tensor(name, shape, F32))

    def dram(name, shape):
        return nc.dram_tensor(name, shape, F32, kind="Internal").ap()

    PS = [ctx.enter_context(nc.psum_tensor(f"ps{b}", [P, 512], F32)) for b in range(NBANK)]

    def bank(*key):
        return PS[plan.index(*key) % NBANK]

    cst = sb("cst", [P, NTAB])
    ring = sb("ring", [P, NW, WSLOT])
    prow = sb("prow", [P, 2, P])
    par = sb("par", [P, DEPTH, NPAR])
    par2 = sb("par2", [P, DEPTH, NPAR2])
    csil = sb("csil", [P, KT, 2])
    mods = sb("mods", [P, 48, 2])
    gsc = sb("gsc", [P, 2, KT, 2])
    lora = sb("lora", [P, 3, RW])
    lamv = sb("lamv", [P, 256])
    lam = sb("lam", [P, 8])
    subg = sb("subg", [P, 1])
    mu0 = sb("mu0", [P, 15])
    kaneg = sb("kaneg", [P, 4])
    smax = sb("smax", [P, 2, 64])
    ssum = sb("ssum", [P, 2, 64])
    rsum = sb("rsum", [P, 2, 64])
    dend = sb("dend", [P, 8, NCH])
    ARENA = 155 * 256
    arena = sb("arena", [P, ARENA])

    def view(kb, shape):
        o, n = int(kb * 256), int(np.prod(shape))
        assert o + n <= ARENA
        v = arena[:, o:o + n]
        names = "abcd"[:len(shape)]
        if len(shape) == 1:
            return v
        return v.rearrange("p (%s) -> p %s" % (" ".join(names), " ".join(names)),
                           **{n: s for n, s in zip(names, shape)})

    H = view(0, [KT, T])
    X = view(16, [KT, T])
    M = view(16, [KT, T])
    YB = view(32, [4, T])
    YC = view(40, [4, T])
    QK = view(48, [8, T])
    VD = view(64, [4, T])
    ZC = view(72, [6, T])
    MQ = view(84, [8, T])
    MK = view(100, [8, T])
    MV = view(116, [4, T])
    PR = view(124, [2, 2, T])
    PT = view(132, [2, T])
    ROT = view(136, [2, HALF])
    SQ = view(138, [2, T])
    RS = view(153, [T])
    TOK = view(144, [KT * P])
    ZS = view(48, [15, T])
    KK = view(78, [4, T])
    BV = view(86, [4, T])
    SG = view(94, [T])
    AI = view(96, [T])
    TA, TB = view(98, [T]), view(100, [T])
    W65 = view(102, [NCH * (C + 1)])
    E65 = view(104.25, [NCH * (C + 1)])
    RI = view(106.5, [T])
    GT = view(106.5, [T])
    AR = view(109, [2, NCH, P])
    BK = view(117, [NCH, P])
    BH = view(121, [NCH, P])
    BKT = view(125, [NCH, P])
    AS = view(129, [2, 4, P])
    GS = view(133, [2, T])
    VT = view(94, [T])
    NB = view(137, [C, C])
    NT = view(112, [C * C // 4])
    cA = view(48, [2, 16, P])
    cX = view(64, [2, 16, C])
    cR = view(134, [2, 8, P])
    cB = view(94, [2, 8, P])
    cV = view(102, [2, 2, T])
    S = view(110, [8, P])
    R = view(114, [8, P])
    Y = view(118, [2, 4, T])
    YA = view(48, [4, T])
    X2 = view(56, [KT, T])
    FH = view(72, [FT, T])
    RT1, RT2, RT3 = view(94, [T]), view(96, [T]), view(98, [T])
    RO = [view(94, [4, T]), view(102, [4, T])]
    GATE = view(136, [2, T])
    FSG = view(116, [2, T])
    FST = view(120, [2, T])

    ident, ones, bones = cst[:, IDENT:IDENT + P], cst[:, ONES:ONES + P], cst[:, BONES:BONES + P]
    xdram = dram("x_spill", [P, KT * T])
    a_dram = dram("a_spill", [NCH, P, 16, P])
    r_dram = dram("r_spill", [NCH, P, 8, P])
    b_dram = dram("b_spill", [NCH, P, 8, P])
    v_dram = dram("v_spill", [T, RW])
    vr_dram = dram("v_reversed", [T, RW])
    i_dram = dram("i_spill", [P, C, C])

    def directed(ap, d):
        v = ap.rearrange("p (h c t) -> p h c t", h=2, t=C)
        return v[:, :, ::-1, ::-1] if d else v

    def chunked(ap):
        return ap.rearrange("p (h c) t -> p h c t", h=2)

    def sides(l):
        return (0, 1) if l == 0 else (1,)

    def outs(l):
        return slice(0, T) if l == 0 else LAT

    block = ctx.enter_context(nc.Block())

    @block.sync
    def _(sp):
        sp.dma_start(cst[:, :], tab).then_inc(*dma("tables"))
        n = 0
        for l in range(DEPTH):
            if l:
                sp.wait_ge(*drained("par2", l - 1))
                sp.wait_ge(*when("lam", l - 1))
                sp.wait_ge(*full("lora_g", l - 1, 3))
            rows = [("rwkv_shift_mu", MU, 30), ("norm1_g", N1, 8), ("norm2_g", N2, 8), ("rwkv_w0", W0, 8),
                    ("rwkv_a0", A0C, 8), ("rwkv_k_k", KKC, 4), ("rwkv_k_a", KAC, 4), ("rwkv_r_k", RKC, 4),
                    ("rwkv_ln_w", LNW, 4), ("rwkv_ln_b", LNB, 4), ("diff_subln_g", SUBG, 1),
                    ("mla_q_norm_g", QNG, 3), ("mla_kv_norm_g", KVG, 2)]
            for name, r0, nr in rows:
                src = w[name][l]
                if len(src.shape) == 2:
                    src = src.rearrange("a b -> (a b)")
                sp.dma_start(prow[r0:r0 + nr, 0, :], src.rearrange("(r n) -> r n", n=P)).then_inc(*dma("prow", l))
            for src, r0, nr in ((w["ada_b"][l], ADAB, 48), (w["final_norm_g"], FING, 8),
                                (w["c"][0], CVEC, 8), (w["c_ctx"], CCTX, 8)):
                sp.dma_start(prow[r0:r0 + nr, 1, :], src.rearrange("(r n) -> r n", n=P)).then_inc(*dma("prow", l))
            sp.dma_start(lamv[:, :], w["diff_lambda"][l].rearrange("a b -> (a b)").partition_broadcast(P)).then_inc(*dma("lamv", l))
            for i, name in enumerate(("rwkv_w2", "rwkv_a2")):
                sp.dma_start(lora[:, i, :], w[name][l].rearrange("d k n -> (d k) n")).then_inc(*dma("lora", l))
            sp.dma_start(lora[:, 2, :], w["rwkv_g2"][l]).then_inc(*dma("lora", l))
            for name, nk, nn, parts in weight_chunks(w, l):
                if n >= NW:
                    sp.wait_ge(*plan.released(n - NW))
                slot = ring[:, n % NW, 0:nk * nn].rearrange("p (k n) -> p k n", n=nn)
                for c0, c1, k0, k1, src in parts:
                    sp.dma_start(slot[:, k0:k1, c0:c1], src).then_inc(*dma(f"weights_in{n % NW}", n))
                n += 1

    @block.gpsimd
    def _(pool):
        for i in range(4):
            if i:
                pool.wait_ge(*full("xin", i - 1, 1))
            src = w["ctx"][0] if i < 2 else w["x"][0]
            pool.dma_start(TOK, src[P * (i % 2):P * (i % 2) + P, :]).then_inc(*dma("tok", i))
        for l in range(DEPTH):
            for key in [("fd", l - 1, k) for k in range(KT)] if l else [("xin", i, h) for i in range(4) for h in range(2)]:
                pool.wait_ge(*drained(*key))
            pool.dma_start(xdram, X.rearrange("p k t -> p (k t)")).then_inc(*dma("x_spilled", l))
            for c in range(NCH):
                pool.wait_ge(*drained("vtok", l, c))
                pool.dma_start(v_dram[C * c:C * c + C, :], VT[0:C, :]).then_inc(*dma("v_spilled", l, c))
            for c in range(NCH):
                pool.wait_ge(*when("v_spilled", l, c))
            for h in range(2):
                rows = slice(HALF * h, HALF * h + HALF)
                src = v_dram[rows, :].rearrange("t (h v) -> h t v", h=8)[:, ::-1, :]
                pool.dma_start(vr_dram[rows, :].rearrange("t (h v) -> h t v", h=8), src).then_inc(*dma("v_reversed", l))
            for i in range(8):
                for g in range(4):
                    pool.wait_ge(*drained("A", l, i, g))
                    hh, half = g % 2, g // 2
                    pool.dma_start(a_dram[4 * half:4 * half + 4, :, 2 * i + hh, :].rearrange("c p n -> p c n"),
                                   AS[:, g % 2]).then_inc(*dma(f"a_spilled{g % 2}", l, i, g))
                pool.wait_ge(*drained("bkt", l, i, 1))
                pool.dma_start(b_dram[:, :, i, :].rearrange("c p n -> p c n"), BKT).then_inc(*dma("b_spilled", l, i))
                pool.dma_start(r_dram[:, :, i, :].rearrange("c p n -> p c n"), AR[:, i % 2]).then_inc(*dma("r_spilled", l, i))
            for g in range(2):
                pool.wait_ge(*when(f"a_spilled{g}", l, 7, 2 + g))
            for c in range(NCH):
                pool.dma_start(NB[16 * c:16 * c + 16], a_dram[c, 0:C, :, 0:C].rearrange("s u t -> u s t")).then_inc(*dma("nb_in", l))
            pool.wait_ge(*when("inverted", l))
            pool.dma_start(i_dram.rearrange("u s t -> u (s t)"), NB.rearrange("p s t -> p (s t)")).then_inc(*dma("inverse_out", l))
            pool.wait_ge(*when("inverse_out", l))
            pool.wait_ge(*when("b_spilled", l, 7))
            pool.wait_ge(*when("r_spilled", l, 7))
            pool.wait_ge(*when("v_reversed", l))
            for p in range(4):
                pool.wait_ge(*drained("bonus", l, p))
            for c in range(NCH):
                b = c % 2
                if c >= 2:
                    pool.wait_ge(*full("S", l, c - 2, 1))
                    if not (l and c - 2 < 4):
                        pool.wait_ge(*full("Y", l, c - 2, 1))
                name = f"chunk_in{b}"
                pool.dma_start(cA[:, b], a_dram[c]).then_inc(*dma(name, l, c))
                pool.dma_start(cX[0:C, b], i_dram[16 * c:16 * c + 16].rearrange("u s t -> s u t")).then_inc(*dma(name, l, c))
                pool.dma_start(cR[:, b], r_dram[c]).then_inc(*dma(name, l, c))
                pool.dma_start(cB[:, b], b_dram[c]).then_inc(*dma(name, l, c))
                pool.dma_start(cV[C:P, b, 0], v_dram[C * c:C * c + C, :]).then_inc(*dma(name, l, c))
                pool.dma_start(cV[C:P, b, 1], vr_dram[C * c:C * c + C, :]).then_inc(*dma(name, l, c))
            pool.wait_ge(*full("S", l, NCH - 1, 1))
            pool.wait_ge(*full("Y", l, NCH - 1, 1))
            pool.dma_start(X2.rearrange("p k t -> p (k t)"), xdram).then_inc(*dma("x_back", l))
        for i in range(2):
            pool.wait_ge(*drained("xout", i, 1))
            pool.dma_start(out[0, P * i:P * i + P, :], TOK).then_inc(*dma("stored", i))
            pool.wait_ge(*when("stored", i))

    @block.tensor
    def _(pe):
        chunk_no = [0]
        chunk_of = {}

        def job(*key):
            n = plan.job(*key)
            if n >= NBANK:
                pe.wait_ge(sem_of(f"psum_drained{n % NBANK}"), n // NBANK)
            return PS[n % NBANK]

        def done(*key):
            n = plan.jobs[key]
            return sem_of(f"psum_full{n % NBANK}"), 1

        def weights(l, *name):
            n = chunk_no[0]
            chunk_no[0] += 1
            got, nk, nn, _ = chunk_list[n]
            assert got == name, (got, name)
            pe.wait_ge(*when(f"weights_in{n % NW}", n))
            chunk_of[name] = n
            return ring[:, n % NW, 0:nk * nn].rearrange("p (k n) -> p k n", n=nn)

        def release(name, *key):
            plan.release[chunk_of[name]] = key

        chunk_list = [c for l in range(DEPTH) for c in weight_chunks(w, l)]

        def sum_rows(key, tiles, lhs, toks, stage):
            ps = job(*key)
            n = toks.stop - toks.start
            for k in range(tiles):
                pe.wait_ge(*when(stage, *key, k))
                mm = pe.matmul(ps[:, 0:n], lhs, SQ[:, k % 2, toks], start=(k == 0), stop=(k == tiles - 1))
                if k < tiles - 1:
                    mm.then_inc(*mark("squares_read", *key, k))
            mm.then_inc(*done(*key))

        def project(key, wt, c0, m, rhs, nk, ps_rows=slice(0, P), n=T):
            ps = job(*key)
            for k in range(nk):
                mm = pe.matmul(ps[ps_rows, 0:n], wt[:, k, c0:c0 + m], rhs(k), start=(k == 0), stop=(k == nk - 1))
            mm.then_inc(*done(*key))

        pe.wait_ge(*when("tables"))
        for i in range(4):
            pe.wait_ge(*when("tok", i))
            for h in range(2):
                ps = job("xin", i, h)
                for k in range(4):
                    mm = pe.transpose(ps[:, P * k:P * k + P], TOK[:, P * (4 * h + k):P * (4 * h + k) + P], ident)
                mm.then_inc(*done("xin", i, h))

        for l in range(DEPTH):
            o = outs(l)
            no = o.stop - o.start
            pe.wait_ge(*when("prow", l))
            ps = job("par", l)
            pe.transpose(ps[:, 0:NPAR], prow[0:NPAR, 0, :], cst[0:NPAR, IDENT:IDENT + NPAR]).then_inc(*done("par", l))
            ps = job("par2", l)
            pe.transpose(ps[:, 0:NPAR2], prow[0:NPAR2, 1, :], cst[0:NPAR2, IDENT:IDENT + NPAR2]).then_inc(*done("par2", l))
            pe.wait_ge(*when("csil", l))
            ps = job("mods", l)
            for j in range(24):
                wt = weights(l, "ada", j)
                for jj in range(2):
                    for k in range(KT):
                        mm = pe.matmul(ps[:, 4 * j + 2 * jj:4 * j + 2 * jj + 2], wt[:, k, P * jj:P * jj + P],
                                       csil[:, k, :], start=(k == 0), stop=(k == KT - 1))
                if j < 23:
                    mm.then_inc(*mark("ada_read", l, j))
                plan.release[chunk_of[("ada", j)]] = ("mark", "ada_read", l, j) if j < 23 else ("mods", l)
            mm.then_inc(*done("mods", l))
            sum_rows(("n1", l), KT, ones, slice(0, T), "sq")
            for k in range(KT):
                pe.wait_ge(*when("h1", l, k))
            for j in range(4):
                wt = weights(l, "B", j)
                for jj in range(2):
                    b = 2 * j + jj
                    tk = o if b < 4 else slice(0, T)
                    project(("qk", l, b), wt, P * jj, P, lambda k: H[:, k, tk], KT, n=tk.stop - tk.start)
                    if b >= 1:
                        pe.wait_ge(*drained("qk", l, b - 1))
                        ps = job("qkrot", l, b - 1)
                        pe.matmul(ps[:, 0:HALF], cst[:, PERM:PERM + P], QK[:, b - 1, LAT], start=True, stop=True).then_inc(*done("qkrot", l, b - 1))
                release(("B", j), "qk", l, 2 * j + 1)
            for j in range(2):
                wt = weights(l, "B", 4 + j)
                for t in range(4):
                    ps = job("vd", l, j, t)
                    for k in range(KT):
                        mm = pe.matmul(ps[:, 0:256], H[:, k, P * t:P * t + P], wt[:, k, :], start=(k == 0), stop=(k == KT - 1))
                    mm.then_inc(*done("vd", l, j, t))
                release(("B", 4 + j), "vd", l, j, 3)
            pe.wait_ge(*drained("qk", l, 7))
            ps = job("qkrot", l, 7)
            pe.matmul(ps[:, 0:HALF], cst[:, PERM:PERM + P], QK[:, 7, LAT], start=True, stop=True).then_inc(*done("qkrot", l, 7))
            wt = weights(l, "C", 0)
            for b in (0, 1):
                project(("zc", l, b), wt, P * b, P, lambda k: H[:, k, o], KT, n=no)
            release(("C", 0), "zc", l, 1)
            wt = weights(l, "C", 1)
            project(("zc", l, 2), wt, 0, P, lambda k: H[:, k, o], KT, n=no)
            project(("zc", l, 3), wt, P, P, lambda k: H[:, k, :], KT)
            release(("C", 1), "zc", l, 3)
            wt = weights(l, "C", 2)
            project(("zc", l, 4), wt, 0, P, lambda k: H[:, k, :], KT)
            project(("zc", l, 5), wt, P, 32, lambda k: H[:, k, :], KT, ps_rows=slice(64, 96))
            release(("C", 2), "zc", l, 5)
            sum_rows(("qn", l), 3, ones, o, "sq")
            sum_rows(("kvn", l), 2, ones, slice(0, T), "sq")
            pe.wait_ge(*drained("zc", l, 5))
            ps = job("krot", l)
            pe.matmul(ps[64:96, 0:HALF], cst[64:96, PERM32:PERM32 + 32], ZC[64:96, 5, LAT], start=True, stop=True).then_inc(*done("krot", l))
            for k in range(3):
                pe.wait_ge(*when("qnorm", l, k))
            for j in range(2):
                wt = weights(l, "uq", j)
                for hh in range(4):
                    h = 4 * j + hh
                    project(("mq", l, h), wt, 96 * hh, 96, lambda k: ZC[:, k, o], 3, ps_rows=slice(0, 96), n=no)
                    if h >= 1:
                        pe.wait_ge(*drained("mq", l, h - 1))
                        ps = job("mqrot", l, h - 1)
                        pe.matmul(ps[64:96, 0:HALF], cst[64:96, PERM32:PERM32 + 32], MQ[64:96, h - 1, LAT], start=True, stop=True).then_inc(*done("mqrot", l, h - 1))
                release(("uq", j), "mq", l, 4 * j + 3)
            for k in range(2):
                pe.wait_ge(*when("kvnorm", l, k))
            wt = weights(l, "uk")
            for j in range(4):
                project(("mk", l, j), wt, P * j, P, lambda k: ZC[:, 3 + k, :], 2)
            release(("uk",), "mk", l, 3)
            wt = weights(l, "uv")
            for t in range(4):
                ps = job("mv", l, t)
                for k in range(2):
                    mm = pe.matmul(ps[:, :], ZC[:, 3 + k, P * t:P * t + P], wt[:, k, :], start=(k == 0), stop=(k == 1))
                mm.then_inc(*done("mv", l, t))
            release(("uv",), "mv", l, 3)
            pe.wait_ge(*drained("mq", l, 7))
            ps = job("mqrot", l, 7)
            pe.matmul(ps[64:96, 0:HALF], cst[64:96, PERM32:PERM32 + 32], MQ[64:96, 7, LAT], start=True, stop=True).then_inc(*done("mqrot", l, 7))

            units = attention_units(l)

            def scores(i):
                kind, h, q, nk = units[i]
                qs = slice(P * q, P * q + P)
                if kind == "diff":
                    if i == 0:
                        for b in range(8):
                            pe.wait_ge(*when("qk_ready", l, b))
                    for c in range(2):
                        ps = job("sc", l, i, c)
                        pe.matmul(ps[:, 0:P * nk], QK[64 * c:64 * c + 64, h, qs], QK[64 * c:64 * c + 64, 4 + h, 0:P * nk],
                                  start=True, stop=True).then_inc(*done("sc", l, i, c))
                else:
                    if units[i - 1][0] == "diff":
                        pe.wait_ge(*when("mk_rope", l))
                        for j in range(4):
                            pe.wait_ge(*drained("mk", l, j))
                        for j in range(8):
                            pe.wait_ge(*when("mq_ready", l, j))
                    ps = job("sc", l, i, 0)
                    pe.matmul(ps[:, 0:P * nk], MQ[0:96, h, qs], MK[0:96, h, 0:P * nk], start=True, stop=True).then_inc(*done("sc", l, i, 0))

            def transposed(i):
                kind, h, q, nk = units[i]
                pe.wait_ge(*when("probs", l, i))
                ps = job("pt", l, i)
                for t in range(nk):
                    mm = pe.transpose(ps[:, P * t:P * t + P], PR[:, i % 2, 0, P * t:P * t + P], ident)
                mm.then_inc(*done("pt", l, i))

            def values(i):
                kind, h, q, nk = units[i]
                pe.wait_ge(*drained("pt", l, i))
                if i == 0:
                    for j in range(2):
                        for t in range(4):
                            pe.wait_ge(*drained("vd", l, j, t))
                    for t in range(4):
                        pe.wait_ge(*drained("mv", l, t))
                ps = job("av", l, i)
                for t in range(nk):
                    if kind == "diff":
                        mm = pe.matmul(ps[:, 0:P], VD[:, t, P * h:P * h + P], PT[:, i % 2, P * t:P * t + P], start=(t == 0), stop=(t == nk - 1))
                    else:
                        r = 64 * (h % 2)
                        mm = pe.matmul(ps[r:r + 64, 0:P], MV[:, t, 64 * h:64 * h + 64], PT[:, i % 2, P * t:P * t + P], start=(t == 0), stop=(t == nk - 1))
                mm.then_inc(*done("av", l, i))

            scores(0)
            for i in range(len(units)):
                if i + 1 < len(units):
                    scores(i + 1)
                if i >= 1:
                    values(i - 1)
                transposed(i)
            values(len(units) - 1)
            for h in range(4):
                sum_rows(("bn", l, h), 1, ones, o, "sq")

            for j in range(8):
                wt = weights(l, "A", j)
                for jj in range(2 if j < 7 else 1):
                    b = 2 * j + jj
                    tk = o if b < 4 or b == 14 else slice(0, T)
                    project(("za", l, b), wt, P * jj, P, lambda k: H[:, k, tk], KT, n=tk.stop - tk.start)
                release(("A", j), "za", l, min(2 * j + 1, 14))
            for c in range(NCH):
                if c == 0:
                    for p in range(4):
                        pe.wait_ge(*drained("za", l, 8 + p))
                ps = job("vtok", l, c)
                for p in range(4):
                    mm = pe.transpose(ps[0:C, P * p:P * p + P], ZS[:, 8 + p, C * c:C * c + C], ident)
                mm.then_inc(*done("vtok", l, c))
            for p in range(4):
                sum_rows(("kkn", l, p), 1, bones, slice(0, T), "sq")

            def branch12(d):
                wt = weights(l, "G12", d)
                for g in range(2):
                    project(("g12", l, d, g), wt, P * g, P, lambda k: H[:, k, o], KT, n=no)
                release(("G12", d), "g12", l, d, 1)
                wt = weights(l, "W12", d)
                if d == 0:
                    for h in range(4):
                        pe.wait_ge(*when("yb", l, h))
                    for i in range(len(units)):
                        if units[i][0] == "mla":
                            pe.wait_ge(*drained("av", l, i))
                for g, y in enumerate((YB, YC)):
                    ps = job("w12", l, d, g)
                    for k in range(4):
                        mm = pe.matmul(ps[:, 0:no], wt[:, 4 * g + k, :], y[:, k, o], start=(k == 0), stop=(k == 3))
                    mm.then_inc(*done("w12", l, d, g))
                release(("W12", d), "w12", l, d, 1)

            def lora_in(i):
                d, p = i // 4, i % 4
                rows = slice(64 * d, 64 * d + 64)
                for n, name in enumerate(("lora_w", "lora_a")):
                    if i == 0 and n == 0:
                        pe.wait_ge(*when("lora", l))
                        pe.wait_ge(*when("tanh", l))
                        pe.wait_ge(*drained("za", l, 13))
                    ps = job(name, l, i)
                    pe.matmul(ps[:, :], lora[rows, n, P * p:P * p + P], ZS[rows, 12 + n, :], start=True, stop=True).then_inc(*done(name, l, i))

            def scores_in_chunk(i):
                pe.wait_ge(*when("ar", l, i))
                pe.wait_ge(*when("bk", l, i))
                for g in range(0, 4, 2):
                    pss = [job("A", l, i, g + hh) for hh in range(2)]
                    for c in range(4):
                        for hh in range(2):
                            ch = 4 * (g // 2) + c
                            rows = slice(64 * hh, 64 * hh + 64)
                            mm = pe.matmul(pss[hh][:, P * c:P * c + P], BK[rows, ch, :], AR[rows, i % 2, ch, :], start=True, stop=True)
                            if c == 3:
                                mm.then_inc(*done("A", l, i, g + hh))
                pe.wait_ge(*when("bh", l, i))
                for g in range(2):
                    ps = job("bkt", l, i, g)
                    for c in range(4):
                        mm = pe.transpose(ps[:, P * c:P * c + P], BH[:, 4 * g + c, :], ident)
                    mm.then_inc(*done("bkt", l, i, g))

            lora_in(0)
            for i in range(8):
                if i < 4:
                    branch12(i)
                if i + 1 < 8:
                    lora_in(i + 1)
                scores_in_chunk(i)
            for p in range(4):
                pe.wait_ge(*when("rkk", l, p))
                ps = job("bonus", l, p)
                pe.matmul(ps[:, 0:no], bones, BV[:, p, o], start=True, stop=True).then_inc(*done("bonus", l, p))
            for d in range(4, 8):
                branch12(d)

            def state_key(c, g):
                return ("S", l, c, g)

            pe.wait_ge(*when("state_zero", l))
            for c in range(NCH):
                b = c % 2
                pe.wait_ge(*when(f"chunk_in{b}", l, c))
                for g in range(2):
                    ps = job("U", l, c, g)
                    if c:
                        pe.wait_ge(*drained("S", l, c - 1, g))
                    for ii in range(4):
                        i = 4 * g + ii
                        pe.matmul(ps[0:C, P * ii:P * ii + P], cR[:, b, i, 0:C], S[:, i, :], start=True, stop=False, skip_group_check=True)
                        for hh in range(2):
                            v0 = P * (i % 4) + C * hh
                            mm = pe.matmul(ps[0:C, P * ii + C * hh:P * ii + C * hh + C], cA[C:P, b, 2 * i + hh, 0:C],
                                           cV[C:P, b, i // 4, v0:v0 + C], start=False, stop=True, skip_group_check=True)
                    mm.then_inc(*done("U", l, c, g))
                for g in range(2):
                    ps = job("SA", l, c, g)
                    pe.wait_ge(*drained("U", l, c, g))
                    for ii in range(4):
                        i = 4 * g + ii
                        for hh in range(2):
                            mm = pe.matmul(ps[0:C, P * ii + C * hh:P * ii + C * hh + C], cX[0:C, b, 2 * i + hh, :],
                                           R[0:C, i, C * hh:C * hh + C], start=True, stop=True)
                    mm.then_inc(*done("SA", l, c, g))
                yjobs = not (l and c < 4)
                for g in range(2):
                    pe.wait_ge(*drained("SA", l, c, g))
                    if yjobs:
                        ps = job("Y", l, c, g)
                        for ii in range(4):
                            i = 4 * g + ii
                            pe.matmul(ps[:, C * ii:C * ii + C], S[:, i, :], cR[:, b, i, C:P], start=True, stop=False, skip_group_check=True)
                            for hh in range(2):
                                v0 = P * (i % 4) + C * hh
                                mm = pe.matmul(ps[C * hh:C * hh + C, C * ii:C * ii + C], cV[:, b, i // 4, v0:v0 + C],
                                               cA[:, b, 2 * i + hh, C:P], start=False, stop=True, skip_group_check=True)
                        mm.then_inc(*done("Y", l, c, g))
                    ps = job("S", l, c, g)
                    for ii in range(4):
                        i = 4 * g + ii
                        mm = pe.matmul(ps[:, P * ii:P * ii + P], cB[:, b, i, :], cV[:, b, i // 4, P * (i % 4):P * (i % 4) + P],
                                       start=True, stop=True)
                    mm.then_inc(*done("S", l, c, g))

            pe.wait_ge(*when("gd", l))
            for p in range(4):
                pe.wait_ge(*when("ysum", l, p))
                ps = job("gmean", l, p)
                pe.matmul(ps[:, 0:no], bones, Y[:, 0, p, o], start=True, stop=True).then_inc(*done("gmean", l, p))
            for p in range(4):
                ps = job("lora_g", l, p)
                pe.matmul(ps[:, 0:no], lora[:, 2, P * p:P * p + P], ZS[:, 14, o], start=True, stop=True).then_inc(*done("lora_g", l, p))
            for p in range(4):
                pe.wait_ge(*when("ysq", l, p))
                ps = job("gvar", l, p)
                pe.matmul(ps[:, 0:no], bones, RO[0][:, p, o], start=True, stop=True).then_inc(*done("gvar", l, p))

            for d in range(8):
                wt = weights(l, "GW0", d)
                project(("g0", l, d), wt, 0, P, lambda k: H[:, k, o], KT, n=no)
                if d == 0:
                    for p in range(4):
                        pe.wait_ge(*drained("lora_g", l, p))
                ps = job("w0", l, d)
                for k in range(4):
                    mm = pe.matmul(ps[:, 0:no], wt[:, 8 + k, :], YA[:, k, o], start=(k == 0), stop=(k == 3))
                mm.then_inc(*done("w0", l, d))
                release(("GW0", d), "w0", l, d)
            for d in range(8):
                pe.wait_ge(*when("merged", l, d))
            for j in range(4):
                wt = weights(l, "O", j)
                for jj in range(2):
                    project(("wo", l, 2 * j + jj), wt, P * jj, P, lambda k: M[:, k, o], KT, n=no)
                release(("O", j), "wo", l, 2 * j + 1)
            sum_rows(("n2", l), KT, ones, o, "sq")
            for k in range(KT):
                pe.wait_ge(*when("h2", l, k))
            for j in range(11):
                wg = weights(l, "FG", j)
                wu = weights(l, "FU", j)
                for jj in range(2):
                    f = 2 * j + jj
                    project(("fg", l, f), wg, P * jj, P, lambda k: H[:, k, o], KT, n=no)
                    project(("fu", l, f), wu, P * jj, P, lambda k: H[:, k, o], KT, n=no)
                release(("FG", j), "fg", l, 2 * j + 1)
                release(("FU", j), "fu", l, 2 * j + 1)
            for dp in range(4):
                pss = [job("fd", l, 2 * dp + jj) for jj in range(2)]
                for kc, (k0, k1) in enumerate(((0, 8), (8, 16), (16, 22))):
                    wt = weights(l, "FD", dp, kc)
                    for k in range(k0, k1):
                        if dp == 0:
                            pe.wait_ge(*drained("fu", l, k))
                        for jj in range(2):
                            mm = pe.matmul(pss[jj][:, 0:no], wt[:, k - k0, P * jj:P * jj + P], FH[:, k, o],
                                           start=(k == 0), stop=(k == FT - 1), skip_group_check=True)
                            if k == FT - 1:
                                mm.then_inc(*done("fd", l, 2 * dp + jj))
                    if kc < 2:
                        mm.then_inc(*mark("fd_read", l, dp, kc))
                        plan.release[chunk_of[("FD", dp, kc)]] = ("mark", "fd_read", l, dp, kc)
                    else:
                        release(("FD", dp, kc), "fd", l, 2 * dp + 1)
        sum_rows(("nf",), KT, ones, LAT, "sq")
        for k in range(KT):
            pe.wait_ge(*when("final", k))
        for i in range(2):
            for h in range(2):
                ps = job("xout", i, h)
                for k in range(4):
                    mm = pe.transpose(ps[:, P * k:P * k + P], H[:, 4 * h + k, HALF + P * i:HALF + P * i + P], ident)
                mm.then_inc(*done("xout", i, h))

    @block.scalar
    def _(act):
        A = nc.scalar.activation

        def step(ins):
            ins.then_inc(*mark("act_step", plan.count.get("act_step", 0)))
            act.wait_ge(sem_of("act_step"), plan.count["act_step"])

        def squares(key, src, tiles, toks):
            for k in range(tiles):
                if k >= 2:
                    act.wait_ge(*when("squares_read", *key, k - 2))
                elif last_sum[0] is not None:
                    act.wait_ge(*full(*last_sum[0]))
                A(SQ[:, k % 2, toks], src(k), ACT.Square).then_inc(*mark("sq", *key, k))
            last_sum[0] = key

        last_sum = [None]

        def root(key, toks):
            act.wait_ge(*drained(*key))
            A(RS[:, toks], RS[:, toks], ACT.Sqrt).then_inc(*mark("root", *key))

        for i in range(4):
            for h in range(2):
                act.wait_ge(*full("xin", i, h))
                A(X[:, 4 * h:4 * h + 4, P * i:P * i + P], bank("xin", i, h)[:, :].rearrange("p (k t) -> p k t", k=4), ACT.Copy).then_inc(*drain("xin", i, h))
        act.wait_ge(*drained("xin", 3, 1))
        for l in range(DEPTH):
            o = outs(l)
            no = o.stop - o.start
            act.wait_ge(*full("par", l))
            A(par[:, l, :], bank("par", l)[:, 0:NPAR], ACT.Copy).then_inc(*drain("par", l))
            act.wait_ge(*full("par2", l))
            A(par2[:, l, :], bank("par2", l)[:, 0:NPAR2], ACT.Copy).then_inc(*drain("par2", l))
            act.wait_ge(*drained("par2", l))
            A(csil[:, :, 0], par2[:, l, CCTX:CCTX + 8], ACT.Sigmoid).then_inc(*mark("csig", l, 0))
            A(csil[:, :, 1], par2[:, l, CVEC:CVEC + 8], ACT.Sigmoid).then_inc(*mark("csig", l, 1))
            act.wait_ge(*when("lam_dots", l))
            A(lam[:, 0:2], lam[:, 0:2], ACT.Exp).then_inc(*mark("lam_exp", l))
            if l:
                for k in range(KT):
                    act.wait_ge(*drained("fd", l - 1, k))
            squares(("n1", l), lambda k: X[:, k, :], KT, slice(0, T))
            root(("n1", l), slice(0, T))
            for k in range(KT):
                for s in (0, 1):
                    tk = slice(HALF * s, HALF * s + HALF)
                    act.wait_ge(*when("h1_scaled", l, k, s))
                    A(H[:, k, tk], H[:, k, tk], ACT.Identity, bias=mods[:, k, s:s + 1]).then_inc(*mark("h1", l, k))
            for b in range(8):
                tk = o if b < 4 else slice(0, T)
                act.wait_ge(*full("qk", l, b))
                A(QK[:, b, tk], bank("qk", l, b)[:, 0:tk.stop - tk.start], ACT.Copy).then_inc(*drain("qk", l, b))
            for j in range(2):
                for t in range(4):
                    act.wait_ge(*full("vd", l, j, t))
                    A(VD[:, t, 256 * j:256 * j + 256], bank("vd", l, j, t)[:, 0:256], ACT.Copy).then_inc(*drain("vd", l, j, t))
            for b in range(6):
                tk = o if b < 3 else slice(0, T)
                rows = slice(0, P) if b < 5 else slice(64, 96)
                act.wait_ge(*full("zc", l, b))
                A(ZC[rows, b, tk], bank("zc", l, b)[rows, 0:tk.stop - tk.start], ACT.Copy).then_inc(*drain("zc", l, b))
            for b in range(5):
                act.wait_ge(*drained("zc", l, b))
            squares(("qn", l), lambda k: ZC[:, k, o], 3, o)
            squares(("kvn", l), lambda k: ZC[:, 3 + k, :], 2, slice(0, T))
            root(("qn", l), o)
            root(("kvn", l), slice(0, T))
            for h in range(8):
                act.wait_ge(*full("mq", l, h))
                A(MQ[0:96, h, o], bank("mq", l, h)[0:96, 0:no], ACT.Copy).then_inc(*drain("mq", l, h))
            for j in range(4):
                act.wait_ge(*full("mk", l, j))
                for hh in range(2):
                    ins = A(MK[0:64, 2 * j + hh, :], bank("mk", l, j)[64 * hh:64 * hh + 64, :], ACT.Copy)
                ins.then_inc(*drain("mk", l, j))
            for t in range(4):
                act.wait_ge(*full("mv", l, t))
                A(MV[:, t, :], bank("mv", l, t)[:, :], ACT.Copy).then_inc(*drain("mv", l, t))
            units = attention_units(l)

            def exponentials(i):
                kind, h, q, nk = units[i]
                scale = DIFF_SCALE if kind == "diff" else MLA_SCALE
                for c in range(2 if kind == "diff" else 1):
                    act.wait_ge(*when("negmax", l, i, c))
                    if i >= 2 and c == 0:
                        act.wait_ge(*full("pt", l, i - 2))
                    A(PR[:, i % 2, c, 0:P * nk], bank("sc", l, i, c)[:, 0:P * nk], ACT.Exp, bias=smax[:, c, i:i + 1],
                      scale=scale, accum_out=ssum[:, c, i:i + 1]).then_inc(*drain("sc", l, i, c))

            def evacuate(i):
                kind, h, q, nk = units[i]
                act.wait_ge(*full("pt", l, i))
                if i >= 2:
                    act.wait_ge(*full("av", l, i - 2))
                A(PT[:, i % 2, 0:P * nk], bank("pt", l, i)[:, 0:P * nk], ACT.Copy).then_inc(*drain("pt", l, i))

            def attended(i):
                kind, h, q, nk = units[i]
                qs = slice(P * q, P * q + P)
                act.wait_ge(*full("av", l, i))
                if kind == "diff":
                    A(YB[:, h, qs], bank("av", l, i)[:, 0:P], ACT.Copy).then_inc(*drain("av", l, i))
                else:
                    r = slice(64 * (h % 2), 64 * (h % 2) + 64)
                    A(YC[r, h // 2, qs], bank("av", l, i)[r, 0:P], ACT.Copy).then_inc(*drain("av", l, i))

            exponentials(0)
            for i in range(len(units)):
                if i + 1 < len(units):
                    exponentials(i + 1)
                if i >= 1:
                    attended(i - 1)
                evacuate(i)
            attended(len(units) - 1)
            nq = 4 if l == 0 else 2
            for h in range(4):
                act.wait_ge(*drained("av", l, nq * h + nq - 1))
                squares(("bn", l, h), lambda k: YB[:, h, o], 1, o)
                root(("bn", l, h), o)

            for b in range(15):
                lo = l == 1 and (b < 4 or b == 14)
                tk = LAT if lo else slice(0, T)
                act.wait_ge(*full("za", l, b))
                if b == 0:
                    act.wait_ge(*when("mu0", l))
                A(ZS[:, b, tk], bank("za", l, b)[:, 0:tk.stop - tk.start], ACT.Copy, scale=mu0[:, b:b + 1]).then_inc(*mark("zs_own", l, b))
            act.wait_ge(*drained("za", l, 12))
            A(ZS[:, 12, :], ZS[:, 12, :], ACT.Tanh).then_inc(*mark("tanh", l))
            act.wait_ge(*drained("za", l, 14))
            A(ZS[:, 14, o], ZS[:, 14, o], ACT.Sigmoid).then_inc(*mark("gd", l))
            for c in range(NCH):
                act.wait_ge(*full("vtok", l, c))
                if c:
                    act.wait_ge(*when("v_spilled", l, c - 1))
                A(VT[0:C, :], bank("vtok", l, c)[0:C, :], ACT.Copy).then_inc(*drain("vtok", l, c))
            for p in range(4):
                act.wait_ge(*when("kkraw", l, p))
                squares(("kkn", l, p), lambda k: KK[:, p, :], 1, slice(0, T))
                act.wait_ge(*full("kkn", l, p))
                if p:
                    act.wait_ge(*when("kk", l, p - 1))
                A(RS, bank("kkn", l, p)[:, :], ACT.Sqrt).then_inc(*drain("kkn", l, p))

            act.wait_ge(*when("v_spilled", l, NCH - 1))

            def gates(i):
                d, p = i // 4, i % 4
                act.wait_ge(*full("lora_w", l, i))
                if i:
                    act.wait_ge(*when("decayed", l, i - 1))
                    act.wait_ge(*when("b", l, i - 1))
                A(SG, bank("lora_w", l, i)[:, :], ACT.Sigmoid, bias=par[:, l, W0 + i:W0 + i + 1]).then_inc(*drain("lora_w", l, i))
                act.wait_ge(*full("lora_a", l, i))
                A(AI, bank("lora_a", l, i)[:, :], ACT.Sigmoid, bias=par[:, l, A0C + i:A0C + i + 1]).then_inc(*drain("lora_a", l, i))
                act.wait_ge(*drained("lora_w", l, i))
                if i == 0:
                    act.wait_ge(*when("w65_zero", l))
                else:
                    act.wait_ge(*when("bk", l, i - 1))
                wv = W65.rearrange("p (h c t) -> p h c t", h=2, t=C + 1)
                for h in range(2):
                    ins = A(wv[:, h, :, 1:C + 1], directed(SG, d)[:, h], ACT.Exp, scale=-DECAY)
                ins.then_inc(*mark("decayed", l, i))

            def turned(i):
                for g in range(2):
                    act.wait_ge(*full("bkt", l, i, g))
                    if g == 0 and i:
                        act.wait_ge(*when("b_spilled", l, i - 1))
                    A(BKT[:, 4 * g:4 * g + 4, :], bank("bkt", l, i, g)[:, :].rearrange("p (c n) -> p c n", c=4), ACT.Copy).then_inc(*drain("bkt", l, i, g))

            def gate12(d):
                for g in range(2):
                    act.wait_ge(*full("g12", l, d, g))
                    if d:
                        act.wait_ge(*when("m12", l, d - 1))
                    A(GS[:, g, 0:no], bank("g12", l, d, g)[:, 0:no], ACT.Sigmoid).then_inc(*drain("g12", l, d, g))

            gates(0)
            for i in range(8):
                if i < 4:
                    gate12(i)
                if i + 1 < 8:
                    gates(i + 1)
                turned(i)
            for d in range(4, 8):
                gate12(d)

            for c in range(NCH):
                for g in range(2):
                    act.wait_ge(*full("U", l, c, g))
                    if c:
                        act.wait_ge(*full("SA", l, c - 1, g))
                    A(R[0:C, 4 * g:4 * g + 4, :], bank("U", l, c, g)[0:C, :].rearrange("p (i n) -> p i n", i=4), ACT.Copy).then_inc(*drain("U", l, c, g))
                if not (l and c < 4):
                    for g in range(2):
                        act.wait_ge(*full("Y", l, c, g))
                        rc = c if g == 0 else 4 * (c // 4) + 3 - c % 4
                        dst = Y[:, g, :, C * rc:C * rc + C]
                        if g:
                            dst = dst[:, :, ::-1]
                        A(dst, bank("Y", l, c, g)[:, 0:4 * C].rearrange("p (i t) -> p i t", i=4), ACT.Copy).then_inc(*drain("Y", l, c, g))

            for p in range(4):
                act.wait_ge(*drained("gmean", l, p))
                A(RO[0][:, p, o], Y[:, 0, p, o], ACT.Square).then_inc(*mark("ysq", l, p))
            for p in range(4):
                act.wait_ge(*drained("gvar", l, p))
                A(RO[1][:, p, o], RO[1][:, p, o], ACT.Sqrt).then_inc(*mark("groot", l, p))
            for d in range(8):
                act.wait_ge(*full("g0", l, d))
                if d >= 2:
                    act.wait_ge(*when("merged", l, d - 2))
                if d == 0:
                    act.wait_ge(*when("m12", l, 7))
                A(GATE[:, d % 2, 0:no], bank("g0", l, d)[:, 0:no], ACT.Sigmoid).then_inc(*drain("g0", l, d))
            for k in range(KT):
                act.wait_ge(*drained("wo", l, k))
            squares(("n2", l), lambda k: X2[:, k, o], KT, o)
            root(("n2", l), o)
            for k in range(KT):
                for s in sides(l):
                    tk = slice(HALF * s, HALF * s + HALF)
                    act.wait_ge(*when("h2_scaled", l, k, s))
                    A(H[:, k, tk], H[:, k, tk], ACT.Identity, bias=mods[:, 24 + k, s:s + 1]).then_inc(*mark("h2", l, k))
            for f in range(FT):
                act.wait_ge(*full("fg", l, f))
                if f >= 2:
                    act.wait_ge(*drained("fg", l, f - 2))
                A(FSG[:, f % 2, 0:no], bank("fg", l, f)[:, 0:no], ACT.Sigmoid).then_inc(*mark("fsg", l, f))
        for k in range(KT):
            act.wait_ge(*drained("fd", DEPTH - 1, k))
        squares(("nf",), lambda k: X[:, k, LAT], KT, LAT)
        root(("nf",), LAT)
        for i in range(2):
            for h in range(2):
                act.wait_ge(*full("xout", i, h))
                if i:
                    act.wait_ge(*when("stored", i - 1))
                A(TOK[:, 512 * h:512 * h + 512], bank("xout", i, h)[:, :], ACT.Copy).then_inc(*drain("xout", i, h))

    @block.vector
    def _(dve):
        V = nc.vector

        def step(ins):
            ins.then_inc(*mark("dve_step", plan.count.get("dve_step", 0)))
            dve.wait_ge(sem_of("dve_step"), plan.count["dve_step"])

        def mean_square(key, n, toks):
            dve.wait_ge(*full(*key))
            ps = bank(*key)
            V.tensor_scalar(RS[:, toks], ps[:, 0:toks.stop - toks.start], 1.0 / n, EPS, ALU.mult, ALU.add).then_inc(*drain(*key))
            dve.wait_ge(*when("root", *key))
            step(V.reciprocal(RS[:, toks], RS[:, toks]))

        for l in range(DEPTH):
            o = outs(l)
            no = o.stop - o.start
            lam_init = 0.8 - 0.6 * math.exp(-0.3 * l)
            pcol = par[:, l, :]
            dve.wait_ge(*when("lamv", l))
            for j in range(2):
                step(V.tensor_tensor(lamv[:, 128 * j:128 * j + 64], lamv[:, 128 * j:128 * j + 64], lamv[:, 128 * j + 64:128 * j + 128], ALU.mult))
                ins = V.reduce_sum(lam[:, j:j + 1], lamv[:, 128 * j:128 * j + 64], AX.X)
            ins.then_inc(*mark("lam_dots", l))
            dve.wait_ge(*when("csig", l, 1))
            V.tensor_tensor(csil[:, :, 0], csil[:, :, 0], par2[:, l, CCTX:CCTX + 8], ALU.mult)
            V.tensor_tensor(csil[:, :, 1], csil[:, :, 1], par2[:, l, CVEC:CVEC + 8], ALU.mult).then_inc(*mark("csil", l))
            dve.wait_ge(*when("lam_exp", l))
            step(V.tensor_tensor(lam[:, 2:3], lam[:, 0:1], lam[:, 1:2], ALU.subtract))
            V.tensor_scalar(lam[:, 2:3], lam[:, 2:3], lam_init, None, ALU.add).then_inc(*mark("lam", l))
            V.tensor_scalar(subg[:, :], pcol[:, SUBG:SUBG + 1], 1.0 - lam_init, None, ALU.mult)
            step(V.tensor_tensor(mu0[:, :], pcol[:, MU:MU + 15], pcol[:, MU + 15:MU + 30], ALU.add))
            V.tensor_scalar(mu0[:, :], mu0[:, :], -1.0, 1.0, ALU.mult, ALU.add).then_inc(*mark("mu0", l))
            step(V.tensor_scalar(kaneg[:, :], pcol[:, KAC:KAC + 4], -1.0, 1.0, ALU.mult, ALU.add))
            dve.wait_ge(*full("mods", l))
            V.tensor_tensor(mods[:, :, :], bank("mods", l)[:, 0:96].rearrange("p (j s) -> p j s", s=2),
                            par2[:, l, ADAB:ADAB + 48].unsqueeze(2).broadcast_to([P, 48, 2]), ALU.add).then_inc(*drain("mods", l))
            dve.wait_ge(*drained("mods", l))
            for n, (sc, g) in enumerate(((8, N1), (32, N2))):
                ins = V.scalar_tensor_tensor(gsc[:, n], mods[:, sc:sc + 8, :], 1.0,
                                             pcol[:, g:g + 8].unsqueeze(2).broadcast_to([P, 8, 2]), ALU.add, ALU.mult)
            step(ins)
            mean_square(("n1", l), D, slice(0, T))
            for k in range(KT):
                for s in (0, 1):
                    tk = slice(HALF * s, HALF * s + HALF)
                    V.scalar_tensor_tensor(H[:, k, tk], X[:, k, tk], gsc[:, 0, k, s:s + 1], RS[:, tk], ALU.mult, ALU.mult).then_inc(*mark("h1_scaled", l, k, s))

            def rope(raw, x, cosc, sinc, rows, name, key, n):
                dve.wait_ge(*full(*raw))
                r = ROT[rows, n % 2, :]
                V.tensor_tensor(r, bank(*raw)[rows, 0:HALF], cst[rows, sinc:sinc + HALF], ALU.mult).then_inc(*drain(*raw))
                step(V.tensor_tensor(x, x, cst[rows, cosc:cosc + HALF], ALU.mult))
                dve.wait_ge(*drained(*raw))
                V.tensor_tensor(x, x, r, ALU.add).then_inc(*mark(name, *key))

            allp = slice(0, P)
            q32 = slice(64, 96)
            for b in range(8):
                rope(("qkrot", l, b), QK[:, b, LAT], COSB, SINB, allp, "qk_ready", (l, b), b)
            mean_square(("qn", l), 384, o)
            for k in range(3):
                V.scalar_tensor_tensor(ZC[:, k, o], ZC[:, k, o], pcol[:, QNG + k:QNG + k + 1], RS[:, o], ALU.mult, ALU.mult).then_inc(*mark("qnorm", l, k))
            dve.wait_ge(*when("qnorm", l, 2))
            mean_square(("kvn", l), 256, slice(0, T))
            for k in range(2):
                V.scalar_tensor_tensor(ZC[:, 3 + k, :], ZC[:, 3 + k, :], pcol[:, KVG + k:KVG + k + 1], RS, ALU.mult, ALU.mult).then_inc(*mark("kvnorm", l, k))
            dve.wait_ge(*when("kvnorm", l, 1))
            rope(("krot", l), ZC[q32, 5, LAT], COSC, SINC, q32, "krope", (l,), 0)
            dve.wait_ge(*when("krope", l))
            V.tensor_copy(MK[q32, :, :], ZC[q32, 5:6, :].broadcast_to([32, 8, T])).then_inc(*mark("mk_rope", l))
            for h in range(8):
                rope(("mqrot", l, h), MQ[q32, h, LAT], COSC, SINC, q32, "mq_ready", (l, h), h)

            units = attention_units(l)

            def maxima(i):
                kind, h, q, nk = units[i]
                scale = DIFF_SCALE if kind == "diff" else MLA_SCALE
                for c in range(2 if kind == "diff" else 1):
                    dve.wait_ge(*full("sc", l, i, c))
                    if l and i == 0 and c == 0:
                        pass
                    step(V.reduce_max(smax[:, c, i:i + 1], bank("sc", l, i, c)[:, 0:P * nk], AX.X))
                    V.tensor_scalar(smax[:, c, i:i + 1], smax[:, c, i:i + 1], -scale, None, ALU.mult).then_inc(*mark("negmax", l, i, c))

            def normalised(i):
                kind, h, q, nk = units[i]
                n = P * nk
                nc_ = 2 if kind == "diff" else 1
                for c in range(nc_):
                    dve.wait_ge(*drained("sc", l, i, c))
                step(V.reciprocal(rsum[:, 0:nc_, i:i + 1], ssum[:, 0:nc_, i:i + 1]))
                if kind == "diff":
                    step(V.tensor_scalar(PR[:, i % 2, 1, 0:n], PR[:, i % 2, 1, 0:n], rsum[:, 1, i:i + 1], lam[:, 2:3], ALU.mult, ALU.mult))
                    V.scalar_tensor_tensor(PR[:, i % 2, 0, 0:n], PR[:, i % 2, 0, 0:n], rsum[:, 0, i:i + 1], PR[:, i % 2, 1, 0:n],
                                           ALU.mult, ALU.subtract).then_inc(*mark("probs", l, i))
                else:
                    V.tensor_scalar(PR[:, i % 2, 0, 0:n], PR[:, i % 2, 0, 0:n], rsum[:, 0, i:i + 1], None, ALU.mult).then_inc(*mark("probs", l, i))

            maxima(0)
            for i in range(len(units)):
                if i + 1 < len(units):
                    maxima(i + 1)
                normalised(i)
            for h in range(4):
                mean_square(("bn", l, h), P, o)
                V.scalar_tensor_tensor(YB[:, h, o], YB[:, h, o], subg[:, 0:1], RS[:, o], ALU.mult, ALU.mult).then_inc(*mark("yb", l, h))
                dve.wait_ge(*when("yb", l, h))

            for b in range(15):
                lo = l == 1 and (b < 4 or b == 14)
                ps = bank("za", l, b)
                dve.wait_ge(*when("zs_own", l, b))
                if lo:
                    z, s = ps[:, 0:HALF].unsqueeze(1), ZS[:, b, LAT].unsqueeze(1)
                else:
                    z, s = ps[:, :].rearrange("p (h t) -> p h t", h=2), ZS[:, b, :].rearrange("p (h t) -> p h t", h=2)
                step(V.scalar_tensor_tensor(s[:, :, 1:HALF], z[:, :, 0:HALF - 1], pcol[:, MU + b:MU + b + 1], s[:, :, 1:HALF], ALU.mult, ALU.add))
                V.scalar_tensor_tensor(s[:, :, 0:HALF - 1], z[:, :, 1:HALF], pcol[:, MU + 15 + b:MU + 16 + b], s[:, :, 0:HALF - 1],
                                       ALU.mult, ALU.add).then_inc(*drain("za", l, b))
            for p in range(4):
                dve.wait_ge(*drained("za", l, 4 + p))
                V.tensor_scalar(KK[:, p, :], ZS[:, 4 + p, :], pcol[:, KKC + p:KKC + p + 1], None, ALU.mult).then_inc(*mark("kkraw", l, p))
            for p in range(4):
                dve.wait_ge(*drained("kkn", l, p))
                step(V.tensor_scalar(RS, RS, 1e-12, None, ALU.max))
                step(V.reciprocal(RS, RS))
                V.tensor_tensor(KK[:, p, :], KK[:, p, :], RS, ALU.mult).then_inc(*mark("kk", l, p))
            dve.wait_ge(*when("kk", l, 3))
            w65v = W65.rearrange("p (c t) -> p c t", t=C + 1)
            V.memset(w65v[:, :, 0:1], 0.0).then_inc(*mark("w65_zero", l))

            def scaled(i):
                d, p = i // 4, i % 4
                k, r, kk = ZS[:, 4 + p, :], ZS[:, p, :], KK[:, p, :]
                ar = AR[:, i % 2]
                e = E65.rearrange("p (c t) -> p c t", t=C + 1)
                dve.wait_ge(*drained("lora_a", l, i))
                step(V.tensor_scalar(TA, AI, pcol[:, KAC + p:KAC + p + 1], kaneg[:, p:p + 1], ALU.mult, ALU.add))
                step(V.tensor_tensor(TA, TA, k, ALU.mult))
                V.tensor_tensor(TB, kk, AI, ALU.mult).then_inc(*mark("b", l, i))
                if d == 0:
                    V.scalar_tensor_tensor(BV[:, p, o], TA[:, o], pcol[:, RKC + p:RKC + p + 1], r[:, o], ALU.mult, ALU.mult)
                else:
                    step(V.scalar_tensor_tensor(GT[:, o], TA[:, o], pcol[:, RKC + p:RKC + p + 1], r[:, o], ALU.mult, ALU.mult))
                    V.tensor_tensor(BV[:, p, o], BV[:, p, o], GT[:, o], ALU.add).then_inc(*mark("rkk", l, p))
                dve.wait_ge(*when("decayed", l, i))
                step(V.tensor_tensor_scan(E65, W65, cst[:, STARTS:STARTS + NCH * (C + 1)], 0.0, ALU.mult, ALU.add))
                if i >= 2:
                    dve.wait_ge(*when("r_spilled", l, i - 2))
                step(V.reciprocal(RI.rearrange("p (c t) -> p c t", t=C), e[:, :, 1:C + 1]))
                V.tensor_copy(dend[:, i, :], e[:, :, C])
                r3 = RI.rearrange("p (c t) -> p c t", t=C)
                for h in range(2):
                    cs = slice(4 * h, 4 * h + 4)
                    V.scalar_tensor_tensor(ar[:, cs, 0:C], directed(kk, d)[:, h], -1.0, e[:, cs, 0:C], ALU.mult, ALU.mult)
                    if l and h == 0:
                        ins = V.memset(ar[:, cs, C:P], 0.0)
                    else:
                        ins = V.tensor_tensor(ar[:, cs, C:P], directed(r, d)[:, h], e[:, cs, 1:C + 1], ALU.mult)
                ins.then_inc(*mark("ar", l, i))
                if i:
                    dve.wait_ge(*full("A", l, i - 1, 3))
                for h in range(2):
                    cs = slice(4 * h, 4 * h + 4)
                    V.tensor_tensor(BK[:, cs, 0:C], directed(TB, d)[:, h], r3[:, cs, :], ALU.mult)
                    ins = V.tensor_tensor(BK[:, cs, C:P], directed(TA, d)[:, h], r3[:, cs, :], ALU.mult)
                ins.then_inc(*mark("bk", l, i))
                dve.wait_ge(*when("bk", l, i))
                if i:
                    dve.wait_ge(*full("bkt", l, i - 1, 1))
                V.tensor_tensor(BH, BK, dend[:, i, :].unsqueeze(2).broadcast_to([P, NCH, P]), ALU.mult).then_inc(*mark("bh", l, i))

            def masked(i):
                for g in range(4):
                    dve.wait_ge(*full("A", l, i, g))
                    if g >= 2:
                        dve.wait_ge(*when(f"a_spilled{g % 2}", l, i, g - 2))
                    elif i:
                        dve.wait_ge(*when(f"a_spilled{g % 2}", l, i - 1, g + 2))
                    V.tensor_tensor(AS[:, g % 2], bank("A", l, i, g)[:, :].rearrange("p (c n) -> p c n", c=4),
                                    cst[:, MASK:MASK + P].unsqueeze(1).broadcast_to([P, 4, P]), ALU.mult).then_inc(*drain("A", l, i, g))

            def merged12(d):
                for g in range(2):
                    dve.wait_ge(*full("w12", l, d, g))
                    dve.wait_ge(*drained("g12", l, d, g))
                    V.tensor_tensor(GS[:, g, 0:no], bank("w12", l, d, g)[:, 0:no], GS[:, g, 0:no], ALU.mult).then_inc(*drain("w12", l, d, g))
                for g in range(2):
                    dve.wait_ge(*drained("w12", l, d, g))
                if d == 0:
                    dve.wait_ge(*when("x_spilled", l))
                V.tensor_tensor(M[:, d, o], GS[:, 0, 0:no], GS[:, 1, 0:no], ALU.add).then_inc(*mark("m12", l, d))

            for i in range(8):
                scaled(i)
                if i < 4:
                    merged12(i)
                masked(i)
            for p in range(4):
                dve.wait_ge(*full("bonus", l, p))
                V.tensor_tensor(BV[:, p, o], bank("bonus", l, p)[:, 0:no], ZS[:, 8 + p, o], ALU.mult).then_inc(*drain("bonus", l, p))

            dve.wait_ge(*when("nb_in", l))
            dve.wait_ge(*when("r_spilled", l, 7))
            for s in range(1, C - 1):
                n = C - 1 - s
                tmp = NT[:, 0:s * n].rearrange("p (j t) -> p j t", t=n)
                step(V.tensor_tensor(tmp, NB[:, 0:s, s:s + 1].broadcast_to([P, s, n]), NB[:, s:s + 1, s + 1:C].broadcast_to([P, s, n]), ALU.mult))
                step(V.tensor_tensor(NB[:, 0:s, s + 1:C], NB[:, 0:s, s + 1:C], tmp, ALU.add))
                if s % 8 == 7 and s // 8 < 4:
                    merged12(4 + s // 8)
            V.memset(NB.rearrange("p s t -> p (s t)")[:, 0:C * C:C + 1], 1.0).then_inc(*mark("inverted", l))
            V.memset(S, 0.0).then_inc(*mark("state_zero", l))
            dve.wait_ge(*when("state_zero", l))
            for c in range(NCH):
                b = c % 2
                for g in range(2):
                    dve.wait_ge(*full("SA", l, c, g))
                    dve.wait_ge(*when(f"chunk_in{b}", l, c))
                    V.tensor_copy(cV[0:C, b, g, :], bank("SA", l, c, g)[0:C, :]).then_inc(*drain("SA", l, c, g))
                for g in range(2):
                    if c:
                        dve.wait_ge(*drained("S", l, c - 1, g))
                    dve.wait_ge(*full("S", l, c, g))
                    ps = bank("S", l, c, g)
                    for ii in range(4):
                        i = 4 * g + ii
                        for hh in range(2):
                            r = slice(C * hh, C * hh + C)
                            ins = V.scalar_tensor_tensor(S[r, i, r], S[r, i, r], dend[r, i, c:c + 1],
                                                         ps[r, P * ii + C * hh:P * ii + C * hh + C], ALU.mult, ALU.add)
                    ins.then_inc(*drain("S", l, c, g))

            for p in range(4):
                if p == 0:
                    for g in range(2):
                        dve.wait_ge(*drained("Y", l, NCH - 1, g))
                V.tensor_tensor(Y[:, 0, p, o], Y[:, 0, p, o], Y[:, 1, p, o], ALU.add).then_inc(*mark("ysum", l, p))
            for p in range(4):
                dve.wait_ge(*full("gmean", l, p))
                V.scalar_tensor_tensor(Y[:, 0, p, o], bank("gmean", l, p)[:, 0:no], -1.0 / 64, Y[:, 0, p, o], ALU.mult, ALU.add).then_inc(*drain("gmean", l, p))
            for p in range(4):
                dve.wait_ge(*full("gvar", l, p))
                V.tensor_scalar(RO[1][:, p, o], bank("gvar", l, p)[:, 0:no], 1.0 / 64, GN_EPS, ALU.mult, ALU.add).then_inc(*drain("gvar", l, p))
            for p in range(4):
                dve.wait_ge(*when("groot", l, p))
                step(V.reciprocal(RO[1][:, p, o], RO[1][:, p, o]))
                step(V.scalar_tensor_tensor(Y[:, 0, p, o], Y[:, 0, p, o], pcol[:, LNW + p:LNW + p + 1], RO[1][:, p, o], ALU.mult, ALU.mult))
                step(V.scalar_tensor_tensor(Y[:, 0, p, o], Y[:, 0, p, o], pcol[:, LNB + p:LNB + p + 1], BV[:, p, o], ALU.add, ALU.add))
                dve.wait_ge(*full("lora_g", l, p))
                V.tensor_tensor(YA[:, p, o], bank("lora_g", l, p)[:, 0:no], Y[:, 0, p, o], ALU.mult).then_inc(*drain("lora_g", l, p))
            for d in range(8):
                dve.wait_ge(*full("w0", l, d))
                dve.wait_ge(*drained("g0", l, d))
                V.tensor_tensor(GATE[:, d % 2, 0:no], bank("w0", l, d)[:, 0:no], GATE[:, d % 2, 0:no], ALU.mult).then_inc(*drain("w0", l, d))
                dve.wait_ge(*drained("w0", l, d))
                V.tensor_tensor(M[:, d, o], M[:, d, o], GATE[:, d % 2, 0:no], ALU.add).then_inc(*mark("merged", l, d))
            dve.wait_ge(*when("x_back", l))
            for k in range(KT):
                dve.wait_ge(*full("wo", l, k))
                for s in sides(l):
                    tk = slice(HALF * s, HALF * s + HALF)
                    ins = V.scalar_tensor_tensor(X2[:, k, tk], bank("wo", l, k)[:, tk.start - o.start:tk.stop - o.start],
                                                 mods[:, 16 + k, s:s + 1], X2[:, k, tk], ALU.mult, ALU.add)
                ins.then_inc(*drain("wo", l, k))
            mean_square(("n2", l), D, o)
            for k in range(KT):
                for s in sides(l):
                    tk = slice(HALF * s, HALF * s + HALF)
                    V.scalar_tensor_tensor(H[:, k, tk], X2[:, k, tk], gsc[:, 1, k, s:s + 1], RS[:, tk], ALU.mult, ALU.mult).then_inc(*mark("h2_scaled", l, k, s))
            for f in range(FT):
                dve.wait_ge(*when("fsg", l, f))
                V.tensor_tensor(FST[:, f % 2, 0:no], bank("fg", l, f)[:, 0:no], FSG[:, f % 2, 0:no], ALU.mult).then_inc(*drain("fg", l, f))
                dve.wait_ge(*drained("fg", l, f))
                dve.wait_ge(*full("fu", l, f))
                V.tensor_tensor(FH[:, f, o], bank("fu", l, f)[:, 0:no], FST[:, f % 2, 0:no], ALU.mult).then_inc(*drain("fu", l, f))
            for k in range(KT):
                dve.wait_ge(*full("fd", l, k))
                for s in sides(l):
                    tk = slice(HALF * s, HALF * s + HALF)
                    ins = V.scalar_tensor_tensor(X[:, k, tk], bank("fd", l, k)[:, tk.start - o.start:tk.stop - o.start],
                                                 mods[:, 40 + k, s:s + 1], X2[:, k, tk], ALU.mult, ALU.add)
                ins.then_inc(*drain("fd", l, k))
        mean_square(("nf",), D, LAT)
        for k in range(KT):
            V.scalar_tensor_tensor(H[:, k, LAT], X[:, k, LAT], par2[:, DEPTH - 1, FING + k:FING + k + 1], RS[:, LAT], ALU.mult, ALU.mult).then_inc(*mark("final", k))


_NAMES = ['x', 'c', 'ctx', 'c_ctx', 'ada_w', 'ada_b', 'norm1_g', 'norm2_g', 'w_in', 'rwkv_shift_mu', 'rwkv_w0',
          'rwkv_w2', 'rwkv_a0', 'rwkv_a2', 'rwkv_g2', 'rwkv_k_k', 'rwkv_k_a', 'rwkv_r_k', 'rwkv_ln_w', 'rwkv_ln_b',
          'diff_lambda', 'diff_subln_g', 'mla_q_norm_g', 'mla_kv_norm_g', 'mla_w_uq', 'mla_w_uk', 'mla_w_uv',
          'w_branch', 'w_out', 'ffn_w_gate', 'ffn_w_up', 'ffn_w_down', 'final_norm_g']


def program(new_bass, shapes):
    plan = None
    for _ in range(2):
        nc = new_bass()
        plan = Plan(plan)
        w = {n: nc.dram_tensor(f"in_{n}", s, F32, kind="ExternalInput").ap() for n, s in shapes.items()}
        tab = nc.dram_tensor("in_tables", (P, NTAB), F32, kind="ExternalInput").ap()
        out = nc.dram_tensor("out_0", (1, HALF, D), F32, kind="ExternalOutput").ap()
        with ExitStack() as ctx:
            build(nc, w, tab, out, plan, ctx)
    return nc


def kernel(**inputs):
    import concourse.bacc as bacc
    from concourse.bass_utils import run_bass_kernel_spmd

    arrays = {f"in_{n}": np.ascontiguousarray(inputs[n]) for n in _NAMES}
    nc = program(lambda: bacc.Bacc("TRN2", target_bir_lowering=False, num_devices=1),
                 {n: tuple(inputs[n].shape) for n in _NAMES})
    arrays["in_tables"] = tables()
    return run_bass_kernel_spmd(nc, [arrays], core_ids=[0]).results[0]["out_0"]
```

```python
import math
from contextlib import ExitStack

import numpy as np
import concourse.bass as bass
from concourse import mybir

F32 = mybir.dt.float32
F32R = mybir.dt.float32r
ALU = mybir.AluOpType
ACT = mybir.ActivationFunctionType
AX = mybir.AxisListType

P = 128
DEPTH, D, KT = 2, 1024, 8
T, HALF = 512, 256
C = 64
NCH = T // C
RW, RT = 512, 4
W_COLS = 7200
A0, B0, C0, G0 = 0, 1920, 1920 + 1536, 1920 + 1536 + 672
DFF, FT = 2816, 22
EPS = 1e-6
GN_EPS = 64e-5
DECAY = math.exp(-0.5)
NBANK = 8
CSPLIT = 56
NW, WSLOT = 4, 2048
NHI = 4
LAT = slice(HALF, T)
DIFF_SCALE = 64 ** -0.5
MLA_SCALE = 96 ** -0.5

IDENT, MASK, ONES, BONES, PERM, PERM32, COSB, SINB, COSC, SINC, STARTS = (
    0, 128, 256, 384, 512, 640, 768, 1024, 1280, 1536, 1792)
NTAB = STARTS + NCH * (C + 1)
MU, N1, N2, W0, A0C, KKC, KAC, RKC, LNW, LNB, SUBG, QNG, KVG, NPAR = (
    0, 30, 38, 46, 54, 62, 66, 70, 74, 78, 82, 83, 86, 88)
ADAB, FING, CVEC, CCTX, NPAR2 = 0, 48, 56, 64, 72


def tables():
    t = np.zeros((P, NTAB), np.float32)
    i = np.arange(P)
    t[:, IDENT:IDENT + P] = np.eye(P)
    s, q = i[:, None] % 64, i[None, :]
    t[:, MASK:MASK + P] = np.where(q < 64, s < q, s <= q - 64)
    t[:, ONES:ONES + P] = 1
    t[:, BONES:BONES + P] = (i[:, None] // 64) == (i[None, :] // 64)
    for b in range(2):
        for j in range(32):
            t[64 * b + 32 + j, PERM + 64 * b + j] = -1
            t[64 * b + j, PERM + 64 * b + 32 + j] = 1
    for j in range(16):
        t[64 + 16 + j, PERM32 + j] = -1
        t[64 + j, PERM32 + 16 + j] = 1
    tok = np.arange(HALF)
    row, col = (tok // 64).astype(np.float32), (tok % 64).astype(np.float32)
    for rot, c0, s0 in ((64, COSB, SINB), (32, COSC, SINC)):
        n = rot // 4
        inv = (np.float32(10000.0) ** (-np.arange(n, dtype=np.float32) / np.float32(n))).astype(np.float32)
        ang = np.concatenate([row[:, None] * inv, col[:, None] * inv], -1).T
        cs, sn = np.cos(ang, dtype=np.float32), np.sin(ang, dtype=np.float32)
        if rot == 64:
            t[:, c0:c0 + HALF], t[:, s0:s0 + HALF] = np.tile(cs, (4, 1)), np.tile(sn, (4, 1))
        else:
            t[64:96, c0:c0 + HALF], t[64:96, s0:s0 + HALF] = np.tile(cs, (2, 1)), np.tile(sn, (2, 1))
    t[:, STARTS:].reshape(P, NCH, C + 1)[:, :, 0] = 1
    return t


class Plan:

    def __init__(self, known=None):
        self.known = known
        self.count, self.at, self.jobs, self.release, self.read = {}, {}, {}, {}, {}

    def start(self, sem_of):
        self.sem_of = sem_of

    def mark(self, name, *key, by=1):
        self.count[name] = self.count.get(name, 0) + by
        self.at[(name, *key)] = self.count[name]
        return self.sem_of(name), by

    def dma(self, name, *key):
        return self.mark(name, *key, by=16)

    def when(self, name, *key):
        return self.sem_of(name), (self.known.at[(name, *key)] if self.known else 1)

    def job(self, *key):
        n = len(self.jobs)
        self.jobs[key] = n
        return n

    def index(self, *key):
        return self.known.jobs[key] if self.known else 0

    def full(self, *key):
        n = self.index(*key)
        return self.sem_of(f"psum_full{n % NBANK}"), n // NBANK + 1

    def drained(self, *key):
        n = self.index(*key)
        return self.sem_of(f"psum_drained{n % NBANK}"), n // NBANK + 1

    def released(self, n):
        key = self.known.release[n] if self.known else ("x",)
        return self.when(*key[1:]) if key[0] == "mark" else self.full(*key)

    def half_read(self, m):
        key = self.known.read[m] if self.known else ("x",)
        return self.when(*key[1:]) if key[0] == "mark" else self.full(*key)

    def drain(self, *key):
        return self.sem_of(f"psum_drained{self.index(*key) % NBANK}"), 1


def weight_chunks(w, l):
    win = w["w_in"][l]

    def cols(m, a, n):
        return m[:, a:a + n].rearrange("(k p) n -> p k n", p=P)

    def ada(layer, part):
        for j in range(8 * part, 8 * part + 8):
            yield ("ada", layer, j), 8, 256, [(0, 256, 0, 8, cols(w["ada_w"][layer], 256 * j, 256))]

    if l == 0:
        yield from ada(0, 0)
    for j in range(6):
        yield ("B", j), 8, 256, [(0, 256, 0, 8, cols(win, B0 + 256 * j, 256))]
    for j, n in enumerate((256, 256, 160)):
        yield ("C", j), 8, n, [(0, n, 0, 8, cols(win, C0 + 256 * j, n))]
    for j in range(2):
        yield ("uq", j), 3, 384, [(0, 384, 0, 3, cols(w["mla_w_uq"][l], 384 * j, 384))]
    yield ("uk",), 2, 512, [(0, 512, 0, 2, cols(w["mla_w_uk"][l], 0, 512))]
    yield ("uv",), 2, 512, [(0, 512, 0, 2, cols(w["mla_w_uv"][l], 0, 512))]
    for j in range(8):
        n = 256 if j < 7 else 128
        yield ("A", j), 8, n, [(0, n, 0, 8, cols(win, A0 + 256 * j, n))]
    for d in range(8):
        yield ("G12", d), 8, 256, [(P * g, P * g + P, 0, 8, cols(win, G0 + D * (1 + g) + P * d, P))
                                   for g in range(2)]
        wb = w["w_branch"][l].rearrange("g e n -> (g e) n")
        yield ("W12", d), 8, P, [(0, P, 0, 8, cols(wb[RW:3 * RW], P * d, P))]
    yield from ada(l, 1)
    yield from ada(l, 2)
    if l + 1 < DEPTH:
        yield from ada(l + 1, 0)
    wb = w["w_branch"][l].rearrange("g e n -> (g e) n")
    for d in range(8):
        yield ("G0", d), 8, P, [(0, P, 0, 8, cols(win, G0 + P * d, P))]
        if l < DEPTH - 1:
            yield ("W0", d), 4, P, [(0, P, 0, 4, cols(wb[0:RW], P * d, P))]
    if l == DEPTH - 1:
        for d in range(8):
            yield ("W0", d), 4, P, [(0, P, 0, 4, cols(wb[0:RW], P * d, P))]
    for j in range(4):
        yield ("O", j), 8, 256, [(0, 256, 0, 8, cols(w["w_out"][l], 256 * j, 256))]
    for j in range(11):
        yield ("FG", j), 8, 256, [(0, 256, 0, 8, cols(w["ffn_w_gate"][l], 256 * j, 256))]
        yield ("FU", j), 8, 256, [(0, 256, 0, 8, cols(w["ffn_w_up"][l], 256 * j, 256))]
    for d in range(4):
        for kc, (k0, k1) in enumerate(((0, 8), (8, 16), (16, 22))):
            yield ("FD", d, kc), k1 - k0, 256, [
                (0, 256, 0, k1 - k0, cols(w["ffn_w_down"][l][P * k0:P * k1, :], 256 * d, 256))]


def split_halves(l):
    for j in range(11):
        for half in range(2):
            yield ("FG", j), half
            yield ("FU", j), half
    for d in range(4):
        for kc in range(3):
            for half in range(2):
                yield ("FD", d, kc), half


def attention_units(l):
    tiles = range(4) if l == 0 else range(2, 4)
    return ([("diff", h, q, 2 if q < 2 else 4) for h in range(4) for q in tiles]
            + [("mla", h, q, 2 if q < 2 else 4) for h in range(8) for q in tiles])


def build(nc, w, tab, out, plan, ctx):
    sems = {}

    def sem_of(name):
        if name not in sems:
            sems[name] = ctx.enter_context(nc.semaphore(name))
        return sems[name]

    plan.start(sem_of)
    mark, dma, when, full, drained, drain = plan.mark, plan.dma, plan.when, plan.full, plan.drained, plan.drain

    def sb(name, shape):
        return ctx.enter_context(nc.sbuf_tensor(name, shape, F32))

    def dram(name, shape):
        return nc.dram_tensor(name, shape, F32, kind="Internal").ap()

    PS = [ctx.enter_context(nc.psum_tensor(f"ps{b}", [P, 512], F32)) for b in range(NBANK)]

    def bank(*key):
        return PS[plan.index(*key) % NBANK]

    ARENA = 155 * 256
    arena = sb("arena", [P, ARENA])
    arena_at = nc.sbuf_base - 4 * ARENA
    ring = sb("ring", [P, NW, WSLOT])
    ring_at = nc.sbuf_base - 4 * NW * WSLOT
    cst = sb("cst", [P, NTAB])
    par = sb("par", [P, DEPTH, NPAR])
    par2 = sb("par2", [P, DEPTH, NPAR2])
    csil = sb("csil", [P, KT, 2])
    mods_all = sb("mods", [P, DEPTH, 48, 2])
    gsc_all = sb("gsc", [P, DEPTH, 2, KT, 2])
    mrow = sb("mrow", [32, 3, P])
    lora = sb("lora", [P, 3, RW])
    lam_all = sb("lam", [P, DEPTH, 8])
    subg = sb("subg", [P, 1])
    mu0 = sb("mu0", [P, 15])
    kaneg = sb("kaneg", [P, 4])
    smax = sb("smax", [P, 2, 64])
    ssum = sb("ssum", [P, 2, 64])
    rsum = sb("rsum", [P, 2, 64])
    dend = sb("dend", [P, 8, NCH])

    def view(kb, shape):
        o, n = int(kb * 256), int(np.prod(shape))
        assert o + n <= ARENA
        v = arena[:, o:o + n]
        names = "abcd"[:len(shape)]
        if len(shape) == 1:
            return v
        return v.rearrange("p (%s) -> p %s" % (" ".join(names), " ".join(names)),
                           **{n: s for n, s in zip(names, shape)})

    def rounded(name, kb, shape):
        return nc.alloc_sbuf_tensor_at(name, [P, *shape], F32R, offset=arena_at + int(1024 * kb))

    w_lo = nc.alloc_sbuf_tensor_at("w_lo", [P, NW, WSLOT], F32R, offset=ring_at)
    w_hi = rounded("w_hi", 136, [NHI, KT, P])
    h2_hi = rounded("h2_hi", 0, [KT, T])
    h2_lo = rounded("h2_lo", 16, [KT, T])
    h2_raw = view(16, [KT, T])
    f_lo = rounded("f_lo", 72, [FT, T])
    f_raw = view(72, [FT, T])
    f_hi_a, f_hi_b = rounded("f_hi_a", 32, [12, T]), rounded("f_hi_b", 116, [FT - 12, T])

    def f_hi(k, toks):
        return f_hi_a[:, k, toks] if k < 12 else f_hi_b[:, k - 12, toks]

    H = view(0, [KT, T])
    X = view(16, [KT, T])
    M = view(16, [KT, T])
    YB = view(32, [4, T])
    YC = view(40, [4, T])
    QK = view(48, [8, T])
    VD = view(64, [4, T])
    ZC = view(72, [6, T])
    MQ = view(84, [8, T])
    MK = view(100, [8, T])
    MV = view(116, [4, T])
    PR = view(124, [3, 2, T])
    PT = view(136, [2, T])
    ROT = view(140, [2, HALF])
    SQ = view(142, [2, T])
    SQH = view(0, [2, T])
    RS = view(153, [T])
    prow = view(96, [DEPTH, 2, P])
    lamv_all = view(94, [DEPTH, 256])
    TOK = view(146, [KT * P])
    ZS = view(48, [15, T])
    KK = view(78, [4, T])
    BV = view(86, [4, T])
    SG = view(94, [T])
    AI = view(96, [T])
    TA, TB = view(98, [T]), view(100, [T])
    W65 = view(102, [NCH * (C + 1)])
    E65 = view(104.125, [NCH * (C + 1)])
    RI = view(106.25, [T])
    GT = view(106.25, [T])
    AR = view(108.25,  [2, NCH, P])
    BK = view(116.25, [NCH, P])
    BH = view(120.25, [NCH, P])
    BKT = view(144.25, [2, NCH, P])
    AS = view(136.25, [4, 4, P])
    GS = view(132.25, [2, T])
    VT = view(116.25, [4, T])
    AROWF = view(116.25, [2, 2048])
    NB = view(136.25, [C, C])
    NT = view(112, [C * C // 4])
    NTP = view(108.25, [(C - CSPLIT) * C])
    cA = view(48, [2, 16, P])
    cX = view(64, [2, 16, C])
    cR = view(134, [2, 8, P])
    cB = view(94, [2, 8, P])
    cV = view(102, [2, 2, T])
    S = view(110, [8, P])
    R = view(114, [8, P])
    Y = view(118, [2, 4, T])
    YA = view(48, [4, T])
    X2 = view(56, [KT, T])
    RO = [view(94, [4, T]), view(102, [4, T])]
    GATE = view(136, [2, T])

    ident, ones, bones = cst[:, IDENT:IDENT + P], cst[:, ONES:ONES + P], cst[:, BONES:BONES + P]
    m_dram = dram("mod_rows", [DEPTH, 3, 2, 2048])
    xdram = dram("x_spill", [P, KT * T])
    a_dram = dram("a_spill", [NCH, P, 16, P])
    r_dram = dram("r_spill", [NCH, P, 8, P])
    b_dram = dram("b_spill", [NCH, P, 8, P])
    v_dram = dram("v_spill", [T, RW])
    vr_dram = dram("v_reversed", [T, RW])
    i_dram = dram("i_spill", [P, C, C])

    def directed(ap, d):
        v = ap.rearrange("p (h c t) -> p h c t", h=2, t=C)
        return v[:, :, ::-1, ::-1] if d else v

    def chunked(ap):
        return ap.rearrange("p (h c) t -> p h c t", h=2)

    def sides(l):
        return (0, 1) if l == 0 else (1,)

    def outs(l):
        return slice(0, T) if l == 0 else LAT

    chunk_list = [c for l in range(DEPTH) for c in weight_chunks(w, l)]
    chunk_at, split_at = {}, {}
    n = 0
    for l in range(DEPTH):
        for c in weight_chunks(w, l):
            chunk_at[(l, c[0])] = n
            n += 1
    split_list = [(l, name, half) for l in range(DEPTH) for name, half in split_halves(l)]
    for m, (l, name, half) in enumerate(split_list):
        split_at[(l, name, half)] = m

    def half_views(m, ring_tensor):
        l, name, half = split_list[m]
        n = chunk_at[(l, name)]
        _, nk, nn, _ = chunk_list[n]
        slot = ring_tensor[:, n % NW, 0:nk * nn].rearrange("p (k n) -> p k n", n=nn)
        return slot[:, :, P * half:P * half + P], w_hi[:, m % NHI, 0:nk, :], n

    block = ctx.enter_context(nc.Block())

    @block.sync
    def _(sp):
        sp.dma_start(cst[:, :], tab).then_inc(*dma("tables"))
        n = 0
        rows = [("rwkv_shift_mu", MU, 30), ("norm1_g", N1, 8), ("norm2_g", N2, 8), ("rwkv_w0", W0, 8),
                ("rwkv_a0", A0C, 8), ("rwkv_k_k", KKC, 4), ("rwkv_k_a", KAC, 4), ("rwkv_r_k", RKC, 4),
                ("rwkv_ln_w", LNW, 4), ("rwkv_ln_b", LNB, 4), ("diff_subln_g", SUBG, 1),
                ("mla_q_norm_g", QNG, 3), ("mla_kv_norm_g", KVG, 2)]
        for l in range(DEPTH):
            for src, r0, nr in ((w["ada_b"][l], ADAB, 48), (w["final_norm_g"], FING, 8),
                                (w["c"][0], CVEC, 8), (w["c_ctx"], CCTX, 8)):
                sp.dma_start(prow[r0:r0 + nr, l, 1, :], src.rearrange("(r n) -> r n", n=P)).then_inc(*dma(f"prow2_{l}"))
        for l in range(DEPTH):
            if l:
                sp.wait_ge(*full("lora_g", l - 1, 3))
            for i, name in enumerate(("rwkv_w2", "rwkv_a2")):
                sp.dma_start(lora[:, i, :], w[name][l].rearrange("d k n -> (d k) n")).then_inc(*dma("lora", l))
            sp.dma_start(lora[:, 2, :], w["rwkv_g2"][l]).then_inc(*dma("lora", l))
            for name, nk, nn, parts in weight_chunks(w, l):
                if n >= NW:
                    sp.wait_ge(*plan.released(n - NW))
                slot = ring[:, n % NW, 0:nk * nn].rearrange("p (k n) -> p k n", n=nn)
                for c0, c1, k0, k1, src in parts:
                    sp.dma_start(slot[:, k0:k1, c0:c1], src).then_inc(*dma(f"weights_in{n % NW}", n))
                n += 1
                if n == 4:
                    for ll in range(DEPTH):
                        for name, r0, nr in rows:
                            src = w[name][ll]
                            if len(src.shape) == 2:
                                src = src.rearrange("a b -> (a b)")
                            sp.dma_start(prow[r0:r0 + nr, ll, 0, :], src.rearrange("(r n) -> r n", n=P)).then_inc(*dma(f"prow_{ll}"))
                        sp.dma_start(lamv_all[:, ll, :], w["diff_lambda"][ll].rearrange("a b -> (a b)").partition_broadcast(P)).then_inc(*dma(f"lamv_{ll}"))

    @block.gpsimd
    def _(pool):
        for i in range(4):
            if i:
                pool.wait_ge(*full("xin", i - 1, 1))
            src = w["ctx"][0] if i < 2 else w["x"][0]
            pool.dma_start(TOK, src[P * (i % 2):P * (i % 2) + P, :]).then_inc(*dma("tok", i))
        for l in range(DEPTH):
            for key in [("fd", l - 1, k) for k in range(KT)] if l else [("xin", i, h) for i in range(4) for h in range(2)]:
                pool.wait_ge(*drained(*key))
            pool.dma_start(xdram, X.rearrange("p k t -> p (k t)")).then_inc(*dma("x_spilled", l))
            for c in range(NCH):
                pool.wait_ge(*drained("vtok", l, c))
                pool.dma_start(v_dram[C * c:C * c + C, :], VT[0:C, c % 4, :]).then_inc(*dma(f"v_spilled{c % 4}", l, c))
            for c in range(NCH):
                pool.wait_ge(*when(f"v_spilled{c % 4}", l, c))
            for h in range(2):
                rows = slice(HALF * h, HALF * h + HALF)
                src = v_dram[rows, :].rearrange("t (h v) -> h t v", h=8)[:, ::-1, :]
                pool.dma_start(vr_dram[rows, :].rearrange("t (h v) -> h t v", h=8), src).then_inc(*dma("v_reversed", l))
            for i in range(8):
                pool.wait_ge(*when("bk", l, i))
                if i:
                    pool.wait_ge(*full("bkt", l, i - 1, 1))
                nc.gpsimd.tensor_tensor(BH, BK, dend[:, i, :].unsqueeze(2).broadcast_to([P, NCH, P]), ALU.mult).then_inc(*mark("bh", l, i))
            for g in range(4):
                pool.wait_ge(*when(f"a_spilled{g}", l, 7))
            for i in (6, 7):
                pool.wait_ge(*when(f"b_spilled{i % 2}", l, i))
            for c in range(NCH):
                pool.dma_start(NB[16 * c:16 * c + 16], a_dram[c, 0:C, :, 0:C].rearrange("s u t -> u s t")).then_inc(*dma("nb_in", l))
            pool.wait_ge(*when("nb_in", l))
            for i in (6, 7):
                pool.wait_ge(*when(f"r_spilled{i % 2}", l, i))
            for s in range(1, C - 1):
                t0 = max(s + 1, CSPLIT)
                n = C - t0
                tmp = NTP[:, 0:s * n].rearrange("p (j t) -> p j t", t=n)
                if 2 <= s < CSPLIT:
                    pool.wait_ge(*when("inverse_col", l, s))
                nc.gpsimd.tensor_tensor(tmp, NB[:, 0:s, s:s + 1].broadcast_to([P, s, n]), NB[:, s:s + 1, t0:C].broadcast_to([P, s, n]), ALU.mult).then_inc(*mark("inverse_term", l, s))
                pool.wait_ge(*when("inverse_term", l, s))
                nc.gpsimd.tensor_tensor(NB[:, 0:s, t0:C], NB[:, 0:s, t0:C], tmp, ALU.add).then_inc(*mark("inverse_right", l, s))
                pool.wait_ge(*when("inverse_right", l, s))
            pool.wait_ge(*when("inverted", l))
            pool.dma_start(i_dram.rearrange("u s t -> u (s t)"), NB.rearrange("p s t -> p (s t)")).then_inc(*dma("inverse_out", l))
            pool.wait_ge(*when("inverse_out", l))
            for i in (6, 7):
                pool.wait_ge(*when(f"r_spilled{i % 2}", l, i))
            pool.wait_ge(*when("v_reversed", l))
            for p in range(4):
                pool.wait_ge(*drained("bonus", l, p))
            for c in range(NCH):
                b = c % 2
                if c >= 2:
                    pool.wait_ge(*full("S", l, c - 2, 1))
                    if not (l and c - 2 < 4):
                        pool.wait_ge(*full("Y", l, c - 2, 1))
                name = f"chunk_in{b}"
                pool.dma_start(cA[:, b], a_dram[c]).then_inc(*dma(name, l, c))
                pool.dma_start(cX[0:C, b], i_dram[16 * c:16 * c + 16].rearrange("u s t -> s u t")).then_inc(*dma(name, l, c))
                pool.dma_start(cR[:, b], r_dram[c]).then_inc(*dma(name, l, c))
                pool.dma_start(cB[:, b], b_dram[c]).then_inc(*dma(name, l, c))
                pool.dma_start(cV[C:P, b, 0], v_dram[C * c:C * c + C, :]).then_inc(*dma(name, l, c))
                pool.dma_start(cV[C:P, b, 1], vr_dram[C * c:C * c + C, :]).then_inc(*dma(name, l, c))
            pool.wait_ge(*full("S", l, NCH - 1, 1))
            pool.wait_ge(*full("Y", l, NCH - 1, 1))
            pool.dma_start(X2.rearrange("p k t -> p (k t)"), xdram).then_inc(*dma("x_back", l))
        for i in range(2):
            pool.wait_ge(*drained("xout", i, 1))
            pool.dma_start(out[0, P * i:P * i + P, :], TOK).then_inc(*dma("stored", i))
            pool.wait_ge(*when("stored", i))

    @block.tensor
    def _(pe):
        chunk_no = [0]
        chunk_of = {}

        def job(*key):
            n = plan.job(*key)
            if n >= NBANK:
                pe.wait_ge(sem_of(f"psum_drained{n % NBANK}"), n // NBANK)
            return PS[n % NBANK]

        def done(*key):
            n = plan.jobs[key]
            return sem_of(f"psum_full{n % NBANK}"), 1

        def weights(l, *name):
            n = chunk_no[0]
            chunk_no[0] += 1
            got, nk, nn, _ = chunk_list[n]
            assert got == name, (got, name)
            pe.wait_ge(*when(f"weights_in{n % NW}", n))
            chunk_of[name] = n
            return ring[:, n % NW, 0:nk * nn].rearrange("p (k n) -> p k n", n=nn)

        def release(name, *key):
            plan.release[chunk_of[name]] = key

        def sum_rows(key, tiles, lhs, toks, sq=SQ):
            ps = job(*key)
            n = toks.stop - toks.start
            for k in range(tiles):
                pe.wait_ge(*when("sq", *key, k))
                mm = pe.matmul(ps[:, 0:n], lhs, sq[:, k % 2, toks], start=(k == 0), stop=(k == tiles - 1))
                if k < tiles - 1:
                    mm.then_inc(*mark("squares_read", *key, k))
            mm.then_inc(*done(*key))

        def project(key, wt, c0, m, rhs, nk, ps_rows=slice(0, P), n=T, ready=None):
            ps = job(*key)
            for k in range(nk):
                if ready:
                    pe.wait_ge(*ready(k))
                mm = pe.matmul(ps[ps_rows, 0:n], wt[:, k, c0:c0 + m], rhs(k), start=(k == 0), stop=(k == nk - 1))
            mm.then_inc(*done(*key))

        def project_split(key, l, name, half, x_hi, x_lo, n, first=0, last=None, ready=None, split_ready=True):
            m = split_at[(l, name, half)]
            lo, hi, chunk = half_views(m, w_lo)
            ps = bank(*key)
            nk = chunk_list[chunk][1]
            last = first + nk if last is None else last
            pe.wait_ge(*when("w_lo", m))
            for k in range(nk):
                if ready:
                    pe.wait_ge(*ready(first + k))
                start, stop = first + k == 0, first + k == last - 1
                pe.matmul(ps[:, 0:n], hi[:, k, :], x_hi(first + k), start=start, stop=False, skip_group_check=True)
                pe.matmul(ps[:, 0:n], hi[:, k, :], x_lo(first + k), start=False, stop=False, skip_group_check=True)
                mm = pe.matmul(ps[:, 0:n], lo[:, k, :], x_hi(first + k), start=False, stop=stop, skip_group_check=True)
            if stop:
                mm.then_inc(*done(*key))
                plan.read[m] = key
            else:
                mm.then_inc(*mark("half_read", m))
                plan.read[m] = ("mark", "half_read", m)

        pe.wait_ge(*when("tables"))
        for i in range(4):
            pe.wait_ge(*when("tok", i))
            for h in range(2):
                ps = job("xin", i, h)
                for k in range(4):
                    mm = pe.transpose(ps[:, P * k:P * k + P], TOK[:, P * (4 * h + k):P * (4 * h + k) + P], ident)
                mm.then_inc(*done("xin", i, h))

        def modulation(l, part):
            for j in range(8 * part, 8 * part + 8):
                wt = weights(l, "ada", l, j)
                ps = job("ada", l, j)
                for k in range(KT):
                    mm = pe.matmul(ps[0:2, 0:256], csil[:, k, :], wt[:, k, :], start=(k == 0), stop=(k == KT - 1))
                mm.then_inc(*done("ada", l, j))
                release(("ada", l, j), "ada", l, j)

        def modulation_columns(l, part):
            pe.wait_ge(*when(f"mods_in_{l}_{part}"))
            ps = job("modt", l, part)
            pe.transpose(ps[:, 0:32], mrow[:, part, :], cst[0:32, IDENT:IDENT + 32]).then_inc(*done("modt", l, part))

        for l in range(DEPTH):
            pe.wait_ge(*when(f"prow2_{l}"))
            ps = job("par2", l)
            pe.transpose(ps[:, 0:NPAR2], prow[0:NPAR2, l, 1, :], cst[0:NPAR2, IDENT:IDENT + NPAR2]).then_inc(*done("par2", l))
        pe.wait_ge(*when("csil"))
        modulation(0, 0)
        for l in range(DEPTH):
            pe.wait_ge(*when(f"prow_{l}"))
            ps = job("par", l)
            pe.transpose(ps[:, 0:NPAR], prow[0:NPAR, l, 0, :], cst[0:NPAR, IDENT:IDENT + NPAR]).then_inc(*done("par", l))
        modulation_columns(0, 0)

        for l in range(DEPTH):
            o = outs(l)
            no = o.stop - o.start
            sum_rows(("n1", l), KT, ones, slice(0, T), SQH)
            for j in range(4):
                wt = weights(l, "B", j)
                for jj in range(2):
                    b = 2 * j + jj
                    tk = o if b < 4 else slice(0, T)
                    project(("qk", l, b), wt, P * jj, P, lambda k: H[:, k, tk], KT, n=tk.stop - tk.start,
                            ready=(lambda k: when("h1", l, k)) if b == 0 else None)
                    if b >= 1:
                        pe.wait_ge(*drained("qk", l, b - 1))
                        ps = job("qkrot", l, b - 1)
                        pe.matmul(ps[:, 0:HALF], cst[:, PERM:PERM + P], QK[:, b - 1, LAT], start=True, stop=True).then_inc(*done("qkrot", l, b - 1))
                release(("B", j), "qk", l, 2 * j + 1)
            for j in range(2):
                wt = weights(l, "B", 4 + j)
                for t in range(4):
                    ps = job("vd", l, j, t)
                    for k in range(KT):
                        mm = pe.matmul(ps[:, 0:256], H[:, k, P * t:P * t + P], wt[:, k, :], start=(k == 0), stop=(k == KT - 1))
                    mm.then_inc(*done("vd", l, j, t))
                release(("B", 4 + j), "vd", l, j, 3)
            pe.wait_ge(*drained("qk", l, 7))
            ps = job("qkrot", l, 7)
            pe.matmul(ps[:, 0:HALF], cst[:, PERM:PERM + P], QK[:, 7, LAT], start=True, stop=True).then_inc(*done("qkrot", l, 7))
            wt = weights(l, "C", 0)
            for b in (0, 1):
                project(("zc", l, b), wt, P * b, P, lambda k: H[:, k, o], KT, n=no)
            release(("C", 0), "zc", l, 1)
            wt = weights(l, "C", 1)
            project(("zc", l, 2), wt, 0, P, lambda k: H[:, k, o], KT, n=no)
            project(("zc", l, 3), wt, P, P, lambda k: H[:, k, :], KT)
            release(("C", 1), "zc", l, 3)
            wt = weights(l, "C", 2)
            project(("zc", l, 4), wt, 0, P, lambda k: H[:, k, :], KT)
            project(("zc", l, 5), wt, P, 32, lambda k: H[:, k, :], KT, ps_rows=slice(64, 96))
            release(("C", 2), "zc", l, 5)
            sum_rows(("qn", l), 3, ones, o)
            sum_rows(("kvn", l), 2, ones, slice(0, T))
            pe.wait_ge(*drained("zc", l, 5))
            ps = job("krot", l)
            pe.matmul(ps[64:96, 0:HALF], cst[64:96, PERM32:PERM32 + 32], ZC[64:96, 5, LAT], start=True, stop=True).then_inc(*done("krot", l))
            for k in range(3):
                pe.wait_ge(*when("qnorm", l, k))
            for j in range(2):
                wt = weights(l, "uq", j)
                for hh in range(4):
                    h = 4 * j + hh
                    project(("mq", l, h), wt, 96 * hh, 96, lambda k: ZC[:, k, o], 3, ps_rows=slice(0, 96), n=no)
                    if h >= 1:
                        pe.wait_ge(*drained("mq", l, h - 1))
                        ps = job("mqrot", l, h - 1)
                        pe.matmul(ps[64:96, 0:HALF], cst[64:96, PERM32:PERM32 + 32], MQ[64:96, h - 1, LAT], start=True, stop=True).then_inc(*done("mqrot", l, h - 1))
                release(("uq", j), "mq", l, 4 * j + 3)
            for k in range(2):
                pe.wait_ge(*when("kvnorm", l, k))
            wt = weights(l, "uk")
            for j in range(4):
                project(("mk", l, j), wt, P * j, P, lambda k: ZC[:, 3 + k, :], 2)
            release(("uk",), "mk", l, 3)
            wt = weights(l, "uv")
            for t in range(4):
                ps = job("mv", l, t)
                for k in range(2):
                    mm = pe.matmul(ps[:, :], ZC[:, 3 + k, P * t:P * t + P], wt[:, k, :], start=(k == 0), stop=(k == 1))
                mm.then_inc(*done("mv", l, t))
            release(("uv",), "mv", l, 3)
            pe.wait_ge(*drained("mq", l, 7))
            ps = job("mqrot", l, 7)
            pe.matmul(ps[64:96, 0:HALF], cst[64:96, PERM32:PERM32 + 32], MQ[64:96, 7, LAT], start=True, stop=True).then_inc(*done("mqrot", l, 7))

            units = attention_units(l)

            def scores(i):
                kind, h, q, nk = units[i]
                qs = slice(P * q, P * q + P)
                if kind == "diff":
                    if i == 0:
                        for b in range(8):
                            pe.wait_ge(*when("qk_ready", l, b))
                    for c in range(2):
                        ps = job("sc", l, i, c)
                        pe.matmul(ps[:, 0:P * nk], QK[64 * c:64 * c + 64, h, qs], QK[64 * c:64 * c + 64, 4 + h, 0:P * nk],
                                  start=True, stop=True).then_inc(*done("sc", l, i, c))
                else:
                    if units[i - 1][0] == "diff":
                        pe.wait_ge(*when("mk_rope", l))
                        for j in range(4):
                            pe.wait_ge(*drained("mk", l, j))
                        for j in range(8):
                            pe.wait_ge(*when("mq_ready", l, j))
                    ps = job("sc", l, i, 0)
                    pe.matmul(ps[:, 0:P * nk], MQ[0:96, h, qs], MK[0:96, h, 0:P * nk], start=True, stop=True).then_inc(*done("sc", l, i, 0))

            def transposed(i):
                kind, h, q, nk = units[i]
                pe.wait_ge(*when("probs", l, i))
                ps = job("pt", l, i)
                for t in range(nk):
                    mm = pe.transpose(ps[:, P * t:P * t + P], PR[:, i % 3, 0, P * t:P * t + P], ident)
                mm.then_inc(*done("pt", l, i))

            def values(i):
                kind, h, q, nk = units[i]
                pe.wait_ge(*drained("pt", l, i))
                if i == 0:
                    for j in range(2):
                        for t in range(4):
                            pe.wait_ge(*drained("vd", l, j, t))
                    for t in range(4):
                        pe.wait_ge(*drained("mv", l, t))
                ps = job("av", l, i)
                for t in range(nk):
                    if kind == "diff":
                        mm = pe.matmul(ps[:, 0:P], VD[:, t, P * h:P * h + P], PT[:, i % 2, P * t:P * t + P], start=(t == 0), stop=(t == nk - 1))
                    else:
                        r = 64 * (h % 2)
                        mm = pe.matmul(ps[r:r + 64, 0:P], MV[:, t, 64 * h:64 * h + 64], PT[:, i % 2, P * t:P * t + P], start=(t == 0), stop=(t == nk - 1))
                mm.then_inc(*done("av", l, i))

            scores(0)
            scores(1)
            for i in range(len(units)):
                if i + 2 < len(units):
                    scores(i + 2)
                if i >= 1:
                    values(i - 1)
                transposed(i)
            values(len(units) - 1)
            for h in range(4):
                sum_rows(("bn", l, h), 1, ones, o)

            for j in range(8):
                wt = weights(l, "A", j)
                for jj in range(2 if j < 7 else 1):
                    b = 2 * j + jj
                    tk = o if b < 4 or b == 14 else slice(0, T)
                    project(("za", l, b), wt, P * jj, P, lambda k: H[:, k, tk], KT, n=tk.stop - tk.start)
                release(("A", j), "za", l, min(2 * j + 1, 14))
            for p in range(4):
                sum_rows(("kkn", l, p), 1, bones, slice(0, T))
            for c in range(NCH):
                if c == 0:
                    for p in range(4):
                        pe.wait_ge(*drained("za", l, 8 + p))
                ps = job("vtok", l, c)
                for p in range(4):
                    mm = pe.transpose(ps[0:C, P * p:P * p + P], ZS[:, 8 + p, C * c:C * c + C], ident)
                mm.then_inc(*done("vtok", l, c))

            def branch12(d):
                wt = weights(l, "G12", d)
                for g in range(2):
                    project(("g12", l, d, g), wt, P * g, P, lambda k: H[:, k, o], KT, n=no)
                release(("G12", d), "g12", l, d, 1)
                wt = weights(l, "W12", d)
                if d == 0:
                    for h in range(4):
                        pe.wait_ge(*when("yb", l, h))
                    for i in range(len(units)):
                        if units[i][0] == "mla":
                            pe.wait_ge(*drained("av", l, i))
                for g, y in enumerate((YB, YC)):
                    ps = job("w12", l, d, g)
                    for k in range(4):
                        mm = pe.matmul(ps[:, 0:no], wt[:, 4 * g + k, :], y[:, k, o], start=(k == 0), stop=(k == 3))
                    mm.then_inc(*done("w12", l, d, g))
                release(("W12", d), "w12", l, d, 1)

            def lora_in(i):
                d, p = i // 4, i % 4
                rows = slice(64 * d, 64 * d + 64)
                for n, name in enumerate(("lora_w", "lora_a")):
                    if i == 0 and n == 0:
                        pe.wait_ge(*when("lora", l))
                        pe.wait_ge(*when("tanh", l))
                        pe.wait_ge(*drained("za", l, 13))
                    ps = job(name, l, i)
                    pe.matmul(ps[:, :], lora[rows, n, P * p:P * p + P], ZS[rows, 12 + n, :], start=True, stop=True).then_inc(*done(name, l, i))

            def scores_in_chunk(i):
                pe.wait_ge(*when("ar", l, i))
                pe.wait_ge(*when("bk", l, i))
                for g in range(0, 4, 2):
                    pss = [job("A", l, i, g + hh) for hh in range(2)]
                    for c in range(4):
                        for hh in range(2):
                            ch = 4 * (g // 2) + c
                            rows = slice(64 * hh, 64 * hh + 64)
                            mm = pe.matmul(pss[hh][:, P * c:P * c + P], BK[rows, ch, :], AR[rows, i % 2, ch, :], start=True, stop=True)
                            if c == 3:
                                mm.then_inc(*done("A", l, i, g + hh))
                pe.wait_ge(*when("bh", l, i))
                for g in range(2):
                    ps = job("bkt", l, i, g)
                    for c in range(4):
                        mm = pe.transpose(ps[:, P * c:P * c + P], BH[:, 4 * g + c, :], ident)
                    mm.then_inc(*done("bkt", l, i, g))

            lora_in(0)
            lora_in(1)
            for i in range(8):
                if i < 4:
                    branch12(i)
                if i + 2 < 8:
                    lora_in(i + 2)
                scores_in_chunk(i)
            for p in range(4):
                pe.wait_ge(*when("rkk", l, p))
                ps = job("bonus", l, p)
                pe.matmul(ps[:, 0:no], bones, BV[:, p, o], start=True, stop=True).then_inc(*done("bonus", l, p))
            for d in range(4, 8):
                branch12(d)
            modulation(l, 1)
            modulation(l, 2)
            if l + 1 < DEPTH:
                modulation(l + 1, 0)

            def gate0(d):
                wt = weights(l, "G0", d)
                project(("g0", l, d), wt, 0, P, lambda k: H[:, k, o], KT, n=no)
                release(("G0", d), "g0", l, d)

            if l == DEPTH - 1:
                for d in range(8):
                    gate0(d)

            def state_key(c, g):
                return ("S", l, c, g)

            pe.wait_ge(*when("state_zero", l))
            for c in range(NCH):
                b = c % 2
                pe.wait_ge(*when(f"chunk_in{b}", l, c))
                for g in range(2):
                    ps = job("U", l, c, g)
                    if c:
                        pe.wait_ge(*drained("S", l, c - 1, g))
                    for ii in range(4):
                        i = 4 * g + ii
                        pe.matmul(ps[0:C, P * ii:P * ii + P], cR[:, b, i, 0:C], S[:, i, :], start=True, stop=False, skip_group_check=True)
                        for hh in range(2):
                            v0 = P * (i % 4) + C * hh
                            mm = pe.matmul(ps[0:C, P * ii + C * hh:P * ii + C * hh + C], cA[C:P, b, 2 * i + hh, 0:C],
                                           cV[C:P, b, i // 4, v0:v0 + C], start=False, stop=True, skip_group_check=True)
                    mm.then_inc(*done("U", l, c, g))
                for g in range(2):
                    ps = job("SA", l, c, g)
                    pe.wait_ge(*drained("U", l, c, g))
                    for ii in range(4):
                        i = 4 * g + ii
                        for hh in range(2):
                            mm = pe.matmul(ps[0:C, P * ii + C * hh:P * ii + C * hh + C], cX[0:C, b, 2 * i + hh, :],
                                           R[0:C, i, C * hh:C * hh + C], start=True, stop=True)
                    mm.then_inc(*done("SA", l, c, g))
                yjobs = not (l and c < 4)
                for g in range(2):
                    pe.wait_ge(*drained("SA", l, c, g))
                    if yjobs:
                        ps = job("Y", l, c, g)
                        for ii in range(4):
                            i = 4 * g + ii
                            pe.matmul(ps[:, C * ii:C * ii + C], S[:, i, :], cR[:, b, i, C:P], start=True, stop=False, skip_group_check=True)
                            for hh in range(2):
                                v0 = P * (i % 4) + C * hh
                                mm = pe.matmul(ps[C * hh:C * hh + C, C * ii:C * ii + C], cV[:, b, i // 4, v0:v0 + C],
                                               cA[:, b, 2 * i + hh, C:P], start=False, stop=True, skip_group_check=True)
                        mm.then_inc(*done("Y", l, c, g))
                    ps = job("S", l, c, g)
                    for ii in range(4):
                        i = 4 * g + ii
                        mm = pe.matmul(ps[:, P * ii:P * ii + P], cB[:, b, i, :], cV[:, b, i // 4, P * (i % 4):P * (i % 4) + P],
                                       start=True, stop=True)
                    mm.then_inc(*done("S", l, c, g))

            modulation_columns(l, 1)
            modulation_columns(l, 2)
            if l + 1 < DEPTH:
                modulation_columns(l + 1, 0)
            pe.wait_ge(*when("gd", l))
            for p in range(4):
                pe.wait_ge(*when("ysum", l, p))
                ps = job("gmean", l, p)
                pe.matmul(ps[:, 0:no], bones, Y[:, 0, p, o], start=True, stop=True).then_inc(*done("gmean", l, p))
            for p in range(4):
                ps = job("lora_g", l, p)
                pe.matmul(ps[:, 0:no], lora[:, 2, P * p:P * p + P], ZS[:, 14, o], start=True, stop=True).then_inc(*done("lora_g", l, p))
            for p in range(4):
                pe.wait_ge(*when("ysq", l, p))
                ps = job("gvar", l, p)
                pe.matmul(ps[:, 0:no], bones, RO[0][:, p, o], start=True, stop=True).then_inc(*done("gvar", l, p))

            for d in range(8):
                if l < DEPTH - 1:
                    gate0(d)
                wt = weights(l, "W0", d)
                if d == 0:
                    for p in range(4):
                        pe.wait_ge(*drained("lora_g", l, p))
                ps = job("w0", l, d)
                for k in range(4):
                    mm = pe.matmul(ps[:, 0:no], wt[:, k, :], YA[:, k, o], start=(k == 0), stop=(k == 3))
                mm.then_inc(*done("w0", l, d))
                release(("W0", d), "w0", l, d)
            for d in range(8):
                pe.wait_ge(*when("merged", l, d))
            for j in range(4):
                wt = weights(l, "O", j)
                for jj in range(2):
                    project(("wo", l, 2 * j + jj), wt, P * jj, P, lambda k: M[:, k, o], KT, n=no)
                release(("O", j), "wo", l, 2 * j + 1)
            sum_rows(("n2", l), KT, ones, o, SQH)
            for j in range(11):
                weights(l, "FG", j)
                weights(l, "FU", j)
                for jj in range(2):
                    for key, name in ((("fg", l, 2 * j + jj), "FG"), (("fu", l, 2 * j + jj), "FU")):
                        job(*key)
                        project_split(key, l, (name, j), jj, lambda k: h2_hi[:, k, o], lambda k: h2_lo[:, k, o], no,
                                      ready=(lambda k: when("h2", l, k)) if key[2] == 0 and name == "FG" else None)
                release(("FG", j), "fg", l, 2 * j + 1)
                release(("FU", j), "fu", l, 2 * j + 1)
            for dp in range(4):
                for jj in range(2):
                    job("fd", l, 2 * dp + jj)
                for kc, (k0, k1) in enumerate(((0, 8), (8, 16), (16, 22))):
                    weights(l, "FD", dp, kc)
                    for jj in range(2):
                        project_split(("fd", l, 2 * dp + jj), l, ("FD", dp, kc), jj, lambda k: f_hi(k, o), lambda k: f_lo[:, k, o], no,
                                      first=k0, last=FT, ready=(lambda k: when("ffn_hidden", l, k)) if dp == 0 and jj == 0 else None)
                    plan.release[chunk_of[("FD", dp, kc)]] = plan.read[split_at[(l, ("FD", dp, kc), 1)]]
        sum_rows(("nf",), KT, ones, LAT, SQH)
        for k in range(KT):
            pe.wait_ge(*when("final", k))
        for i in range(2):
            for h in range(2):
                ps = job("xout", i, h)
                for k in range(4):
                    mm = pe.transpose(ps[:, P * k:P * k + P], H[:, 4 * h + k, HALF + P * i:HALF + P * i + P], ident)
                mm.then_inc(*done("xout", i, h))

    @block.scalar
    def _(act):
        A = nc.scalar.activation

        def step(ins):
            ins.then_inc(*mark("act_step", plan.count.get("act_step", 0)))
            act.wait_ge(sem_of("act_step"), plan.count["act_step"])

        def weights_rounded(m):
            raw, hi, n = half_views(m, ring)
            act.wait_ge(*when(f"weights_in{n % NW}", n))
            if m >= NHI:
                act.wait_ge(*plan.half_read(m - NHI))
            A(hi, raw, ACT.Copy).then_inc(*mark("w_hi", m))

        def squares(key, src, tiles, toks, sq=SQ):
            for k in range(tiles):
                if k >= 2:
                    act.wait_ge(*when("squares_read", *key, k - 2))
                elif last_sum[0] is not None:
                    act.wait_ge(*full(*last_sum[0]))
                A(sq[:, k % 2, toks], src(k), ACT.Square).then_inc(*mark("sq", *key, k))
            last_sum[0] = key

        last_sum = [None]

        def root(key, toks):
            act.wait_ge(*drained(*key))
            A(RS[:, toks], RS[:, toks], ACT.Sqrt).then_inc(*mark("root", *key))

        for i in range(4):
            for h in range(2):
                act.wait_ge(*full("xin", i, h))
                A(X[:, 4 * h:4 * h + 4, P * i:P * i + P], bank("xin", i, h)[:, :].rearrange("p (k t) -> p k t", k=4), ACT.Copy).then_inc(*drain("xin", i, h))
        def modulation(l, part):
            for j in range(8 * part, 8 * part + 8):
                act.wait_ge(*full("ada", l, j))
                if j == 8 * part and (l, part) == (1, 2):
                    act.wait_ge(*when("mods_out_1_0"))
                    act.wait_ge(*when("mods_out_0_2"))
                if j == 8 * part and (l, part) == (1, 0):
                    act.wait_ge(*when("mods_out_0_1"))
                if j == 8 * part and part:
                    act.wait_ge(*full("bkt", l, 7, 1))
                A(AROWF[0:2, (l + part) % 2, 256 * (j % 8):256 * (j % 8) + 256], bank("ada", l, j)[0:2, 0:256], ACT.Copy).then_inc(*drain("ada", l, j))
            for j in range(8 * part, 8 * part + 8):
                act.wait_ge(*drained("ada", l, j))
            act.dma_start(m_dram[l, part], AROWF[0:2, (l + part) % 2, :]).then_inc(*dma(f"mods_out_{l}_{part}"))

        def modulation_back(l, part):
            act.wait_ge(*when(f"mods_out_{l}_{part}"))
            act.dma_start(mrow[:, part, :], m_dram[l, part].rearrange("s (j n) -> (s j) n", n=P)).then_inc(*dma(f"mods_in_{l}_{part}"))

        for l in range(DEPTH):
            act.wait_ge(*full("par2", l))
            A(par2[:, l, :], bank("par2", l)[:, 0:NPAR2], ACT.Copy).then_inc(*drain("par2", l))
        act.wait_ge(*drained("par2", 0))
        A(csil[:, :, 0], par2[:, 0, CCTX:CCTX + 8], ACT.Sigmoid).then_inc(*mark("csig", 0))
        A(csil[:, :, 1], par2[:, 0, CVEC:CVEC + 8], ACT.Sigmoid).then_inc(*mark("csig", 1))
        modulation(0, 0)
        modulation_back(0, 0)
        for l in range(DEPTH):
            act.wait_ge(*full("par", l))
            A(par[:, l, :], bank("par", l)[:, 0:NPAR], ACT.Copy).then_inc(*drain("par", l))
        for l in range(DEPTH):
            act.wait_ge(*when("lam_dots", l))
            A(lam_all[:, l, 0:2], lam_all[:, l, 0:2], ACT.Exp).then_inc(*mark("lam_exp", l))
        act.wait_ge(*drained("xin", 3, 1))
        for l in range(DEPTH):
            mods = mods_all[:, l]
            o = outs(l)
            no = o.stop - o.start
            if l:
                for k in range(KT):
                    act.wait_ge(*drained("fd", l - 1, k))
            squares(("n1", l), lambda k: X[:, k, :], KT, slice(0, T), SQH)
            root(("n1", l), slice(0, T))
            for k in range(KT):
                for s in (0, 1):
                    tk = slice(HALF * s, HALF * s + HALF)
                    act.wait_ge(*when("h1_scaled", l, k, s))
                    A(H[:, k, tk], H[:, k, tk], ACT.Identity, bias=mods[:, k, s:s + 1]).then_inc(*mark("h1", l, k))
            for b in range(8):
                tk = o if b < 4 else slice(0, T)
                act.wait_ge(*full("qk", l, b))
                A(QK[:, b, tk], bank("qk", l, b)[:, 0:tk.stop - tk.start], ACT.Copy).then_inc(*drain("qk", l, b))
            for j in range(2):
                for t in range(4):
                    act.wait_ge(*full("vd", l, j, t))
                    A(VD[:, t, 256 * j:256 * j + 256], bank("vd", l, j, t)[:, 0:256], ACT.Copy).then_inc(*drain("vd", l, j, t))
            for b in range(6):
                tk = o if b < 3 else slice(0, T)
                rows = slice(0, P) if b < 5 else slice(64, 96)
                act.wait_ge(*full("zc", l, b))
                A(ZC[rows, b, tk], bank("zc", l, b)[rows, 0:tk.stop - tk.start], ACT.Copy).then_inc(*drain("zc", l, b))
            for b in range(5):
                act.wait_ge(*drained("zc", l, b))
            squares(("qn", l), lambda k: ZC[:, k, o], 3, o)
            squares(("kvn", l), lambda k: ZC[:, 3 + k, :], 2, slice(0, T))
            root(("qn", l), o)
            root(("kvn", l), slice(0, T))
            for h in range(8):
                act.wait_ge(*full("mq", l, h))
                A(MQ[0:96, h, o], bank("mq", l, h)[0:96, 0:no], ACT.Copy).then_inc(*drain("mq", l, h))
            for j in range(4):
                act.wait_ge(*full("mk", l, j))
                for hh in range(2):
                    ins = A(MK[0:64, 2 * j + hh, :], bank("mk", l, j)[64 * hh:64 * hh + 64, :], ACT.Copy)
                ins.then_inc(*drain("mk", l, j))
            for t in range(4):
                act.wait_ge(*full("mv", l, t))
                A(MV[:, t, :], bank("mv", l, t)[:, :], ACT.Copy).then_inc(*drain("mv", l, t))
            units = attention_units(l)

            def exponentials(i):
                kind, h, q, nk = units[i]
                scale = DIFF_SCALE if kind == "diff" else MLA_SCALE
                for c in range(2 if kind == "diff" else 1):
                    act.wait_ge(*when("negmax", l, i, c))
                    if i >= 3 and c == 0:
                        act.wait_ge(*full("pt", l, i - 3))
                    A(PR[:, i % 3, c, 0:P * nk], bank("sc", l, i, c)[:, 0:P * nk], ACT.Exp, bias=smax[:, c, i:i + 1],
                      scale=scale, accum_out=ssum[:, c, i:i + 1]).then_inc(*drain("sc", l, i, c))

            def evacuate(i):
                kind, h, q, nk = units[i]
                act.wait_ge(*full("pt", l, i))
                if i >= 2:
                    act.wait_ge(*full("av", l, i - 2))
                A(PT[:, i % 2, 0:P * nk], bank("pt", l, i)[:, 0:P * nk], ACT.Copy).then_inc(*drain("pt", l, i))

            def attended(i):
                kind, h, q, nk = units[i]
                qs = slice(P * q, P * q + P)
                act.wait_ge(*full("av", l, i))
                if kind == "diff":
                    A(YB[:, h, qs], bank("av", l, i)[:, 0:P], ACT.Copy).then_inc(*drain("av", l, i))
                else:
                    r = slice(64 * (h % 2), 64 * (h % 2) + 64)
                    A(YC[r, h // 2, qs], bank("av", l, i)[r, 0:P], ACT.Copy).then_inc(*drain("av", l, i))

            exponentials(0)
            exponentials(1)
            for i in range(len(units)):
                if i >= 1:
                    attended(i - 1)
                evacuate(i)
                if i + 2 < len(units):
                    exponentials(i + 2)
            attended(len(units) - 1)
            nq = 4 if l == 0 else 2
            for h in range(4):
                act.wait_ge(*drained("av", l, nq * h + nq - 1))
                squares(("bn", l, h), lambda k: YB[:, h, o], 1, o)
                root(("bn", l, h), o)

            for b in range(15):
                lo = l == 1 and (b < 4 or b == 14)
                tk = LAT if lo else slice(0, T)
                act.wait_ge(*full("za", l, b))
                if b == 0:
                    act.wait_ge(*when("mu0", l))
                A(ZS[:, b, tk], bank("za", l, b)[:, 0:tk.stop - tk.start], ACT.Copy, scale=mu0[:, b:b + 1]).then_inc(*mark("zs_own", l, b))
            act.wait_ge(*drained("za", l, 12))
            A(ZS[:, 12, :], ZS[:, 12, :], ACT.Tanh).then_inc(*mark("tanh", l))
            act.wait_ge(*drained("za", l, 14))
            A(ZS[:, 14, o], ZS[:, 14, o], ACT.Sigmoid).then_inc(*mark("gd", l))
            for p in range(4):
                act.wait_ge(*when("kkraw", l, p))
                squares(("kkn", l, p), lambda k: KK[:, p, :], 1, slice(0, T))
                act.wait_ge(*full("kkn", l, p))
                if p:
                    act.wait_ge(*when("kk", l, p - 1))
                A(RS, bank("kkn", l, p)[:, :], ACT.Sqrt).then_inc(*drain("kkn", l, p))
            for c in range(NCH):
                act.wait_ge(*full("vtok", l, c))
                if c >= 4:
                    act.wait_ge(*when(f"v_spilled{c % 4}", l, c - 4))
                A(VT[0:C, c % 4, :], bank("vtok", l, c)[0:C, :], ACT.Copy).then_inc(*drain("vtok", l, c))

            def gates(i):
                d, p = i // 4, i % 4
                act.wait_ge(*full("lora_w", l, i))
                if i:
                    act.wait_ge(*when("decayed", l, i - 1))
                    act.wait_ge(*when("b", l, i - 1))
                A(SG, bank("lora_w", l, i)[:, :], ACT.Sigmoid, bias=par[:, l, W0 + i:W0 + i + 1]).then_inc(*drain("lora_w", l, i))
                act.wait_ge(*full("lora_a", l, i))
                A(AI, bank("lora_a", l, i)[:, :], ACT.Sigmoid, bias=par[:, l, A0C + i:A0C + i + 1]).then_inc(*drain("lora_a", l, i))
                act.wait_ge(*drained("lora_w", l, i))
                if i == 0:
                    act.wait_ge(*when("w65_zero", l))
                else:
                    act.wait_ge(*when("bk", l, i - 1))
                wv = W65.rearrange("p (h c t) -> p h c t", h=2, t=C + 1)
                for h in range(2):
                    ins = A(wv[:, h, :, 1:C + 1], directed(SG, d)[:, h], ACT.Exp, scale=-DECAY)
                ins.then_inc(*mark("decayed", l, i))

            def turned(i):
                for g in range(2):
                    act.wait_ge(*full("bkt", l, i, g))
                    if g == 0 and i >= 2:
                        act.wait_ge(*when(f"b_spilled{i % 2}", l, i - 2))
                    A(BKT[:, i % 2, 4 * g:4 * g + 4, :], bank("bkt", l, i, g)[:, :].rearrange("p (c n) -> p c n", c=4), ACT.Copy).then_inc(*drain("bkt", l, i, g))

            def gate12(d):
                for g in range(2):
                    act.wait_ge(*full("g12", l, d, g))
                    if d:
                        act.wait_ge(*when("m12", l, d - 1))
                    A(GS[:, g, 0:no], bank("g12", l, d, g)[:, 0:no], ACT.Sigmoid).then_inc(*drain("g12", l, d, g))

            def spills(i):
                act.wait_ge(*when("ar", l, i))
                act.dma_start(r_dram[:, :, i, :].rearrange("c p n -> p c n"), AR[:, i % 2]).then_inc(*dma(f"r_spilled{i % 2}", l, i))
                for g in range(2):
                    act.wait_ge(*drained("bkt", l, i, g))
                act.dma_start(b_dram[:, :, i, :].rearrange("c p n -> p c n"), BKT[:, i % 2]).then_inc(*dma(f"b_spilled{i % 2}", l, i))
                for g in range(4):
                    hh, half = g % 2, g // 2
                    act.wait_ge(*drained("A", l, i, g))
                    act.dma_start(a_dram[4 * half:4 * half + 4, :, 2 * i + hh, :].rearrange("c p n -> p c n"),
                                  AS[:, g]).then_inc(*dma(f"a_spilled{g}", l, i))

            gates(0)
            gates(1)
            for i in range(8):
                if i < 4:
                    gate12(i)
                if i + 2 < 8:
                    gates(i + 2)
                turned(i)
                spills(i)
            for d in range(4, 8):
                gate12(d)
            modulation(l, 1)
            modulation(l, 2)
            modulation_back(l, 1)
            if l + 1 < DEPTH:
                modulation(l + 1, 0)
            modulation_back(l, 2)
            if l + 1 < DEPTH:
                modulation_back(l + 1, 0)
            if l == DEPTH - 1:
                for d in range(8):
                    act.wait_ge(*full("g0", l, d))
                    if d == 0:
                        act.wait_ge(*when("x_spilled", l))
                    A(M[:, d, 0:no], bank("g0", l, d)[:, 0:no], ACT.Sigmoid).then_inc(*drain("g0", l, d))

            for c in range(NCH):
                for g in range(2):
                    act.wait_ge(*full("U", l, c, g))
                    if c:
                        act.wait_ge(*full("SA", l, c - 1, g))
                    A(R[0:C, 4 * g:4 * g + 4, :], bank("U", l, c, g)[0:C, :].rearrange("p (i n) -> p i n", i=4), ACT.Copy).then_inc(*drain("U", l, c, g))
                if not (l and c < 4):
                    for g in range(2):
                        act.wait_ge(*full("Y", l, c, g))
                        rc = c if g == 0 else 4 * (c // 4) + 3 - c % 4
                        dst = Y[:, g, :, C * rc:C * rc + C]
                        if g:
                            dst = dst[:, :, ::-1]
                        A(dst, bank("Y", l, c, g)[:, 0:4 * C].rearrange("p (i t) -> p i t", i=4), ACT.Copy).then_inc(*drain("Y", l, c, g))

            for p in range(4):
                act.wait_ge(*drained("gmean", l, p))
                A(RO[0][:, p, o], Y[:, 0, p, o], ACT.Square).then_inc(*mark("ysq", l, p))
            for p in range(4):
                act.wait_ge(*drained("gvar", l, p))
                A(RO[1][:, p, o], RO[1][:, p, o], ACT.Sqrt).then_inc(*mark("groot", l, p))
            if l < DEPTH - 1:
                for d in range(8):
                    act.wait_ge(*full("g0", l, d))
                    if d >= 2:
                        act.wait_ge(*when("merged", l, d - 2))
                    if d == 0:
                        act.wait_ge(*when("m12", l, 7))
                    A(GATE[:, d % 2, 0:no], bank("g0", l, d)[:, 0:no], ACT.Sigmoid).then_inc(*drain("g0", l, d))
            act.wait_ge(*when("merged", l, 7))
            m0 = split_at[(l, ("FG", 0), 0)]
            for m in range(m0, m0 + NHI):
                weights_rounded(m)
            for k in range(KT):
                act.wait_ge(*drained("wo", l, k))
            squares(("n2", l), lambda k: X2[:, k, o], KT, o, SQH)
            root(("n2", l), o)
            for k in range(KT):
                for s in sides(l):
                    tk = slice(HALF * s, HALF * s + HALF)
                    act.wait_ge(*when("h2_scaled", l, k, s))
                    A(h2_hi[:, k, tk], h2_raw[:, k, tk], ACT.Identity, bias=mods[:, 24 + k, s:s + 1]).then_inc(*mark("h2_hi", l, k, s))
            for f in range(FT):
                act.wait_ge(*full("fg", l, f))
                A(f_raw[:, f, o], bank("fg", l, f)[:, 0:no], ACT.Sigmoid).then_inc(*mark("fsg", l, f))
                if f:
                    act.wait_ge(*drained("fu", l, f - 1))
                    A(f_hi(f - 1, o), f_raw[:, f - 1, o], ACT.Copy).then_inc(*mark("f_hi", l, f - 1))
                weights_rounded(m0 + 2 * f + NHI)
                weights_rounded(m0 + 2 * f + 1 + NHI)
            act.wait_ge(*drained("fu", l, FT - 1))
            A(f_hi(FT - 1, o), f_raw[:, FT - 1, o], ACT.Copy).then_inc(*mark("f_hi", l, FT - 1))
            for m in range(m0 + 2 * FT + NHI, m0 + 2 * FT + 24):
                weights_rounded(m)
        for k in range(KT):
            act.wait_ge(*drained("fd", DEPTH - 1, k))
        squares(("nf",), lambda k: X[:, k, LAT], KT, LAT, SQH)
        root(("nf",), LAT)
        for i in range(2):
            for h in range(2):
                act.wait_ge(*full("xout", i, h))
                if i:
                    act.wait_ge(*when("stored", i - 1))
                A(TOK[:, 512 * h:512 * h + 512], bank("xout", i, h)[:, :], ACT.Copy).then_inc(*drain("xout", i, h))

    @block.vector
    def _(dve):
        V = nc.vector

        def step(ins):
            ins.then_inc(*mark("dve_step", plan.count.get("dve_step", 0)))
            dve.wait_ge(sem_of("dve_step"), plan.count["dve_step"])

        def weights_rest(m):
            raw, hi, n = half_views(m, ring)
            lo, _, _ = half_views(m, w_lo)
            dve.wait_ge(*when("w_hi", m))
            V.tensor_tensor(lo, raw, hi.bitcast(F32), ALU.subtract).then_inc(*mark("w_lo", m))

        def mean_square(key, n, toks):
            dve.wait_ge(*full(*key))
            ps = bank(*key)
            V.tensor_scalar(RS[:, toks], ps[:, 0:toks.stop - toks.start], 1.0 / n, EPS, ALU.mult, ALU.add).then_inc(*drain(*key))
            dve.wait_ge(*when("root", *key))
            step(V.reciprocal(RS[:, toks], RS[:, toks]))

        def modulation_columns(l, part):
            mods = mods_all[:, l]
            js = slice(16 * part, 16 * part + 16)
            dve.wait_ge(*full("modt", l, part))
            V.tensor_tensor(mods[:, js, :], bank("modt", l, part)[:, 0:32].rearrange("p (s j) -> p j s", s=2),
                            par2[:, l, ADAB + 16 * part:ADAB + 16 * part + 16].unsqueeze(2).broadcast_to([P, 16, 2]), ALU.add).then_inc(*drain("modt", l, part))
            if part != 1:
                n, sc, g = (0, 8, N1) if part == 0 else (1, 32, N2)
                dve.wait_ge(*drained("modt", l, part))
                step(V.scalar_tensor_tensor(gsc_all[:, l, n], mods[:, sc:sc + 8, :], 1.0,
                                            par[:, l, g:g + 8].unsqueeze(2).broadcast_to([P, 8, 2]), ALU.add, ALU.mult))

        dve.wait_ge(*when("csig", 1))
        V.tensor_tensor(csil[:, :, 0], csil[:, :, 0], par2[:, 0, CCTX:CCTX + 8], ALU.mult)
        V.tensor_tensor(csil[:, :, 1], csil[:, :, 1], par2[:, 0, CVEC:CVEC + 8], ALU.mult).then_inc(*mark("csil"))
        for l in range(DEPTH):
            lam, lamv = lam_all[:, l], lamv_all[:, l]
            dve.wait_ge(*when(f"lamv_{l}"))
            for j in range(2):
                step(V.tensor_tensor(lamv[:, 128 * j:128 * j + 64], lamv[:, 128 * j:128 * j + 64], lamv[:, 128 * j + 64:128 * j + 128], ALU.mult))
                ins = V.reduce_sum(lam[:, j:j + 1], lamv[:, 128 * j:128 * j + 64], AX.X)
            ins.then_inc(*mark("lam_dots", l))
        for l in range(DEPTH):
            dve.wait_ge(*drained("par", l))
        modulation_columns(0, 0)

        for l in range(DEPTH):
            o = outs(l)
            no = o.stop - o.start
            lam_init = 0.8 - 0.6 * math.exp(-0.3 * l)
            pcol, mods, gsc, lam = par[:, l], mods_all[:, l], gsc_all[:, l], lam_all[:, l]
            dve.wait_ge(*when("lam_exp", l))
            step(V.tensor_tensor(lam[:, 2:3], lam[:, 0:1], lam[:, 1:2], ALU.subtract))
            step(V.tensor_scalar(lam[:, 2:3], lam[:, 2:3], lam_init, None, ALU.add))
            V.tensor_scalar(subg[:, :], pcol[:, SUBG:SUBG + 1], 1.0 - lam_init, None, ALU.mult)
            step(V.tensor_tensor(mu0[:, :], pcol[:, MU:MU + 15], pcol[:, MU + 15:MU + 30], ALU.add))
            V.tensor_scalar(mu0[:, :], mu0[:, :], -1.0, 1.0, ALU.mult, ALU.add).then_inc(*mark("mu0", l))
            step(V.tensor_scalar(kaneg[:, :], pcol[:, KAC:KAC + 4], -1.0, 1.0, ALU.mult, ALU.add))
            mean_square(("n1", l), D, slice(0, T))
            for k in range(KT):
                for s in (0, 1):
                    tk = slice(HALF * s, HALF * s + HALF)
                    V.scalar_tensor_tensor(H[:, k, tk], X[:, k, tk], gsc[:, 0, k, s:s + 1], RS[:, tk], ALU.mult, ALU.mult).then_inc(*mark("h1_scaled", l, k, s))

            def rope(raw, x, cosc, sinc, rows, name, key, n):
                dve.wait_ge(*full(*raw))
                r = ROT[rows, n % 2, :]
                V.tensor_tensor(r, bank(*raw)[rows, 0:HALF], cst[rows, sinc:sinc + HALF], ALU.mult).then_inc(*drain(*raw))
                step(V.tensor_tensor(x, x, cst[rows, cosc:cosc + HALF], ALU.mult))
                dve.wait_ge(*drained(*raw))
                V.tensor_tensor(x, x, r, ALU.add).then_inc(*mark(name, *key))

            allp = slice(0, P)
            q32 = slice(64, 96)
            for b in range(8):
                rope(("qkrot", l, b), QK[:, b, LAT], COSB, SINB, allp, "qk_ready", (l, b), b)
            mean_square(("qn", l), 384, o)
            for k in range(3):
                V.scalar_tensor_tensor(ZC[:, k, o], ZC[:, k, o], pcol[:, QNG + k:QNG + k + 1], RS[:, o], ALU.mult, ALU.mult).then_inc(*mark("qnorm", l, k))
            dve.wait_ge(*when("qnorm", l, 2))
            mean_square(("kvn", l), 256, slice(0, T))
            for k in range(2):
                V.scalar_tensor_tensor(ZC[:, 3 + k, :], ZC[:, 3 + k, :], pcol[:, KVG + k:KVG + k + 1], RS, ALU.mult, ALU.mult).then_inc(*mark("kvnorm", l, k))
            dve.wait_ge(*when("kvnorm", l, 1))
            rope(("krot", l), ZC[q32, 5, LAT], COSC, SINC, q32, "krope", (l,), 0)
            dve.wait_ge(*when("krope", l))
            V.tensor_copy(MK[q32, :, :], ZC[q32, 5:6, :].broadcast_to([32, 8, T])).then_inc(*mark("mk_rope", l))
            for h in range(8):
                rope(("mqrot", l, h), MQ[q32, h, LAT], COSC, SINC, q32, "mq_ready", (l, h), h)

            units = attention_units(l)

            def maxima(i):
                kind, h, q, nk = units[i]
                scale = DIFF_SCALE if kind == "diff" else MLA_SCALE
                for c in range(2 if kind == "diff" else 1):
                    dve.wait_ge(*full("sc", l, i, c))
                    if l and i == 0 and c == 0:
                        pass
                    step(V.reduce_max(smax[:, c, i:i + 1], bank("sc", l, i, c)[:, 0:P * nk], AX.X))
                    V.tensor_scalar(smax[:, c, i:i + 1], smax[:, c, i:i + 1], -scale, None, ALU.mult).then_inc(*mark("negmax", l, i, c))

            def normalised(i):
                kind, h, q, nk = units[i]
                n = P * nk
                nc_ = 2 if kind == "diff" else 1
                for c in range(nc_):
                    dve.wait_ge(*drained("sc", l, i, c))
                step(V.reciprocal(rsum[:, 0:nc_, i:i + 1], ssum[:, 0:nc_, i:i + 1]))
                if kind == "diff":
                    step(V.tensor_scalar(PR[:, i % 3, 1, 0:n], PR[:, i % 3, 1, 0:n], rsum[:, 1, i:i + 1], lam[:, 2:3], ALU.mult, ALU.mult))
                    V.scalar_tensor_tensor(PR[:, i % 3, 0, 0:n], PR[:, i % 3, 0, 0:n], rsum[:, 0, i:i + 1], PR[:, i % 3, 1, 0:n],
                                           ALU.mult, ALU.subtract).then_inc(*mark("probs", l, i))
                else:
                    V.tensor_scalar(PR[:, i % 3, 0, 0:n], PR[:, i % 3, 0, 0:n], rsum[:, 0, i:i + 1], None, ALU.mult).then_inc(*mark("probs", l, i))

            maxima(0)
            maxima(1)
            for i in range(len(units)):
                normalised(i)
                if i + 2 < len(units):
                    maxima(i + 2)
            for h in range(4):
                mean_square(("bn", l, h), P, o)
                V.scalar_tensor_tensor(YB[:, h, o], YB[:, h, o], subg[:, 0:1], RS[:, o], ALU.mult, ALU.mult).then_inc(*mark("yb", l, h))
                dve.wait_ge(*when("yb", l, h))

            for b in range(15):
                lo = l == 1 and (b < 4 or b == 14)
                ps = bank("za", l, b)
                dve.wait_ge(*when("zs_own", l, b))
                if lo:
                    z, s = ps[:, 0:HALF].unsqueeze(1), ZS[:, b, LAT].unsqueeze(1)
                else:
                    z, s = ps[:, :].rearrange("p (h t) -> p h t", h=2), ZS[:, b, :].rearrange("p (h t) -> p h t", h=2)
                step(V.scalar_tensor_tensor(s[:, :, 1:HALF], z[:, :, 0:HALF - 1], pcol[:, MU + b:MU + b + 1], s[:, :, 1:HALF], ALU.mult, ALU.add))
                V.scalar_tensor_tensor(s[:, :, 0:HALF - 1], z[:, :, 1:HALF], pcol[:, MU + 15 + b:MU + 16 + b], s[:, :, 0:HALF - 1],
                                       ALU.mult, ALU.add).then_inc(*drain("za", l, b))
            for p in range(4):
                dve.wait_ge(*drained("za", l, 4 + p))
                V.tensor_scalar(KK[:, p, :], ZS[:, 4 + p, :], pcol[:, KKC + p:KKC + p + 1], None, ALU.mult).then_inc(*mark("kkraw", l, p))
            for p in range(4):
                dve.wait_ge(*drained("kkn", l, p))
                step(V.tensor_scalar(RS, RS, 1e-12, None, ALU.max))
                step(V.reciprocal(RS, RS))
                V.tensor_tensor(KK[:, p, :], KK[:, p, :], RS, ALU.mult).then_inc(*mark("kk", l, p))
            dve.wait_ge(*when("kk", l, 3))
            w65v = W65.rearrange("p (c t) -> p c t", t=C + 1)
            V.memset(w65v[:, :, 0:1], 0.0).then_inc(*mark("w65_zero", l))

            def scaled(i):
                d, p = i // 4, i % 4
                k, r, kk = ZS[:, 4 + p, :], ZS[:, p, :], KK[:, p, :]
                ar = AR[:, i % 2]
                e = E65.rearrange("p (c t) -> p c t", t=C + 1)
                dve.wait_ge(*drained("lora_a", l, i))
                if i:
                    dve.wait_ge(*when("bk", l, i - 1))
                step(V.tensor_scalar(TA, AI, pcol[:, KAC + p:KAC + p + 1], kaneg[:, p:p + 1], ALU.mult, ALU.add))
                step(V.tensor_tensor(TA, TA, k, ALU.mult))
                V.tensor_tensor(TB, kk, AI, ALU.mult).then_inc(*mark("b", l, i))
                if d == 0:
                    V.scalar_tensor_tensor(BV[:, p, o], TA[:, o], pcol[:, RKC + p:RKC + p + 1], r[:, o], ALU.mult, ALU.mult)
                else:
                    step(V.scalar_tensor_tensor(GT[:, o], TA[:, o], pcol[:, RKC + p:RKC + p + 1], r[:, o], ALU.mult, ALU.mult))
                    V.tensor_tensor(BV[:, p, o], BV[:, p, o], GT[:, o], ALU.add).then_inc(*mark("rkk", l, p))
                dve.wait_ge(*when("decayed", l, i))
                step(V.tensor_tensor_scan(E65, W65, cst[:, STARTS:STARTS + NCH * (C + 1)], 0.0, ALU.mult, ALU.add))
                if i >= 2:
                    dve.wait_ge(*when(f"r_spilled{i % 2}", l, i - 2))
                step(V.reciprocal(RI.rearrange("p (c t) -> p c t", t=C), e[:, :, 1:C + 1]))
                V.tensor_copy(dend[:, i, :], e[:, :, C])
                r3 = RI.rearrange("p (c t) -> p c t", t=C)
                for h in range(2):
                    cs = slice(4 * h, 4 * h + 4)
                    V.scalar_tensor_tensor(ar[:, cs, 0:C], directed(kk, d)[:, h], -1.0, e[:, cs, 0:C], ALU.mult, ALU.mult)
                    if l and h == 0:
                        ins = V.memset(ar[:, cs, C:P], 0.0)
                    else:
                        ins = V.tensor_tensor(ar[:, cs, C:P], directed(r, d)[:, h], e[:, cs, 1:C + 1], ALU.mult)
                ins.then_inc(*mark("ar", l, i))
                if i:
                    dve.wait_ge(*full("A", l, i - 1, 3))
                    dve.wait_ge(*when("bh", l, i - 1))
                else:
                    for c in range(4, NCH):
                        dve.wait_ge(*when(f"v_spilled{c % 4}", l, c))
                for h in range(2):
                    cs = slice(4 * h, 4 * h + 4)
                    V.tensor_tensor(BK[:, cs, 0:C], directed(TB, d)[:, h], r3[:, cs, :], ALU.mult)
                    ins = V.tensor_tensor(BK[:, cs, C:P], directed(TA, d)[:, h], r3[:, cs, :], ALU.mult)
                ins.then_inc(*mark("bk", l, i))

            def masked(i):
                for g in range(4):
                    dve.wait_ge(*full("A", l, i, g))
                    if i:
                        dve.wait_ge(*when(f"a_spilled{g}", l, i - 1))
                    V.tensor_tensor(AS[:, g], bank("A", l, i, g)[:, :].rearrange("p (c n) -> p c n", c=4),
                                    cst[:, MASK:MASK + P].unsqueeze(1).broadcast_to([P, 4, P]), ALU.mult).then_inc(*drain("A", l, i, g))

            def merged12(d):
                for g in range(2):
                    dve.wait_ge(*full("w12", l, d, g))
                    dve.wait_ge(*drained("g12", l, d, g))
                    V.tensor_tensor(GS[:, g, 0:no], bank("w12", l, d, g)[:, 0:no], GS[:, g, 0:no], ALU.mult).then_inc(*drain("w12", l, d, g))
                for g in range(2):
                    dve.wait_ge(*drained("w12", l, d, g))
                if d == 0:
                    dve.wait_ge(*when("x_spilled", l))
                V.tensor_tensor(M[:, d, o], GS[:, 0, 0:no], GS[:, 1, 0:no], ALU.add).then_inc(*mark("m12", l, d))

            scaled(0)
            for i in range(8):
                if i + 1 < 8:
                    scaled(i + 1)
                if i < 4:
                    merged12(i)
                masked(i)
            for p in range(4):
                dve.wait_ge(*full("bonus", l, p))
                V.tensor_tensor(BV[:, p, o], bank("bonus", l, p)[:, 0:no], ZS[:, 8 + p, o], ALU.mult).then_inc(*drain("bonus", l, p))

            dve.wait_ge(*when("nb_in", l))
            for i in (6, 7):
                dve.wait_ge(*when(f"r_spilled{i % 2}", l, i))
            for s in range(1, CSPLIT - 1):
                n = CSPLIT - 1 - s
                tmp = NT[:, 0:s * n].rearrange("p (j t) -> p j t", t=n)
                step(V.tensor_tensor(tmp, NB[:, 0:s, s:s + 1].broadcast_to([P, s, n]), NB[:, s:s + 1, s + 1:CSPLIT].broadcast_to([P, s, n]), ALU.mult))
                V.tensor_tensor(NB[:, 0:s, s + 1:CSPLIT], NB[:, 0:s, s + 1:CSPLIT], tmp, ALU.add).then_inc(*mark("inverse_col", l, s + 1))
                dve.wait_ge(*when("inverse_col", l, s + 1))
                if s % 8 == 7 and s // 8 < 4:
                    merged12(4 + s // 8)
            dve.wait_ge(*when("inverse_right", l, C - 2))
            V.memset(NB.rearrange("p s t -> p (s t)")[:, 0:C * C:C + 1], 1.0).then_inc(*mark("inverted", l))
            V.memset(S, 0.0).then_inc(*mark("state_zero", l))
            dve.wait_ge(*when("state_zero", l))
            for c in range(NCH):
                b = c % 2
                for g in range(2):
                    dve.wait_ge(*full("SA", l, c, g))
                    dve.wait_ge(*when(f"chunk_in{b}", l, c))
                    V.tensor_copy(cV[0:C, b, g, :], bank("SA", l, c, g)[0:C, :]).then_inc(*drain("SA", l, c, g))
                for g in range(2):
                    if c:
                        dve.wait_ge(*drained("S", l, c - 1, g))
                    dve.wait_ge(*full("S", l, c, g))
                    ps = bank("S", l, c, g)
                    for ii in range(4):
                        i = 4 * g + ii
                        for hh in range(2):
                            r = slice(C * hh, C * hh + C)
                            ins = V.scalar_tensor_tensor(S[r, i, r], S[r, i, r], dend[r, i, c:c + 1],
                                                         ps[r, P * ii + C * hh:P * ii + C * hh + C], ALU.mult, ALU.add)
                    ins.then_inc(*drain("S", l, c, g))

            modulation_columns(l, 1)
            modulation_columns(l, 2)
            if l + 1 < DEPTH:
                modulation_columns(l + 1, 0)
            for p in range(4):
                if p == 0:
                    for g in range(2):
                        dve.wait_ge(*drained("Y", l, NCH - 1, g))
                V.tensor_tensor(Y[:, 0, p, o], Y[:, 0, p, o], Y[:, 1, p, o], ALU.add).then_inc(*mark("ysum", l, p))
            for p in range(4):
                dve.wait_ge(*full("gmean", l, p))
                V.scalar_tensor_tensor(Y[:, 0, p, o], bank("gmean", l, p)[:, 0:no], -1.0 / 64, Y[:, 0, p, o], ALU.mult, ALU.add).then_inc(*drain("gmean", l, p))
            for p in range(4):
                dve.wait_ge(*full("gvar", l, p))
                V.tensor_scalar(RO[1][:, p, o], bank("gvar", l, p)[:, 0:no], 1.0 / 64, GN_EPS, ALU.mult, ALU.add).then_inc(*drain("gvar", l, p))
            for p in range(4):
                dve.wait_ge(*when("groot", l, p))
                step(V.reciprocal(RO[1][:, p, o], RO[1][:, p, o]))
                step(V.scalar_tensor_tensor(Y[:, 0, p, o], Y[:, 0, p, o], pcol[:, LNW + p:LNW + p + 1], RO[1][:, p, o], ALU.mult, ALU.mult))
                step(V.scalar_tensor_tensor(Y[:, 0, p, o], Y[:, 0, p, o], pcol[:, LNB + p:LNB + p + 1], BV[:, p, o], ALU.add, ALU.add))
                dve.wait_ge(*full("lora_g", l, p))
                V.tensor_tensor(YA[:, p, o], bank("lora_g", l, p)[:, 0:no], Y[:, 0, p, o], ALU.mult).then_inc(*drain("lora_g", l, p))
            for d in range(8):
                dve.wait_ge(*full("w0", l, d))
                dve.wait_ge(*drained("g0", l, d))
                gate = GATE[:, d % 2, 0:no] if l < DEPTH - 1 else M[:, d, 0:no]
                V.tensor_tensor(gate, bank("w0", l, d)[:, 0:no], gate, ALU.mult).then_inc(*drain("w0", l, d))
                dve.wait_ge(*drained("w0", l, d))
                V.tensor_tensor(M[:, d, o], M[:, d, o], gate, ALU.add).then_inc(*mark("merged", l, d))
            dve.wait_ge(*when("x_back", l))
            for k in range(KT):
                dve.wait_ge(*full("wo", l, k))
                for s in sides(l):
                    tk = slice(HALF * s, HALF * s + HALF)
                    ins = V.scalar_tensor_tensor(X2[:, k, tk], bank("wo", l, k)[:, tk.start - o.start:tk.stop - o.start],
                                                 mods[:, 16 + k, s:s + 1], X2[:, k, tk], ALU.mult, ALU.add)
                ins.then_inc(*drain("wo", l, k))
            m0 = split_at[(l, ("FG", 0), 0)]
            for m in range(m0, m0 + NHI):
                weights_rest(m)
            mean_square(("n2", l), D, o)

            def h2_rest(k):
                for s in sides(l):
                    tk = slice(HALF * s, HALF * s + HALF)
                    dve.wait_ge(*when("h2_hi", l, k, s))
                    V.scalar_tensor_tensor(h2_lo[:, k, tk], h2_raw[:, k, tk], mods[:, 24 + k, s:s + 1],
                                           h2_hi[:, k, tk].bitcast(F32), ALU.add, ALU.subtract).then_inc(*mark("h2", l, k))

            for k in range(KT):
                for s in sides(l):
                    tk = slice(HALF * s, HALF * s + HALF)
                    V.scalar_tensor_tensor(h2_raw[:, k, tk], X2[:, k, tk], gsc[:, 1, k, s:s + 1], RS[:, tk], ALU.mult, ALU.mult).then_inc(*mark("h2_scaled", l, k, s))
                if k:
                    h2_rest(k - 1)
            h2_rest(KT - 1)

            def hidden_rest(f):
                dve.wait_ge(*when("f_hi", l, f))
                V.tensor_tensor(f_lo[:, f, o], f_raw[:, f, o], f_hi(f, o).bitcast(F32), ALU.subtract).then_inc(*mark("ffn_hidden", l, f))

            for f in range(FT):
                dve.wait_ge(*when("fsg", l, f))
                V.tensor_tensor(f_raw[:, f, o], bank("fg", l, f)[:, 0:no], f_raw[:, f, o], ALU.mult).then_inc(*drain("fg", l, f))
                weights_rest(m0 + 2 * f + NHI)
                if f:
                    hidden_rest(f - 1)
                dve.wait_ge(*drained("fg", l, f))
                dve.wait_ge(*full("fu", l, f))
                V.tensor_tensor(f_raw[:, f, o], bank("fu", l, f)[:, 0:no], f_raw[:, f, o], ALU.mult).then_inc(*drain("fu", l, f))
                weights_rest(m0 + 2 * f + 1 + NHI)
            hidden_rest(FT - 1)
            for k in range(KT):
                if k % 2 == 0:
                    m1 = m0 + 2 * FT + NHI + 3 * k
                    for m in range(m1, min(m1 + 6, m0 + 2 * FT + 24)):
                        weights_rest(m)
                dve.wait_ge(*full("fd", l, k))
                for s in sides(l):
                    tk = slice(HALF * s, HALF * s + HALF)
                    ins = V.scalar_tensor_tensor(X[:, k, tk], bank("fd", l, k)[:, tk.start - o.start:tk.stop - o.start],
                                                 mods[:, 40 + k, s:s + 1], X2[:, k, tk], ALU.mult, ALU.add)
                ins.then_inc(*drain("fd", l, k))
        mean_square(("nf",), D, LAT)
        for k in range(KT):
            V.scalar_tensor_tensor(H[:, k, LAT], X[:, k, LAT], par2[:, DEPTH - 1, FING + k:FING + k + 1], RS[:, LAT], ALU.mult, ALU.mult).then_inc(*mark("final", k))


_NAMES = ['x', 'c', 'ctx', 'c_ctx', 'ada_w', 'ada_b', 'norm1_g', 'norm2_g', 'w_in', 'rwkv_shift_mu', 'rwkv_w0',
          'rwkv_w2', 'rwkv_a0', 'rwkv_a2', 'rwkv_g2', 'rwkv_k_k', 'rwkv_k_a', 'rwkv_r_k', 'rwkv_ln_w', 'rwkv_ln_b',
          'diff_lambda', 'diff_subln_g', 'mla_q_norm_g', 'mla_kv_norm_g', 'mla_w_uq', 'mla_w_uk', 'mla_w_uv',
          'w_branch', 'w_out', 'ffn_w_gate', 'ffn_w_up', 'ffn_w_down', 'final_norm_g']


def program(new_bass, shapes):
    plan = None
    for _ in range(2):
        nc = new_bass()
        plan = Plan(plan)
        w = {n: nc.dram_tensor(f"in_{n}", s, F32, kind="ExternalInput").ap() for n, s in shapes.items()}
        tab = nc.dram_tensor("in_tables", (P, NTAB), F32, kind="ExternalInput").ap()
        out = nc.dram_tensor("out_0", (1, HALF, D), F32, kind="ExternalOutput").ap()
        with ExitStack() as ctx:
            build(nc, w, tab, out, plan, ctx)
    return nc


def kernel(**inputs):
    import concourse.bacc as bacc
    from concourse.bass_utils import run_bass_kernel_spmd

    arrays = {f"in_{n}": np.ascontiguousarray(inputs[n]) for n in _NAMES}
    nc = program(lambda: bacc.Bacc("TRN2", target_bir_lowering=False, num_devices=1),
                 {n: tuple(inputs[n].shape) for n in _NAMES})
    arrays["in_tables"] = tables()
    return run_bass_kernel_spmd(nc, [arrays], core_ids=[0]).results[0]["out_0"]
```

```python
import math
from contextlib import ExitStack

import numpy as np
import concourse.bass as bass
from concourse import mybir

F32 = mybir.dt.float32
F32R = mybir.dt.float32r
ALU = mybir.AluOpType
ACT = mybir.ActivationFunctionType
AX = mybir.AxisListType

P = 128
DEPTH, D, KT = 2, 1024, 8
T, HALF = 512, 256
C = 64
NCH = T // C
RW, RT = 512, 4
W_COLS = 7200
A0, B0, C0, G0 = 0, 1920, 1920 + 1536, 1920 + 1536 + 672
DFF, FT = 2816, 22
EPS = 1e-6
GN_EPS = 64e-5
DECAY = math.exp(-0.5)
NBANK = 8
BN_AT, KK_AT = (0, 2, 4, 6), (8, 9, 10, 11)
CSPLIT, LATE = 56, 50
NW, WSLOT = 4, 2048
LAT = slice(HALF, T)
DIFF_SCALE = 64 ** -0.5
MLA_SCALE = 96 ** -0.5

IDENT, MASK, ONES, BONES, PERM, PERM32, COSB, SINB, COSC, SINC, INSIDE = (
    0, 128, 256, 384, 512, 640, 768, 1024, 1280, 1536, 1792)
NTAB = INSIDE + NCH * (C + 1)
MU, N1, N2, W0, A0C, KKC, KAC, RKC, LNW, LNB, SUBG, QNG, KVG, NPAR = (
    0, 30, 38, 46, 54, 62, 66, 70, 74, 78, 82, 83, 86, 88)
ADAB, FING, CVEC, CCTX, NPAR2 = 0, 48, 56, 64, 72


def tables():
    t = np.zeros((P, NTAB), np.float32)
    i = np.arange(P)
    t[:, IDENT:IDENT + P] = np.eye(P)
    s, q = i[:, None] % 64, i[None, :]
    t[:, MASK:MASK + P] = np.where(q < 64, s < q, s <= q - 64)
    t[:, ONES:ONES + P] = 1
    t[:, BONES:BONES + P] = (i[:, None] // 64) == (i[None, :] // 64)
    for b in range(2):
        for j in range(32):
            t[64 * b + 32 + j, PERM + 64 * b + j] = -1
            t[64 * b + j, PERM + 64 * b + 32 + j] = 1
    for j in range(16):
        t[64 + 16 + j, PERM32 + j] = -1
        t[64 + j, PERM32 + 16 + j] = 1
    tok = np.arange(HALF)
    row, col = (tok // 64).astype(np.float32), (tok % 64).astype(np.float32)
    for rot, c0, s0 in ((64, COSB, SINB), (32, COSC, SINC)):
        n = rot // 4
        inv = (np.float32(10000.0) ** (-np.arange(n, dtype=np.float32) / np.float32(n))).astype(np.float32)
        ang = np.concatenate([row[:, None] * inv, col[:, None] * inv], -1).T
        cs, sn = np.cos(ang, dtype=np.float32), np.sin(ang, dtype=np.float32)
        if rot == 64:
            t[:, c0:c0 + HALF], t[:, s0:s0 + HALF] = np.tile(cs, (4, 1)), np.tile(sn, (4, 1))
        else:
            t[64:96, c0:c0 + HALF], t[64:96, s0:s0 + HALF] = np.tile(cs, (2, 1)), np.tile(sn, (2, 1))
    t[:, INSIDE:].reshape(P, NCH, C + 1)[:, :, 1:] = 1
    return t


class Plan:

    def __init__(self, known=None):
        self.known = known
        self.count, self.at, self.jobs, self.release, self.read = {}, {}, {}, {}, {}

    def start(self, sem_of):
        self.sem_of = sem_of

    def mark(self, name, *key, by=1):
        self.count[name] = self.count.get(name, 0) + by
        self.at[(name, *key)] = self.count[name]
        return self.sem_of(name), by

    def dma(self, name, *key):
        return self.mark(name, *key, by=16)

    def when(self, name, *key):
        return self.sem_of(name), (self.known.at[(name, *key)] if self.known else 1)

    def job(self, *key):
        n = len(self.jobs)
        self.jobs[key] = n
        return n

    def index(self, *key):
        return self.known.jobs[key] if self.known else 0

    def full(self, *key):
        n = self.index(*key)
        return self.sem_of(f"psum_full{n % NBANK}"), n // NBANK + 1

    def drained(self, *key):
        n = self.index(*key)
        return self.sem_of(f"psum_drained{n % NBANK}"), n // NBANK + 1

    def released(self, n):
        key = self.known.release[n] if self.known else ("x",)
        return self.when(*key[1:]) if key[0] == "mark" else self.full(*key)

    def half_read(self, m):
        key = self.known.read[m] if self.known else ("x",)
        return self.when(*key[1:]) if key[0] == "mark" else self.full(*key)

    def drain(self, *key):
        return self.sem_of(f"psum_drained{self.index(*key) % NBANK}"), 1


def weight_chunks(w, l):
    win = w["w_in"][l]

    def cols(m, a, n):
        return m[:, a:a + n].rearrange("(k p) n -> p k n", p=P)

    def ada(layer, part, halves=(0, 1)):
        for j in [8 * part + 4 * h + i for h in halves for i in range(4)]:
            yield ("ada", layer, j), 8, 256, [(0, 256, 0, 8, cols(w["ada_w"][layer], 256 * j, 256))]

    if l == 0:
        yield from ada(0, 0)
        yield from ada(0, 1, (0,))
    for j in range(6):
        yield ("B", j), 8, 256, [(0, 256, 0, 8, cols(win, B0 + 256 * j, 256))]
    for j in range(2):
        yield ("C", j), 8, 256, [(0, 256, 0, 8, cols(win, C0 + 256 * j, 256))]
    yield ("C", 2), 8, 224, [(0, P, 0, 8, cols(win, C0 + 512, P)), (P, P + 96, 0, 8, cols(win, C0 + 512 + 64, 96))]
    for j in range(2):
        yield ("uq", j), 3, 384, [(0, 384, 0, 3, cols(w["mla_w_uq"][l], 384 * j, 384))]
    yield ("uk",), 2, 512, [(0, 512, 0, 2, cols(w["mla_w_uk"][l], 0, 512))]
    yield ("uv",), 2, 512, [(0, 512, 0, 2, cols(w["mla_w_uv"][l], 0, 512))]
    for j in range(8):
        n = 256 if j < 7 else 128
        yield ("A", j), 8, n, [(0, n, 0, 8, cols(win, A0 + 256 * j, n))]
    wb = w["w_branch"][l].rearrange("g e n -> (g e) n")

    def attention_branches(d):
        yield ("G12", d), 8, 256, [(P * g, P * g + P, 0, 8, cols(win, G0 + D * (1 + g) + P * d, P))
                                   for g in range(2)]
        yield ("W12", d), 8, P, [(0, P, 0, 8, cols(wb[RW:3 * RW], P * d, P))]

    def rwkv_gate(d):
        yield ("G0", d), 8, P, [(0, P, 0, 8, cols(win, G0 + P * d, P))]

    def rwkv_branch(d):
        yield ("W0", d), 4, P, [(0, P, 0, 4, cols(wb[0:RW], P * d, P))]

    for d in range(4):
        yield from attention_branches(d)
    if l == DEPTH - 1:
        for d in range(8):
            yield from rwkv_gate(d)
    for d in range(4, 8):
        yield from attention_branches(d)
    yield from ada(l, 1, (0, 1) if l else (1,))
    yield from ada(l, 2)
    if l + 1 < DEPTH:
        yield from ada(l + 1, 0)
        for d in range(5):
            yield from rwkv_gate(d)
    for d in range(8):
        yield from rwkv_branch(d)
        if l < DEPTH - 1 and d + 5 < 8:
            yield from rwkv_gate(d + 5)
    for j in range(4):
        yield ("O", j), 8, 256, [(0, 256, 0, 8, cols(w["w_out"][l], 256 * j, 256))]
    for j in range(11):
        yield ("FG", j), 8, 256, [(0, 256, 0, 8, cols(w["ffn_w_gate"][l], 256 * j, 256))]
        yield ("FU", j), 8, 256, [(0, 256, 0, 8, cols(w["ffn_w_up"][l], 256 * j, 256))]
    for d in range(4):
        for kc, (k0, k1) in enumerate(((0, 8), (8, 16), (16, 22))):
            yield ("FD", d, kc), k1 - k0, 256, [
                (0, 256, 0, k1 - k0, cols(w["ffn_w_down"][l][P * k0:P * k1, :], 256 * d, 256))]


def split_halves(l):

    def left_right(name, slots):
        for half in range(2):
            yield name, half, (0, 8), (P * half, P * half + P), slots

    early, gates, late = ("early", 3), ("early", 2), ("late", 4)
    for j in range(4):
        yield from left_right(("B", j), early)
    for j in (4, 5):
        for half in range(2):
            yield ("B", j), half, (4 * half, 4 * half + 4), (0, 256), early
    yield from left_right(("C", 0), early)
    yield from left_right(("C", 1), early)
    yield ("C", 2), 0, (0, 8), (0, P), early
    yield ("C", 2), 1, (0, 8), (P, P + 96), early
    for j in range(7):
        yield from left_right(("A", j), early)
    yield ("A", 7), 0, (0, 8), (0, P), early
    for d in range(4):
        yield from left_right(("G12", d), gates)
    if l == DEPTH - 1:
        for d in range(8):
            yield ("G0", d), 0, (0, 8), (0, P), gates
    for d in range(4, 8):
        yield from left_right(("G12", d), gates)
    if l < DEPTH - 1:
        for d in range(8):
            yield ("G0", d), 0, (0, 8), (0, P), late
    for j in range(4):
        yield from left_right(("O", j), late)
    for j in range(11):
        for half in range(2):
            for name in ("FG", "FU"):
                yield (name, j), half, (0, 8), (P * half, P * half + P), late
    for d in range(4):
        for kc, nk in enumerate((8, 8, 6)):
            for half in range(2):
                yield ("FD", d, kc), half, (0, nk), (P * half, P * half + P), late


def attention_units(l):
    tiles = range(4) if l == 0 else range(2, 4)
    return ([("diff", h, q, 2 if q < 2 else 4) for h in range(4) for q in tiles]
            + [("mla", h, q, 2 if q < 2 else 4) for h in range(8) for q in tiles])


def build(nc, w, tab, out, plan, ctx):
    sems = {}

    def sem_of(name):
        if name not in sems:
            sems[name] = ctx.enter_context(nc.semaphore(name))
        return sems[name]

    plan.start(sem_of)
    mark, dma, when, full, drained, drain = plan.mark, plan.dma, plan.when, plan.full, plan.drained, plan.drain

    def sb(name, shape):
        return ctx.enter_context(nc.sbuf_tensor(name, shape, F32))

    def dram(name, shape):
        return nc.dram_tensor(name, shape, F32, kind="Internal").ap()

    PS = [ctx.enter_context(nc.psum_tensor(f"ps{b}", [P, 512], F32)) for b in range(NBANK)]

    def bank(*key):
        return PS[plan.index(*key) % NBANK]

    ARENA = 155 * 256
    arena = sb("arena", [P, ARENA])
    arena_at = nc.sbuf_base - 4 * ARENA
    ring = sb("ring", [P, NW, WSLOT])
    ring_at = nc.sbuf_base - 4 * NW * WSLOT
    cst = sb("cst", [P, NTAB])
    par = sb("par", [P, DEPTH, NPAR])
    par2 = sb("par2", [P, DEPTH, NPAR2])
    csil = sb("csil", [P, KT, 2])
    mods_all = sb("mods", [P, DEPTH, 48, 2])
    gsc_all = sb("gsc", [P, DEPTH, 2, KT, 2])
    mrow = sb("mrow", [32, 3, P])
    lora = sb("lora", [P, 3, RW])
    lam_all = sb("lam", [P, DEPTH, 8])
    subg = sb("subg", [P, 1])
    mu0 = sb("mu0", [P, 15])
    kaneg = sb("kaneg", [P, 4])
    smax = sb("smax", [P, 2, 64])
    ssum = sb("ssum", [P, 2, 64])
    rsum = sb("rsum", [P, 2, 64])
    dend = sb("dend", [P, 8, NCH])

    def view(kb, shape):
        o, n = int(kb * 256), int(np.prod(shape))
        assert o + n <= ARENA
        v = arena[:, o:o + n]
        names = "abcd"[:len(shape)]
        if len(shape) == 1:
            return v
        return v.rearrange("p (%s) -> p %s" % (" ".join(names), " ".join(names)),
                           **{n: s for n, s in zip(names, shape)})

    def rounded(name, kb, shape):
        return nc.alloc_sbuf_tensor_at(name, [P, *shape], F32R, offset=arena_at + int(1024 * kb))

    w_lo = nc.alloc_sbuf_tensor_at("w_lo", [P, NW, WSLOT], F32R, offset=ring_at)
    w_hi = {"early": rounded("w_hi_early", 124.25, [3, KT * P]), "late": rounded("w_hi_late", 136, [4, KT * P])}
    h_hi = rounded("h_hi", 0, [KT, T])
    h_lo = rounded("h_lo", 16, [KT, T])
    h_raw = view(16, [KT, T])
    m_hi, m_lo = rounded("m_hi", 118, [KT, T]), rounded("m_lo", 32, [KT, T])
    f_lo = rounded("f_lo", 72, [FT, T])
    f_raw = view(72, [FT, T])
    f_hi_a, f_hi_b = rounded("f_hi_a", 32, [12, T]), rounded("f_hi_b", 116, [FT - 12, T])

    def f_hi(k, toks):
        return f_hi_a[:, k, toks] if k < 12 else f_hi_b[:, k - 12, toks]

    H = view(0, [KT, T])
    X = view(16, [KT, T])
    M = view(32, [KT, T])
    YB = view(32, [4, T])
    YC = view(40, [4, T])
    QK = view(48, [8, T])
    VD = view(64, [4, T])
    ZC = view(72, [6, T])
    MQ = view(84, [8, T])
    MK = view(100, [8, T])
    MV = view(116, [4, T])
    PR = view(124, [3, 2, T])
    PT = view(136, [2, T])
    ROT = view(140, [2, HALF])
    SQ = view(142, [2, T])
    SQH = view(0, [2, T])
    RS = view(153, [T])
    prow = view(96, [DEPTH, 2, P])
    lamv_all = view(94, [DEPTH, 256])
    TOKS = view(48, [4, KT * P])
    ZS = view(48, [15, T])
    KK = view(78, [4, T])
    BV = view(86, [4, T])
    GT = view(94, [T])
    SQK = view(94, [4, T])
    RK = view(108.25, [4, T])
    AI = view(96, [T])
    TA, TB = view(98, [T]), view(100, [T])
    W65 = view(102, [NCH * (C + 1)])
    E65 = view(104.125, [NCH * (C + 1)])
    RI = view(106.25, [T])
    AR = view(108.25,  [2, NCH, P])
    BK = view(116.25, [NCH, P])
    BH = view(120.25, [NCH, P])
    BKT = view(144.25, [2, NCH, P])
    AS = view(136.25, [4, 4, P])
    GS = view(132.25, [2, T])
    VT = view(116.25, [4, T])
    AROWF = view(116.25, [2, 1024])
    NB = view(136.25, [C, C])
    NT = view(112, [C * C // 4])
    NTP = view(72, [(C - CSPLIT) * C])
    cA = view(48, [2, 16, P])
    cX = view(64, [2, 16, C])
    cR = view(102, [2, 8, P])
    cB = view(94, [2, 8, P])
    cV = view(78, [2, 2, T])
    S = view(110, [8, P])
    R = view(114, [8, P])
    Y = view(118, [2, 4, T])
    YA = view(48, [4, T])
    X2 = view(56, [KT, T])
    RO = [view(94, [4, T]), view(102, [4, T])]
    GATE = view(110, [4, T])

    ident, ones, bones = cst[:, IDENT:IDENT + P], cst[:, ONES:ONES + P], cst[:, BONES:BONES + P]
    m_dram = dram("mod_rows", [DEPTH, 3, 2, 2048])
    m12_dram = dram("m12_spill", [P, KT, T])
    xdram = dram("x_spill", [P, KT * T])
    a_dram = dram("a_spill", [NCH, P, 16, P])
    r_dram = dram("r_spill", [NCH, P, 8, P])
    b_dram = dram("b_spill", [NCH, P, 8, P])
    v_dram = dram("v_spill", [T, RW])
    vr_dram = dram("v_reversed", [T, RW])
    i_dram = dram("i_spill", [P, C, C])

    def directed(ap, d):
        v = ap.rearrange("p (h c t) -> p h c t", h=2, t=C)
        return v[:, :, ::-1, ::-1] if d else v

    def sides(l):
        return (0, 1) if l == 0 else (1,)

    def outs(l):
        return slice(0, T) if l == 0 else LAT

    chunk_list = [c for l in range(DEPTH) for c in weight_chunks(w, l)]
    chunk_at, split_at = {}, {}
    n = 0
    for l in range(DEPTH):
        for c in weight_chunks(w, l):
            chunk_at[(l, c[0])] = n
            n += 1
    split_list = [(l, *item) for l in range(DEPTH) for item in split_halves(l)]
    hi_slot, hi_before, last_in, turn = {}, {}, {}, {}
    for m, (l, name, half, _, _, (slots, count)) in enumerate(split_list):
        split_at[(l, name, half)] = m
        hi_slot[m] = (slots, turn.get((l, slots, count), 0) % count)
        turn[(l, slots, count)] = turn.get((l, slots, count), 0) + 1
        hi_before[m] = last_in.get(hi_slot[m])
        last_in[hi_slot[m]] = m

    def half_views(m, ring_tensor):
        l, name, half, (k0, k1), (c0, c1), _ = split_list[m]
        n = chunk_at[(l, name)]
        _, nk, nn, _ = chunk_list[n]
        slot = ring_tensor[:, n % NW, 0:nk * nn].rearrange("p (k n) -> p k n", n=nn)
        slots, i = hi_slot[m]
        hi = w_hi[slots][:, i, 0:(k1 - k0) * (c1 - c0)].rearrange("p (k n) -> p k n", n=c1 - c0)
        return slot[:, k0:k1, c0:c1], hi, n

    def rest_name(m):
        l, name = split_list[m][0:2]
        groups, first = gate_groups(l)
        on_gpsimd = 2 <= m - first < 2 * (5 if l < DEPTH - 1 else 9)
        return "w_lo_gpsimd" if on_gpsimd else "w_lo"

    def gate_groups(l):
        groups = [("G12", d) for d in range(8)]
        if l == DEPTH - 1:
            groups[4:4] = [("G0", d) for d in range(0, 8, 2)]
        first = split_at[(l, ("G12", 0), 0)]
        return groups, first

    block = ctx.enter_context(nc.Block())

    @block.sync
    def _(sp):
        sp.dma_start(cst[:, :], tab).then_inc(*dma("tables"))
        n = 0
        rows = [("rwkv_shift_mu", MU, 30), ("norm1_g", N1, 8), ("norm2_g", N2, 8), ("rwkv_w0", W0, 8),
                ("rwkv_a0", A0C, 8), ("rwkv_k_k", KKC, 4), ("rwkv_k_a", KAC, 4), ("rwkv_r_k", RKC, 4),
                ("rwkv_ln_w", LNW, 4), ("rwkv_ln_b", LNB, 4), ("diff_subln_g", SUBG, 1),
                ("mla_q_norm_g", QNG, 3), ("mla_kv_norm_g", KVG, 2)]
        for l in range(DEPTH):
            for src, r0, nr in ((w["ada_b"][l], ADAB, 48), (w["final_norm_g"], FING, 8),
                                (w["c"][0], CVEC, 8), (w["c_ctx"], CCTX, 8)):
                sp.dma_start(prow[r0:r0 + nr, l, 1, :], src.rearrange("(r n) -> r n", n=P)).then_inc(*dma(f"prow2_{l}"))
        for l in range(DEPTH):
            if l:
                sp.wait_ge(*full("lora_g", l - 1, 3))
            for i, name in enumerate(("rwkv_w2", "rwkv_a2")):
                sp.dma_start(lora[:, i, :], w[name][l].rearrange("d k n -> (d k) n")).then_inc(*dma("lora", l))
            sp.dma_start(lora[:, 2, :], w["rwkv_g2"][l]).then_inc(*dma("lora", l))
            for name, nk, nn, parts in weight_chunks(w, l):
                if n >= NW:
                    sp.wait_ge(*plan.released(n - NW))
                slot = ring[:, n % NW, 0:nk * nn].rearrange("p (k n) -> p k n", n=nn)
                for c0, c1, k0, k1, src in parts:
                    sp.dma_start(slot[:, k0:k1, c0:c1], src).then_inc(*dma(f"weights_in{n % NW}", n))
                n += 1
                if n == 4:
                    for ll in range(DEPTH):
                        for name, r0, nr in rows:
                            src = w[name][ll]
                            if len(src.shape) == 2:
                                src = src.rearrange("a b -> (a b)")
                            sp.dma_start(prow[r0:r0 + nr, ll, 0, :], src.rearrange("(r n) -> r n", n=P)).then_inc(*dma(f"prow_{ll}"))
                        sp.dma_start(lamv_all[:, ll, :], w["diff_lambda"][ll].rearrange("a b -> (a b)").partition_broadcast(P)).then_inc(*dma(f"lamv_{ll}"))

    @block.gpsimd
    def _(pool):
        for i in range(4):
            src = w["ctx"][0] if i < 2 else w["x"][0]
            pool.dma_start(TOKS[:, i], src[P * (i % 2):P * (i % 2) + P, :]).then_inc(*dma(f"tok{i}"))
        for l in range(DEPTH):
            for key in [("fd", l - 1, k) for k in range(KT)] if l else [("xin", i, h) for i in range(4) for h in range(2)]:
                pool.wait_ge(*drained(*key))
            pool.dma_start(xdram, X.rearrange("p k t -> p (k t)")).then_inc(*dma("x_spilled", l))
            for c in range(NCH):
                pool.wait_ge(*drained("vtok", l, c))
                pool.dma_start(v_dram[C * c:C * c + C, :], VT[0:C, c % 4, :]).then_inc(*dma(f"v_spilled{c % 4}", l, c))
            for c in range(NCH):
                pool.wait_ge(*when(f"v_spilled{c % 4}", l, c))
            for h in range(2):
                rows = slice(HALF * h, HALF * h + HALF)
                src = v_dram[rows, :].rearrange("t (h v) -> h t v", h=8)[:, ::-1, :]
                pool.dma_start(vr_dram[rows, :].rearrange("t (h v) -> h t v", h=8), src).then_inc(*dma("v_reversed", l))
            for i in range(8):
                pool.wait_ge(*when("bk", l, i))
                if i:
                    pool.wait_ge(*full("bkt", l, i - 1, 1))
                nc.gpsimd.tensor_tensor(BH, BK, dend[:, i, :].unsqueeze(2).broadcast_to([P, NCH, P]), ALU.mult).then_inc(*mark("bh", l, i))
                if i < 4 or l == DEPTH - 1:
                    groups, gate_half = gate_groups(l)
                    for m in range(gate_half + 2 * i + 2, gate_half + 2 * i + 4):
                        raw, hi, _ = half_views(m, ring)
                        lo, _, _ = half_views(m, w_lo)
                        pool.wait_ge(*when("w_hi", m))
                        nc.gpsimd.tensor_tensor(lo, raw, hi.bitcast(F32), ALU.subtract).then_inc(*mark(rest_name(m), m))
            for g in range(4):
                pool.wait_ge(*when(f"a_spilled{g}", l, 7))
            for i in (6, 7):
                pool.wait_ge(*when(f"b_spilled{i % 2}", l, i))
                pool.wait_ge(*when(f"r_spilled{i % 2}", l, i))
            pool.wait_ge(*when("v_reversed", l))

            def chunk_early(c):
                b = c % 2
                name = f"chunk_in{b}"
                pool.dma_start(cA[:, b], a_dram[c]).then_inc(*dma(name, l, c))
                pool.dma_start(cR[:, b], r_dram[c]).then_inc(*dma(name, l, c))
                pool.dma_start(cB[:, b], b_dram[c]).then_inc(*dma(name, l, c))
                pool.dma_start(cV[C:P, b, 0], v_dram[C * c:C * c + C, :]).then_inc(*dma(name, l, c))
                pool.dma_start(cV[C:P, b, 1], vr_dram[C * c:C * c + C, :]).then_inc(*dma(name, l, c))

            for c in range(2):
                chunk_early(c)
            pool.wait_ge(*when("nb_in", l))
            for s in range(1, LATE):
                t0 = max(s + 1, CSPLIT)
                n = C - t0
                tmp = NTP[:, 0:s * n].rearrange("p (j t) -> p j t", t=n)
                if 2 <= s < CSPLIT:
                    pool.wait_ge(*when("inverse_col", l, s))
                nc.gpsimd.tensor_tensor(tmp, NB[:, 0:s, s:s + 1].broadcast_to([P, s, n]), NB[:, s:s + 1, t0:C].broadcast_to([P, s, n]), ALU.mult).then_inc(*mark("inverse_term", l, s))
                pool.wait_ge(*when("inverse_term", l, s))
                nc.gpsimd.tensor_tensor(NB[:, 0:s, t0:C], NB[:, 0:s, t0:C], tmp, ALU.add).then_inc(*mark("inverse_right", l, s))
                pool.wait_ge(*when("inverse_right", l, s))
            pool.wait_ge(*when("inverted", l))
            for name, u in (("inverse_out_first", slice(0, 32)), ("inverse_out", slice(32, P))):
                pool.dma_start(i_dram[u].rearrange("u s t -> u (s t)"), NB[u].rearrange("p s t -> p (s t)")).then_inc(*dma(name, l))
            pool.wait_ge(*when("inverse_out_first", l))
            for p in range(4):
                pool.wait_ge(*drained("bonus", l, p))
            for c in range(NCH):
                b = c % 2
                if c == 2:
                    pool.wait_ge(*when("inverse_out", l))
                if c >= 2:
                    pool.wait_ge(*full("S", l, c - 2, 1))
                    if not (l and c - 2 < 4):
                        pool.wait_ge(*full("Y", l, c - 2, 1))
                pool.dma_start(cX[0:C, b], i_dram[16 * c:16 * c + 16].rearrange("u s t -> s u t")).then_inc(*dma(f"chunk_in{b}", l, c))
                if c >= 2:
                    chunk_early(c)
            pool.wait_ge(*full("S", l, NCH - 1, 1))
            pool.wait_ge(*full("Y", l, NCH - 1, 1))
            pool.dma_start(X2.rearrange("p k t -> p (k t)"), xdram).then_inc(*dma("x_back", l))
        for i in range(2):
            for h in range(2):
                cols = slice(512 * h, 512 * h + 512)
                pool.wait_ge(*drained("xout", i, h))
                pool.dma_start(out[0, P * i:P * i + P, cols], TOKS[:, i, cols]).then_inc(*dma("stored", i, h))
        pool.wait_ge(*when("stored", 1, 1))

    @block.tensor
    def _(pe):
        chunk_no = [0]
        chunk_of = {}

        def job(*key):
            n = plan.job(*key)
            if n >= NBANK:
                pe.wait_ge(sem_of(f"psum_drained{n % NBANK}"), n // NBANK)
            return PS[n % NBANK]

        def done(*key):
            n = plan.jobs[key]
            return sem_of(f"psum_full{n % NBANK}"), 1

        def weights(l, *name):
            n = chunk_no[0]
            chunk_no[0] += 1
            got, nk, nn, _ = chunk_list[n]
            assert got == name, (got, name)
            pe.wait_ge(*when(f"weights_in{n % NW}", n))
            chunk_of[name] = n
            return ring[:, n % NW, 0:nk * nn].rearrange("p (k n) -> p k n", n=nn)

        def release(name, *key):
            plan.release[chunk_of[name]] = key

        def sum_rows(key, tiles, lhs, toks, sq=SQ):
            ps = job(*key)
            n = toks.stop - toks.start
            for k in range(tiles):
                pe.wait_ge(*when("sq", *key, k))
                mm = pe.matmul(ps[:, 0:n], lhs, sq[:, k % 2, toks], start=(k == 0), stop=(k == tiles - 1))
                if k < tiles - 1:
                    mm.then_inc(*mark("squares_read", *key, k))
            mm.then_inc(*done(*key))

        def project(key, wt, c0, m, rhs, nk, ps_rows=slice(0, P), n=T, ready=None):
            ps = job(*key)
            for k in range(nk):
                if ready:
                    pe.wait_ge(*ready(k))
                mm = pe.matmul(ps[ps_rows, 0:n], wt[:, k, c0:c0 + m], rhs(k), start=(k == 0), stop=(k == nk - 1))
            mm.then_inc(*done(*key))

        def half_is_read(m, mm, *key):
            if key:
                mm.then_inc(*done(*key))
                plan.read[m] = key
            else:
                mm.then_inc(*mark("half_read", m))
                plan.read[m] = ("mark", "half_read", m)

        def project_split(key, l, name, half, x_hi, x_lo, n, first=0, last=None, ready=None, rows=slice(0, P)):
            m = split_at[(l, name, half)]
            lo, hi, _ = half_views(m, w_lo)
            ps = bank(*key)[rows, 0:n]
            nk = split_list[m][3][1]
            last = first + nk if last is None else last
            pe.wait_ge(*when(rest_name(m), m))
            for k in range(nk):
                if ready:
                    pe.wait_ge(*ready(first + k))
                pe.matmul(ps, hi[:, k, :], x_hi(first + k), start=(first + k == 0), stop=False, skip_group_check=True)
                pe.matmul(ps, hi[:, k, :], x_lo(first + k), start=False, stop=False, skip_group_check=True)
                mm = pe.matmul(ps, lo[:, k, :], x_hi(first + k), start=False, stop=(first + k == last - 1), skip_group_check=True)
            half_is_read(m, mm, *(key if first + nk == last else ()))

        def project_h(key, l, name, half, toks, **more):
            job(*key)
            project_split(key, l, name, half, lambda k: h_hi[:, k, toks], lambda k: h_lo[:, k, toks], toks.stop - toks.start, **more)

        pe.wait_ge(*when("tables"))
        for i in range(4):
            pe.wait_ge(*when(f"tok{i}"))
            for h in range(2):
                ps = job("xin", i, h)
                for k in range(4):
                    mm = pe.transpose(ps[:, P * k:P * k + P], TOKS[:, i, P * (4 * h + k):P * (4 * h + k) + P], ident)
                mm.then_inc(*done("xin", i, h))

        def modulation(l, part, js=range(8)):
            for j in [8 * part + i for i in js]:
                wt = weights(l, "ada", l, j)
                ps = job("ada", l, j)
                for k in range(KT):
                    mm = pe.matmul(ps[0:2, 0:256], csil[:, k, :], wt[:, k, :], start=(k == 0), stop=(k == KT - 1))
                mm.then_inc(*done("ada", l, j))
                release(("ada", l, j), "ada", l, j)

        def modulation_columns(l, part):
            pe.wait_ge(*when(f"mods_in_{l}_{part}"))
            ps = job("modt", l, part)
            pe.transpose(ps[:, 0:32], mrow[:, part, :], cst[0:32, IDENT:IDENT + 32]).then_inc(*done("modt", l, part))

        for l in range(DEPTH):
            pe.wait_ge(*when(f"prow2_{l}"))
            ps = job("par2", l)
            pe.transpose(ps[:, 0:NPAR2], prow[0:NPAR2, l, 1, :], cst[0:NPAR2, IDENT:IDENT + NPAR2]).then_inc(*done("par2", l))
        pe.wait_ge(*when("csil"))
        modulation(0, 0)
        for l in range(DEPTH):
            pe.wait_ge(*when(f"prow_{l}"))
            ps = job("par", l)
            pe.transpose(ps[:, 0:NPAR], prow[0:NPAR, l, 0, :], cst[0:NPAR, IDENT:IDENT + NPAR]).then_inc(*done("par", l))
        modulation(0, 1, (0, 1))
        modulation_columns(0, 0)

        for l in range(DEPTH):
            o = outs(l)
            no = o.stop - o.start
            sum_rows(("n1", l), KT, ones, slice(0, T), SQH)
            if l == 0:
                modulation(0, 1, (2, 3))
            for j in range(4):
                weights(l, "B", j)
                for jj in range(2):
                    b = 2 * j + jj
                    tk = o if b < 4 else slice(0, T)
                    project_h(("qk", l, b), l, ("B", j), jj, tk, ready=(lambda k: when("h1", l, k)) if b == 0 else None)
                    if b >= 1:
                        pe.wait_ge(*drained("qk", l, b - 1))
                        ps = job("qkrot", l, b - 1)
                        pe.matmul(ps[:, 0:HALF], cst[:, PERM:PERM + P], QK[:, b - 1, LAT], start=True, stop=True).then_inc(*done("qkrot", l, b - 1))
                release(("B", j), "qk", l, 2 * j + 1)
            for j in range(2):
                weights(l, "B", 4 + j)
                pss = [job("vd", l, j, t) for t in range(4)]
                for half in range(2):
                    m = split_at[(l, ("B", 4 + j), half)]
                    lo, hi, _ = half_views(m, w_lo)
                    pe.wait_ge(*when(rest_name(m), m))
                    for t in range(4):
                        tt = slice(P * t, P * t + P)
                        for k in range(4):
                            kk = 4 * half + k
                            pe.matmul(pss[t][:, 0:256], h_hi[:, kk, tt], hi[:, k, :], start=(kk == 0), stop=False, skip_group_check=True)
                            pe.matmul(pss[t][:, 0:256], h_lo[:, kk, tt], hi[:, k, :], start=False, stop=False, skip_group_check=True)
                            mm = pe.matmul(pss[t][:, 0:256], h_hi[:, kk, tt], lo[:, k, :], start=False, stop=(kk == KT - 1), skip_group_check=True)
                        if half and t < 3:
                            mm.then_inc(*done("vd", l, j, t))
                    half_is_read(m, mm, *(("vd", l, j, 3) if half else ()))
                release(("B", 4 + j), "vd", l, j, 3)
            pe.wait_ge(*drained("qk", l, 7))
            ps = job("qkrot", l, 7)
            pe.matmul(ps[:, 0:HALF], cst[:, PERM:PERM + P], QK[:, 7, LAT], start=True, stop=True).then_inc(*done("qkrot", l, 7))
            for b in range(6):
                if b % 2 == 0:
                    weights(l, "C", b // 2)
                project_h(("zc", l, b), l, ("C", b // 2), b % 2, o if b < 3 else slice(0, T), rows=slice(0, P) if b < 5 else slice(0, 96))
                if b % 2:
                    release(("C", b // 2), "zc", l, b)
            sum_rows(("qn", l), 3, ones, o)
            sum_rows(("kvn", l), 2, ones, slice(0, T))
            pe.wait_ge(*drained("zc", l, 5))
            ps = job("krot", l)
            pe.matmul(ps[64:96, 0:HALF], cst[64:96, PERM32:PERM32 + 32], ZC[64:96, 5, LAT], start=True, stop=True).then_inc(*done("krot", l))
            for k in range(3):
                pe.wait_ge(*when("qnorm", l, k))
            for j in range(2):
                wt = weights(l, "uq", j)
                for hh in range(4):
                    h = 4 * j + hh
                    project(("mq", l, h), wt, 96 * hh, 96, lambda k: ZC[:, k, o], 3, ps_rows=slice(0, 96), n=no)
                    if h >= 1:
                        pe.wait_ge(*drained("mq", l, h - 1))
                        ps = job("mqrot", l, h - 1)
                        pe.matmul(ps[64:96, 0:HALF], cst[64:96, PERM32:PERM32 + 32], MQ[64:96, h - 1, LAT], start=True, stop=True).then_inc(*done("mqrot", l, h - 1))
                release(("uq", j), "mq", l, 4 * j + 3)
            for k in range(2):
                pe.wait_ge(*when("kvnorm", l, k))
            wt = weights(l, "uk")
            for j in range(4):
                project(("mk", l, j), wt, P * j, P, lambda k: ZC[:, 3 + k, :], 2)
            release(("uk",), "mk", l, 3)
            wt = weights(l, "uv")
            for t in range(4):
                ps = job("mv", l, t)
                for k in range(2):
                    mm = pe.matmul(ps[:, :], ZC[:, 3 + k, P * t:P * t + P], wt[:, k, :], start=(k == 0), stop=(k == 1))
                mm.then_inc(*done("mv", l, t))
            release(("uv",), "mv", l, 3)
            pe.wait_ge(*drained("mq", l, 7))
            ps = job("mqrot", l, 7)
            pe.matmul(ps[64:96, 0:HALF], cst[64:96, PERM32:PERM32 + 32], MQ[64:96, 7, LAT], start=True, stop=True).then_inc(*done("mqrot", l, 7))

            units = attention_units(l)

            def scores(i):
                kind, h, q, nk = units[i]
                qs = slice(P * q, P * q + P)
                if kind == "diff":
                    if i == 0:
                        for b in range(8):
                            pe.wait_ge(*when("qk_ready", l, b))
                    for c in range(2):
                        ps = job("sc", l, i, c)
                        pe.matmul(ps[:, 0:P * nk], QK[64 * c:64 * c + 64, h, qs], QK[64 * c:64 * c + 64, 4 + h, 0:P * nk],
                                  start=True, stop=True).then_inc(*done("sc", l, i, c))
                else:
                    if units[i - 1][0] == "diff":
                        pe.wait_ge(*when("mk_rope", l))
                        for j in range(4):
                            pe.wait_ge(*drained("mk", l, j))
                        for j in range(8):
                            pe.wait_ge(*when("mq_ready", l, j))
                    ps = job("sc", l, i, 0)
                    pe.matmul(ps[:, 0:P * nk], MQ[0:96, h, qs], MK[0:96, h, 0:P * nk], start=True, stop=True).then_inc(*done("sc", l, i, 0))

            def transposed(i):
                kind, h, q, nk = units[i]
                pe.wait_ge(*when("probs", l, i))
                ps = job("pt", l, i)
                for t in range(nk):
                    mm = pe.transpose(ps[:, P * t:P * t + P], PR[:, i % 3, 0, P * t:P * t + P], ident)
                mm.then_inc(*done("pt", l, i))

            def values(i):
                kind, h, q, nk = units[i]
                pe.wait_ge(*drained("pt", l, i))
                if i == 0:
                    for j in range(2):
                        for t in range(4):
                            pe.wait_ge(*drained("vd", l, j, t))
                    for t in range(4):
                        pe.wait_ge(*drained("mv", l, t))
                ps = job("av", l, i)
                for t in range(nk):
                    if kind == "diff":
                        mm = pe.matmul(ps[:, 0:P], VD[:, t, P * h:P * h + P], PT[:, i % 2, P * t:P * t + P], start=(t == 0), stop=(t == nk - 1))
                    else:
                        r = 64 * (h % 2)
                        mm = pe.matmul(ps[r:r + 64, 0:P], MV[:, t, 64 * h:64 * h + 64], PT[:, i % 2, P * t:P * t + P], start=(t == 0), stop=(t == nk - 1))
                mm.then_inc(*done("av", l, i))

            scores(0)
            scores(1)
            for i in range(len(units)):
                if i + 2 < len(units):
                    scores(i + 2)
                if i >= 1:
                    values(i - 1)
                transposed(i)
            values(len(units) - 1)
            for j in range(8):
                weights(l, "A", j)
                for jj in range(2 if j < 7 else 1):
                    b = 2 * j + jj
                    tk = o if b < 4 or b == 14 else slice(0, T)
                    project_h(("za", l, b), l, ("A", j), jj, tk)
                    if b in BN_AT:
                        sum_rows(("bn", l, BN_AT.index(b)), 1, ones, o)
                    if b in KK_AT:
                        p = KK_AT.index(b)
                        pe.wait_ge(*when("kk_squared", l, p))
                        ps = job("kkn", l, p)
                        pe.matmul(ps[:, :], bones, SQK[:, p, :], start=True, stop=True).then_inc(*done("kkn", l, p))
                release(("A", j), "za", l, min(2 * j + 1, 14))
            for c in range(NCH):
                if c == 0:
                    for p in range(4):
                        pe.wait_ge(*drained("za", l, 8 + p))
                ps = job("vtok", l, c)
                for p in range(4):
                    mm = pe.transpose(ps[0:C, P * p:P * p + P], ZS[:, 8 + p, C * c:C * c + C], ident)
                mm.then_inc(*done("vtok", l, c))

            def branch12(d):
                weights(l, "G12", d)
                for g in range(2):
                    project_h(("g12", l, d, g), l, ("G12", d), g, o)
                release(("G12", d), "g12", l, d, 1)
                wt = weights(l, "W12", d)
                if d == 0:
                    for h in range(4):
                        pe.wait_ge(*when("yb", l, h))
                    for i in range(len(units)):
                        if units[i][0] == "mla":
                            pe.wait_ge(*drained("av", l, i))
                for g, y in enumerate((YB, YC)):
                    ps = job("w12", l, d, g)
                    for k in range(4):
                        mm = pe.matmul(ps[:, 0:no], wt[:, 4 * g + k, :], y[:, k, o], start=(k == 0), stop=(k == 3))
                    mm.then_inc(*done("w12", l, d, g))
                release(("W12", d), "w12", l, d, 1)

            def gate0(d):
                weights(l, "G0", d)
                project_h(("g0", l, d), l, ("G0", d), 0, o)
                release(("G0", d), "g0", l, d)

            def lora_in(i):
                d, p = i // 4, i % 4
                rows = slice(64 * d, 64 * d + 64)
                for n, name in enumerate(("lora_w", "lora_a")):
                    if i == 0 and n == 0:
                        pe.wait_ge(*when("lora", l))
                        pe.wait_ge(*when("tanh", l))
                        pe.wait_ge(*drained("za", l, 13))
                    ps = job(name, l, i)
                    pe.matmul(ps[:, :], lora[rows, n, P * p:P * p + P], ZS[rows, 12 + n, :], start=True, stop=True).then_inc(*done(name, l, i))

            def scores_in_chunk(i):
                pe.wait_ge(*when("ar", l, i))
                pe.wait_ge(*when("bk", l, i))
                for g in range(0, 4, 2):
                    pss = [job("A", l, i, g + hh) for hh in range(2)]
                    for c in range(4):
                        for hh in range(2):
                            ch = 4 * (g // 2) + c
                            rows = slice(64 * hh, 64 * hh + 64)
                            mm = pe.matmul(pss[hh][:, P * c:P * c + P], BK[rows, ch, :], AR[rows, i % 2, ch, :], start=True, stop=True)
                            if c == 3:
                                mm.then_inc(*done("A", l, i, g + hh))
                pe.wait_ge(*when("bh", l, i))
                for g in range(2):
                    ps = job("bkt", l, i, g)
                    for c in range(4):
                        mm = pe.transpose(ps[:, P * c:P * c + P], BH[:, 4 * g + c, :], ident)
                    mm.then_inc(*done("bkt", l, i, g))

            def beside_scores(j):
                if j < 4:
                    branch12(j)
                elif l == DEPTH - 1 and j < 8:
                    gate0(2 * j - 8)
                    gate0(2 * j - 7)

            lora_in(0)
            lora_in(1)
            beside_scores(0)
            for i in range(8):
                if i + 2 < 8:
                    lora_in(i + 2)
                scores_in_chunk(i)
                beside_scores(i + 1)
            for p in range(4):
                pe.wait_ge(*when("rkk", l, p))
                ps = job("bonus", l, p)
                pe.matmul(ps[:, 0:no], bones, BV[:, p, o], start=True, stop=True).then_inc(*done("bonus", l, p))
            for d in range(4, 8):
                branch12(d)
            modulation(l, 1, range(8) if l else range(4, 8))
            modulation(l, 2)
            if l + 1 < DEPTH:
                modulation(l + 1, 0)

            def state_key(c, g):
                return ("S", l, c, g)

            pe.wait_ge(*when("state_zero", l))
            for c in range(NCH):
                b = c % 2
                pe.wait_ge(*when(f"chunk_in{b}", l, c))
                for g in range(2):
                    ps = job("U", l, c, g)
                    if c:
                        pe.wait_ge(*drained("S", l, c - 1, g))
                    for ii in range(4):
                        i = 4 * g + ii
                        pe.matmul(ps[0:C, P * ii:P * ii + P], cR[:, b, i, 0:C], S[:, i, :], start=True, stop=False, skip_group_check=True)
                        for hh in range(2):
                            v0 = P * (i % 4) + C * hh
                            mm = pe.matmul(ps[0:C, P * ii + C * hh:P * ii + C * hh + C], cA[C:P, b, 2 * i + hh, 0:C],
                                           cV[C:P, b, i // 4, v0:v0 + C], start=False, stop=True, skip_group_check=True)
                    mm.then_inc(*done("U", l, c, g))
                for g in range(2):
                    ps = job("SA", l, c, g)
                    pe.wait_ge(*drained("U", l, c, g))
                    for ii in range(4):
                        i = 4 * g + ii
                        for hh in range(2):
                            mm = pe.matmul(ps[0:C, P * ii + C * hh:P * ii + C * hh + C], cX[0:C, b, 2 * i + hh, :],
                                           R[0:C, i, C * hh:C * hh + C], start=True, stop=True)
                    mm.then_inc(*done("SA", l, c, g))
                yjobs = not (l and c < 4)
                for g in range(2):
                    pe.wait_ge(*drained("SA", l, c, g))
                    if yjobs:
                        ps = job("Y", l, c, g)
                        for ii in range(4):
                            i = 4 * g + ii
                            pe.matmul(ps[:, C * ii:C * ii + C], S[:, i, :], cR[:, b, i, C:P], start=True, stop=False, skip_group_check=True)
                            for hh in range(2):
                                v0 = P * (i % 4) + C * hh
                                mm = pe.matmul(ps[C * hh:C * hh + C, C * ii:C * ii + C], cV[:, b, i // 4, v0:v0 + C],
                                               cA[:, b, 2 * i + hh, C:P], start=False, stop=True, skip_group_check=True)
                        mm.then_inc(*done("Y", l, c, g))
                    ps = job("S", l, c, g)
                    for ii in range(4):
                        i = 4 * g + ii
                        mm = pe.matmul(ps[:, P * ii:P * ii + P], cB[:, b, i, :], cV[:, b, i // 4, P * (i % 4):P * (i % 4) + P],
                                       start=True, stop=True)
                    mm.then_inc(*done("S", l, c, g))

            modulation_columns(l, 1)
            modulation_columns(l, 2)
            if l + 1 < DEPTH:
                modulation_columns(l + 1, 0)
            pe.wait_ge(*when("gd", l))
            for p in range(4):
                pe.wait_ge(*when("ysum", l, p))
                ps = job("gmean", l, p)
                pe.matmul(ps[:, 0:no], bones, Y[:, 0, p, o], start=True, stop=True).then_inc(*done("gmean", l, p))
            if l < DEPTH - 1:
                gate0(0)
            for p in range(4):
                pe.wait_ge(*when("ysq", l, p))
                ps = job("gvar", l, p)
                pe.matmul(ps[:, 0:no], bones, RO[0][:, p, o], start=True, stop=True).then_inc(*done("gvar", l, p))
            if l < DEPTH - 1:
                gate0(1)
                gate0(2)
            for p in range(4):
                ps = job("lora_g", l, p)
                pe.matmul(ps[:, 0:no], lora[:, 2, P * p:P * p + P], ZS[:, 14, o], start=True, stop=True).then_inc(*done("lora_g", l, p))

            if l < DEPTH - 1:
                gate0(3)
                gate0(4)

            for d in range(8):
                wt = weights(l, "W0", d)
                ps = job("w0", l, d)
                for k in range(4):
                    if d == 0:
                        pe.wait_ge(*drained("lora_g", l, k))
                    mm = pe.matmul(ps[:, 0:no], wt[:, k, :], YA[:, k, o], start=(k == 0), stop=(k == 3))
                mm.then_inc(*done("w0", l, d))
                release(("W0", d), "w0", l, d)
                if l < DEPTH - 1 and d + 5 < 8:
                    gate0(d + 5)
            for j in range(4):
                weights(l, "O", j)
                for jj in range(2):
                    key = ("wo", l, 2 * j + jj)
                    job(*key)
                    project_split(key, l, ("O", j), jj, lambda k: m_hi[:, k, o], lambda k: m_lo[:, k, o], no,
                                  ready=(lambda k: when("m_rest", l, k)) if key[2] == 0 else None)
                release(("O", j), "wo", l, 2 * j + 1)
            sum_rows(("n2", l), KT, ones, o, SQH)
            for j in range(11):
                weights(l, "FG", j)
                weights(l, "FU", j)
                for jj in range(2):
                    for key, name in ((("fg", l, 2 * j + jj), "FG"), (("fu", l, 2 * j + jj), "FU")):
                        project_h(key, l, (name, j), jj, o, ready=(lambda k: when("h2", l, k)) if key[2] == 0 and name == "FG" else None)
                release(("FG", j), "fg", l, 2 * j + 1)
                release(("FU", j), "fu", l, 2 * j + 1)
            for dp in range(4):
                for jj in range(2):
                    job("fd", l, 2 * dp + jj)
                for kc, (k0, k1) in enumerate(((0, 8), (8, 16), (16, 22))):
                    weights(l, "FD", dp, kc)
                    for jj in range(2):
                        project_split(("fd", l, 2 * dp + jj), l, ("FD", dp, kc), jj, lambda k: f_hi(k, o), lambda k: f_lo[:, k, o], no,
                                      first=k0, last=FT, ready=(lambda k: when("ffn_hidden", l, k)) if dp == 0 and jj == 0 else None)
                    plan.release[chunk_of[("FD", dp, kc)]] = plan.read[split_at[(l, ("FD", dp, kc), 1)]]
        sum_rows(("nf",), KT, ones, LAT, SQH)
        for i in range(2):
            for h in range(2):
                ps = job("xout", i, h)
                for k in range(4):
                    if i == 0:
                        pe.wait_ge(*when("final", 4 * h + k))
                    mm = pe.transpose(ps[:, P * k:P * k + P], H[:, 4 * h + k, HALF + P * i:HALF + P * i + P], ident)
                mm.then_inc(*done("xout", i, h))

    @block.scalar
    def _(act):
        A = nc.scalar.activation

        def step(ins):
            ins.then_inc(*mark("act_step", plan.count.get("act_step", 0)))
            act.wait_ge(sem_of("act_step"), plan.count["act_step"])

        def weights_rounded(m):
            raw, hi, n = half_views(m, ring)
            act.wait_ge(*when(f"weights_in{n % NW}", n))
            if hi_before[m] is not None:
                act.wait_ge(*plan.half_read(hi_before[m]))
            A(hi, raw, ACT.Copy).then_inc(*mark("w_hi", m))

        def squares(key, src, tiles, toks, sq=SQ):
            for k in range(tiles):
                if k >= 2:
                    act.wait_ge(*when("squares_read", *key, k - 2))
                elif last_sum[0] is not None:
                    act.wait_ge(*full(*last_sum[0]))
                A(sq[:, k % 2, toks], src(k), ACT.Square).then_inc(*mark("sq", *key, k))
            last_sum[0] = key

        last_sum = [None]

        def root(key, toks):
            act.wait_ge(*drained(*key))
            A(RS[:, toks], RS[:, toks], ACT.Sqrt).then_inc(*mark("root", *key))

        for i in range(4):
            for h in range(2):
                act.wait_ge(*full("xin", i, h))
                A(X[:, 4 * h:4 * h + 4, P * i:P * i + P], bank("xin", i, h)[:, :].rearrange("p (k t) -> p k t", k=4), ACT.Copy).then_inc(*drain("xin", i, h))
        rows_before = {}

        def modulation(l, part, halves=(0, 1)):
            for h in halves:
                js = range(8 * part + 4 * h, 8 * part + 4 * h + 4)
                if h in rows_before:
                    act.wait_ge(*when(f"mods_out{h}", *rows_before[h]))
                for j in js:
                    act.wait_ge(*full("ada", l, j))
                    if j == js[0] and part and (l, part, h) != (0, 1, 0):
                        act.wait_ge(*full("bkt", l, 7, 1))
                    A(AROWF[0:2, h, 256 * (j % 4):256 * (j % 4) + 256], bank("ada", l, j)[0:2, 0:256], ACT.Copy).then_inc(*drain("ada", l, j))
                for j in js:
                    act.wait_ge(*drained("ada", l, j))
                act.dma_start(m_dram[l, part, :, 1024 * h:1024 * h + 1024], AROWF[0:2, h, :]).then_inc(*dma(f"mods_out{h}", l, part))
                rows_before[h] = (l, part)

        def modulation_back(l, part):
            for h in range(2):
                act.wait_ge(*when(f"mods_out{h}", l, part))
            act.dma_start(mrow[:, part, :], m_dram[l, part].rearrange("s (j n) -> (s j) n", n=P)).then_inc(*dma(f"mods_in_{l}_{part}"))

        for l in range(DEPTH):
            act.wait_ge(*full("par2", l))
            A(par2[:, l, :], bank("par2", l)[:, 0:NPAR2], ACT.Copy).then_inc(*drain("par2", l))
        act.wait_ge(*drained("par2", 0))
        A(csil[:, :, 0], par2[:, 0, CCTX:CCTX + 8], ACT.Sigmoid).then_inc(*mark("csig", 0))
        A(csil[:, :, 1], par2[:, 0, CVEC:CVEC + 8], ACT.Sigmoid).then_inc(*mark("csig", 1))
        modulation(0, 0)
        modulation_back(0, 0)
        for l in range(DEPTH):
            act.wait_ge(*full("par", l))
            A(par[:, l, :], bank("par", l)[:, 0:NPAR], ACT.Copy).then_inc(*drain("par", l))
        for l in range(DEPTH):
            act.wait_ge(*when("lam_dots", l))
            A(lam_all[:, l, 0:2], lam_all[:, l, 0:2], ACT.Exp).then_inc(*mark("lam_exp", l))
        act.wait_ge(*drained("xin", 3, 1))
        for l in range(DEPTH):
            mods = mods_all[:, l]
            o = outs(l)
            no = o.stop - o.start
            if l:
                for k in range(KT):
                    act.wait_ge(*drained("fd", l - 1, k))
            squares(("n1", l), lambda k: X[:, k, :], KT, slice(0, T), SQH)
            b0 = split_at[(l, ("B", 0), 0)]
            for m in range(3):
                weights_rounded(b0 + m)
            root(("n1", l), slice(0, T))
            for k in range(KT):
                for s in (0, 1):
                    tk = slice(HALF * s, HALF * s + HALF)
                    act.wait_ge(*when("h1_scaled", l, k, s))
                    A(h_hi[:, k, tk], h_raw[:, k, tk], ACT.Identity, bias=mods[:, k, s:s + 1]).then_inc(*mark("h1_hi", l, k, s))
            if l == 0:
                modulation(0, 1, (0,))
            for b in range(8):
                tk = o if b < 4 else slice(0, T)
                act.wait_ge(*full("qk", l, b))
                A(QK[:, b, tk], bank("qk", l, b)[:, 0:tk.stop - tk.start], ACT.Copy).then_inc(*drain("qk", l, b))
                weights_rounded(b0 + b + 3)
            for j in range(2):
                weights_rounded(b0 + 11 + 2 * j)
                if j == 0:
                    weights_rounded(b0 + 12)
                for t in range(4):
                    act.wait_ge(*full("vd", l, j, t))
                    A(VD[:, t, 256 * j:256 * j + 256], bank("vd", l, j, t)[:, 0:256], ACT.Copy).then_inc(*drain("vd", l, j, t))
            weights_rounded(b0 + 14)
            for b in range(6):
                tk = o if b < 3 else slice(0, T)
                rows = slice(0, P) if b < 5 else slice(64, 96)
                act.wait_ge(*full("zc", l, b))
                A(ZC[rows, b, tk], bank("zc", l, b)[rows, 0:tk.stop - tk.start], ACT.Copy).then_inc(*drain("zc", l, b))
                if b < 3:
                    weights_rounded(b0 + 15 + b)
            for b in range(5):
                act.wait_ge(*drained("zc", l, b))
            squares(("qn", l), lambda k: ZC[:, k, o], 3, o)
            squares(("kvn", l), lambda k: ZC[:, 3 + k, :], 2, slice(0, T))
            root(("qn", l), o)
            root(("kvn", l), slice(0, T))
            for h in range(8):
                act.wait_ge(*full("mq", l, h))
                A(MQ[0:96, h, o], bank("mq", l, h)[0:96, 0:no], ACT.Copy).then_inc(*drain("mq", l, h))
            for j in range(4):
                act.wait_ge(*full("mk", l, j))
                for hh in range(2):
                    ins = A(MK[0:64, 2 * j + hh, :], bank("mk", l, j)[64 * hh:64 * hh + 64, :], ACT.Copy)
                ins.then_inc(*drain("mk", l, j))
            if l == 0:
                act.wait_ge(*when("mods_out0", 0, 1))
                act.wait_ge(*when("mods_out1", 0, 0))
            for t in range(4):
                act.wait_ge(*full("mv", l, t))
                A(MV[:, t, :], bank("mv", l, t)[:, :], ACT.Copy).then_inc(*drain("mv", l, t))
            units = attention_units(l)

            def exponentials(i):
                kind, h, q, nk = units[i]
                scale = DIFF_SCALE if kind == "diff" else MLA_SCALE
                for c in range(2 if kind == "diff" else 1):
                    act.wait_ge(*when("negmax", l, i, c))
                    if i >= 3 and c == 0:
                        act.wait_ge(*full("pt", l, i - 3))
                    A(PR[:, i % 3, c, 0:P * nk], bank("sc", l, i, c)[:, 0:P * nk], ACT.Exp, bias=smax[:, c, i:i + 1],
                      scale=scale, accum_out=ssum[:, c, i:i + 1]).then_inc(*drain("sc", l, i, c))

            def evacuate(i):
                kind, h, q, nk = units[i]
                act.wait_ge(*full("pt", l, i))
                if i >= 2:
                    act.wait_ge(*full("av", l, i - 2))
                A(PT[:, i % 2, 0:P * nk], bank("pt", l, i)[:, 0:P * nk], ACT.Copy).then_inc(*drain("pt", l, i))

            def attended(i):
                kind, h, q, nk = units[i]
                qs = slice(P * q, P * q + P)
                act.wait_ge(*full("av", l, i))
                if kind == "diff":
                    A(YB[:, h, qs], bank("av", l, i)[:, 0:P], ACT.Copy).then_inc(*drain("av", l, i))
                else:
                    r = slice(64 * (h % 2), 64 * (h % 2) + 64)
                    A(YC[r, h // 2, qs], bank("av", l, i)[r, 0:P], ACT.Copy).then_inc(*drain("av", l, i))

            exponentials(0)
            exponentials(1)
            for i in range(len(units)):
                if i >= 1:
                    attended(i - 1)
                evacuate(i)
                if i + 2 < len(units):
                    exponentials(i + 2)
            attended(len(units) - 1)
            for m in range(3):
                weights_rounded(b0 + 18 + m)
            nq = 4 if l == 0 else 2

            def heads_squared(h):
                act.wait_ge(*drained("av", l, nq * h + nq - 1))
                squares(("bn", l, h), lambda k: YB[:, h, o], 1, o)

            heads_squared(0)

            for b in range(15):
                lo = l == 1 and (b < 4 or b == 14)
                tk = LAT if lo else slice(0, T)
                act.wait_ge(*full("za", l, b))
                if b == 0:
                    act.wait_ge(*when("mu0", l))
                A(ZS[:, b, tk], bank("za", l, b)[:, 0:tk.stop - tk.start], ACT.Copy, scale=mu0[:, b:b + 1]).then_inc(*mark("zs_own", l, b))
                if b + 3 < 15:
                    weights_rounded(b0 + 21 + b)
                if b in BN_AT:
                    h = BN_AT.index(b)
                    root(("bn", l, h), o)
                    if h + 1 < 4:
                        heads_squared(h + 1)
                if b - 1 in KK_AT:
                    p = KK_AT.index(b - 1)
                    act.wait_ge(*full("kkn", l, p))
                    A(RK[:, p, :], bank("kkn", l, p)[:, :], ACT.Sqrt).then_inc(*drain("kkn", l, p))
                if b + 1 in KK_AT:
                    p = KK_AT.index(b + 1)
                    act.wait_ge(*when("kkraw", l, p))
                    A(SQK[:, p, :], KK[:, p, :], ACT.Square).then_inc(*mark("kk_squared", l, p))
            act.wait_ge(*drained("za", l, 12))
            A(ZS[:, 12, :], ZS[:, 12, :], ACT.Tanh).then_inc(*mark("tanh", l))
            act.wait_ge(*drained("za", l, 14))
            A(ZS[:, 14, o], ZS[:, 14, o], ACT.Sigmoid).then_inc(*mark("gd", l))
            groups, gate_half = gate_groups(l)

            def gates_rounded(i):
                if i < len(groups):
                    for half in range(2):
                        weights_rounded(gate_half + 2 * i + half)

            gates_rounded(0)
            for c in range(NCH):
                act.wait_ge(*full("vtok", l, c))
                if c >= 4:
                    act.wait_ge(*when(f"v_spilled{c % 4}", l, c - 4))
                A(VT[0:C, c % 4, :], bank("vtok", l, c)[0:C, :], ACT.Copy).then_inc(*drain("vtok", l, c))

            def gates(i):
                d, p = i // 4, i % 4
                act.wait_ge(*full("lora_w", l, i))
                if i:
                    act.wait_ge(*when("scanned", l, i - 1))
                else:
                    act.wait_ge(*when("w65_zero", l))
                wv = W65.rearrange("p (h c t) -> p h c t", h=2, t=C + 1)
                for h in range(2):
                    ins = A(wv[:, h, :, 1:C + 1], directed(bank("lora_w", l, i)[:, :], d)[:, h], ACT.Sigmoid,
                            bias=par[:, l, W0 + i:W0 + i + 1])
                ins.then_inc(*drain("lora_w", l, i))
                act.wait_ge(*full("lora_a", l, i))
                if i:
                    act.wait_ge(*when("b", l, i - 1))
                A(AI, bank("lora_a", l, i)[:, :], ACT.Sigmoid, bias=par[:, l, A0C + i:A0C + i + 1]).then_inc(*drain("lora_a", l, i))

            def decays(i):
                act.wait_ge(*when("scanned", l, i))
                A(RI.rearrange("p (c t) -> p c t", t=C), E65.rearrange("p (c t) -> p c t", t=C + 1)[:, :, 1:C + 1],
                  ACT.Exp, scale=DECAY).then_inc(*mark("undecayed", l, i))
                act.wait_ge(*when("undecayed", l, i))
                A(E65, E65, ACT.Exp, scale=-DECAY).then_inc(*mark("decayed", l, i))

            def turned(i):
                for g in range(2):
                    act.wait_ge(*full("bkt", l, i, g))
                    if g == 0 and i >= 2:
                        act.wait_ge(*when(f"b_spilled{i % 2}", l, i - 2))
                    A(BKT[:, i % 2, 4 * g:4 * g + 4, :], bank("bkt", l, i, g)[:, :].rearrange("p (c n) -> p c n", c=4), ACT.Copy).then_inc(*drain("bkt", l, i, g))

            def gate12(d):
                for g in range(2):
                    act.wait_ge(*full("g12", l, d, g))
                    if d:
                        act.wait_ge(*when("m12_out", l, d - 1))
                    A(GS[:, g, 0:no], bank("g12", l, d, g)[:, 0:no], ACT.Sigmoid).then_inc(*drain("g12", l, d, g))

            def spills(i):
                act.wait_ge(*when("ar", l, i))
                act.dma_start(r_dram[:, :, i, :].rearrange("c p n -> p c n"), AR[:, i % 2]).then_inc(*dma(f"r_spilled{i % 2}", l, i))
                for g in range(2):
                    act.wait_ge(*drained("bkt", l, i, g))
                act.dma_start(b_dram[:, :, i, :].rearrange("c p n -> p c n"), BKT[:, i % 2]).then_inc(*dma(f"b_spilled{i % 2}", l, i))
                for g in range(4):
                    hh, half = g % 2, g // 2
                    act.wait_ge(*drained("A", l, i, g))
                    act.dma_start(a_dram[4 * half:4 * half + 4, :, 2 * i + hh, :].rearrange("c p n -> p c n"),
                                  AS[:, g]).then_inc(*dma(f"a_spilled{g}", l, i))

            def merged12_out(d):
                act.wait_ge(*when("m12", l, d))
                act.dma_start(m12_dram[:, d, 0:no], GS[:, 0, 0:no]).then_inc(*dma("m12_out", l, d))

            def beside_scores(j):
                if j < 4:
                    gate12(j)
                    gates_rounded(j + 1)
                elif l == DEPTH - 1 and j < 8:
                    for d in (2 * j - 8, 2 * j - 7):
                        act.wait_ge(*full("g0", l, d))
                        A(M[:, d, 0:no], bank("g0", l, d)[:, 0:no], ACT.Sigmoid).then_inc(*drain("g0", l, d))
                    gates_rounded(j + 1)

            gates(0)
            decays(0)
            gates(1)
            decays(1)
            beside_scores(0)
            for i in range(8):
                if i + 2 < 8:
                    gates(i + 2)
                turned(i)
                spills(i)
                if i < 4:
                    merged12_out(i)
                if i + 2 < 8:
                    decays(i + 2)
                beside_scores(i + 1)
            for g in range(4):
                act.wait_ge(*when(f"a_spilled{g}", l, 7))
            for i in (6, 7):
                act.wait_ge(*when(f"b_spilled{i % 2}", l, i))
            for c in range(NCH):
                act.dma_start(NB[16 * c:16 * c + 16], a_dram[c, 0:C, :, 0:C].rearrange("s u t -> u s t")).then_inc(*dma("nb_in", l))
            for d in range(4, 8):
                gate12(d)
                gates_rounded(d + 1 + (4 if l == DEPTH - 1 else 0))
                merged12_out(d)
            act.wait_ge(*when("m12_out", l, 7))
            act.wait_ge(*full("w12", l, 7, 1))
            act.dma_start(M[:, :, o], m12_dram[:, :, 0:no]).then_inc(*dma("m12_back", l))
            modulation(l, 1, (0, 1) if l else (1,))
            modulation(l, 2)
            modulation_back(l, 1)
            if l + 1 < DEPTH:
                modulation(l + 1, 0)
            modulation_back(l, 2)
            if l + 1 < DEPTH:
                modulation_back(l + 1, 0)
            for c in range(NCH):
                for g in range(2):
                    act.wait_ge(*full("U", l, c, g))
                    if c:
                        act.wait_ge(*full("SA", l, c - 1, g))
                    A(R[0:C, 4 * g:4 * g + 4, :], bank("U", l, c, g)[0:C, :].rearrange("p (i n) -> p i n", i=4), ACT.Copy).then_inc(*drain("U", l, c, g))
                if not (l and c < 4):
                    for g in range(2):
                        act.wait_ge(*full("Y", l, c, g))
                        rc = c if g == 0 else 4 * (c // 4) + 3 - c % 4
                        dst = Y[:, g, :, C * rc:C * rc + C]
                        if g:
                            dst = dst[:, :, ::-1]
                        A(dst, bank("Y", l, c, g)[:, 0:4 * C].rearrange("p (i t) -> p i t", i=4), ACT.Copy).then_inc(*drain("Y", l, c, g))
                if l < DEPTH - 1 and 2 <= c < 6:
                    if c == 2:
                        act.wait_ge(*when("inverse_out_first", l))
                        act.wait_ge(*when("inverse_out", l))
                    weights_rounded(split_at[(l, ("G0", c - 2), 0)])

            def gate0(d):
                if l < DEPTH - 1:
                    act.wait_ge(*full("g0", l, d))
                    if d >= 4:
                        act.wait_ge(*when("merged", l, d - 4))
                    A(GATE[:, d % 4, 0:no], bank("g0", l, d)[:, 0:no], ACT.Sigmoid).then_inc(*drain("g0", l, d))

            def merge_rounded(d):
                act.wait_ge(*when("merged", l, d))
                A(m_hi[:, d, o], M[:, d, o], ACT.Copy).then_inc(*mark("m_hi", l, d))

            for p in range(4):
                act.wait_ge(*drained("gmean", l, p))
                A(RO[0][:, p, o], Y[:, 0, p, o], ACT.Square).then_inc(*mark("ysq", l, p))
            gate0(0)
            if l < DEPTH - 1:
                weights_rounded(split_at[(l, ("G0", 4), 0)])
            for p in range(4):
                act.wait_ge(*drained("gvar", l, p))
                A(RO[1][:, p, o], RO[1][:, p, o], ACT.Sqrt).then_inc(*mark("groot", l, p))
            for d in range(1, 8):
                gate0(d)
                if l < DEPTH - 1 and 2 <= d < 5:
                    weights_rounded(split_at[(l, ("G0", d + 3), 0)])
                if l < DEPTH - 1 and d >= 4:
                    merge_rounded(d - 4)
            o0 = split_at[(l, ("O", 0), 0)]
            for d in range(4 if l < DEPTH - 1 else 0, 8):
                merge_rounded(d)
                if d in (5, 6):
                    for m in range(2):
                        weights_rounded(o0 + 2 * (d - 5) + m)
            for m in range(4, 8):
                weights_rounded(o0 + m)
            m0 = split_at[(l, ("FG", 0), 0)]
            for m in range(m0, m0 + 4):
                weights_rounded(m)
            for k in range(KT):
                act.wait_ge(*drained("wo", l, k))
            squares(("n2", l), lambda k: X2[:, k, o], KT, o, SQH)
            root(("n2", l), o)
            for k in range(KT):
                for s in sides(l):
                    tk = slice(HALF * s, HALF * s + HALF)
                    act.wait_ge(*when("h2_scaled", l, k, s))
                    A(h_hi[:, k, tk], h_raw[:, k, tk], ACT.Identity, bias=mods[:, 24 + k, s:s + 1]).then_inc(*mark("h2_hi", l, k, s))
            for f in range(FT):
                act.wait_ge(*full("fg", l, f))
                A(f_raw[:, f, o], bank("fg", l, f)[:, 0:no], ACT.Sigmoid).then_inc(*mark("fsg", l, f))
                if f:
                    act.wait_ge(*drained("fu", l, f - 1))
                    A(f_hi(f - 1, o), f_raw[:, f - 1, o], ACT.Copy).then_inc(*mark("f_hi", l, f - 1))
                weights_rounded(m0 + 2 * f + 4)
                weights_rounded(m0 + 2 * f + 1 + 4)
            act.wait_ge(*drained("fu", l, FT - 1))
            A(f_hi(FT - 1, o), f_raw[:, FT - 1, o], ACT.Copy).then_inc(*mark("f_hi", l, FT - 1))
            for m in range(m0 + 2 * FT + 4, m0 + 2 * FT + 24):
                weights_rounded(m)
        for k in range(KT):
            act.wait_ge(*drained("fd", DEPTH - 1, k))
        squares(("nf",), lambda k: X[:, k, LAT], KT, LAT, SQH)
        root(("nf",), LAT)
        for i in range(2):
            for h in range(2):
                act.wait_ge(*full("xout", i, h))
                A(TOKS[:, i, 512 * h:512 * h + 512], bank("xout", i, h)[:, :], ACT.Copy).then_inc(*drain("xout", i, h))

    @block.vector
    def _(dve):
        V = nc.vector

        def step(ins):
            ins.then_inc(*mark("dve_step", plan.count.get("dve_step", 0)))
            dve.wait_ge(sem_of("dve_step"), plan.count["dve_step"])

        def weights_rest(m):
            raw, hi, n = half_views(m, ring)
            lo, _, _ = half_views(m, w_lo)
            dve.wait_ge(*when("w_hi", m))
            V.tensor_tensor(lo, raw, hi.bitcast(F32), ALU.subtract).then_inc(*mark(rest_name(m), m))

        def mean_square(key, n, toks):
            dve.wait_ge(*full(*key))
            ps = bank(*key)
            V.tensor_scalar(RS[:, toks], ps[:, 0:toks.stop - toks.start], 1.0 / n, EPS, ALU.mult, ALU.add).then_inc(*drain(*key))
            dve.wait_ge(*when("root", *key))
            step(V.reciprocal(RS[:, toks], RS[:, toks]))

        def modulation_columns(l, part):
            mods = mods_all[:, l]
            js = slice(16 * part, 16 * part + 16)
            dve.wait_ge(*full("modt", l, part))
            V.tensor_tensor(mods[:, js, :], bank("modt", l, part)[:, 0:32].rearrange("p (s j) -> p j s", s=2),
                            par2[:, l, ADAB + 16 * part:ADAB + 16 * part + 16].unsqueeze(2).broadcast_to([P, 16, 2]), ALU.add).then_inc(*drain("modt", l, part))
            if part != 1:
                n, sc, g = (0, 8, N1) if part == 0 else (1, 32, N2)
                dve.wait_ge(*drained("modt", l, part))
                step(V.scalar_tensor_tensor(gsc_all[:, l, n], mods[:, sc:sc + 8, :], 1.0,
                                            par[:, l, g:g + 8].unsqueeze(2).broadcast_to([P, 8, 2]), ALU.add, ALU.mult))

        dve.wait_ge(*when("csig", 1))
        V.tensor_tensor(csil[:, :, 0], csil[:, :, 0], par2[:, 0, CCTX:CCTX + 8], ALU.mult)
        V.tensor_tensor(csil[:, :, 1], csil[:, :, 1], par2[:, 0, CVEC:CVEC + 8], ALU.mult).then_inc(*mark("csil"))
        for l in range(DEPTH):
            lam, lamv = lam_all[:, l], lamv_all[:, l]
            dve.wait_ge(*when(f"lamv_{l}"))
            for j in range(2):
                step(V.tensor_tensor(lamv[:, 128 * j:128 * j + 64], lamv[:, 128 * j:128 * j + 64], lamv[:, 128 * j + 64:128 * j + 128], ALU.mult))
                ins = V.reduce_sum(lam[:, j:j + 1], lamv[:, 128 * j:128 * j + 64], AX.X)
            ins.then_inc(*mark("lam_dots", l))
        for l in range(DEPTH):
            dve.wait_ge(*drained("par", l))
        modulation_columns(0, 0)

        for l in range(DEPTH):
            o = outs(l)
            no = o.stop - o.start
            lam_init = 0.8 - 0.6 * math.exp(-0.3 * l)
            pcol, mods, gsc, lam = par[:, l], mods_all[:, l], gsc_all[:, l], lam_all[:, l]
            dve.wait_ge(*when("lam_exp", l))
            step(V.tensor_tensor(lam[:, 2:3], lam[:, 0:1], lam[:, 1:2], ALU.subtract))
            step(V.tensor_scalar(lam[:, 2:3], lam[:, 2:3], lam_init, None, ALU.add))
            V.tensor_scalar(subg[:, :], pcol[:, SUBG:SUBG + 1], 1.0 - lam_init, None, ALU.mult)
            step(V.tensor_tensor(mu0[:, :], pcol[:, MU:MU + 15], pcol[:, MU + 15:MU + 30], ALU.add))
            V.tensor_scalar(mu0[:, :], mu0[:, :], -1.0, 1.0, ALU.mult, ALU.add).then_inc(*mark("mu0", l))
            step(V.tensor_scalar(kaneg[:, :], pcol[:, KAC:KAC + 4], -1.0, 1.0, ALU.mult, ALU.add))
            b0 = split_at[(l, ("B", 0), 0)]
            for m in range(3):
                weights_rest(b0 + m)
            mean_square(("n1", l), D, slice(0, T))
            dve.wait_ge(*when("x_spilled", l))

            def modulated(name, x, n, shift, halves):
                def rest(k):
                    for s in halves:
                        tk = slice(HALF * s, HALF * s + HALF)
                        dve.wait_ge(*when(f"{name}_hi", l, k, s))
                        V.scalar_tensor_tensor(h_lo[:, k, tk], h_raw[:, k, tk], mods[:, shift + k, s:s + 1],
                                               h_hi[:, k, tk].bitcast(F32), ALU.add, ALU.subtract).then_inc(*mark(name, l, k))

                for k in range(KT):
                    for s in halves:
                        tk = slice(HALF * s, HALF * s + HALF)
                        V.scalar_tensor_tensor(h_raw[:, k, tk], x[:, k, tk], gsc[:, n, k, s:s + 1], RS[:, tk],
                                               ALU.mult, ALU.mult).then_inc(*mark(f"{name}_scaled", l, k, s))
                    if k:
                        rest(k - 1)
                rest(KT - 1)

            modulated("h1", X, 0, 0, (0, 1))

            def rope(raw, x, cosc, sinc, rows, name, key, n):
                dve.wait_ge(*full(*raw))
                r = ROT[rows, n % 2, :]
                V.tensor_tensor(r, bank(*raw)[rows, 0:HALF], cst[rows, sinc:sinc + HALF], ALU.mult).then_inc(*drain(*raw))
                step(V.tensor_tensor(x, x, cst[rows, cosc:cosc + HALF], ALU.mult))
                dve.wait_ge(*drained(*raw))
                V.tensor_tensor(x, x, r, ALU.add).then_inc(*mark(name, *key))

            allp = slice(0, P)
            q32 = slice(64, 96)
            weights_rest(b0 + 3)
            for b in range(8):
                weights_rest(b0 + b + 4)
                if b == 7:
                    weights_rest(b0 + 12)
                    weights_rest(b0 + 13)
                rope(("qkrot", l, b), QK[:, b, LAT], COSB, SINB, allp, "qk_ready", (l, b), b)
            for m in range(14, 18):
                weights_rest(b0 + m)
            mean_square(("qn", l), 384, o)
            for k in range(3):
                V.scalar_tensor_tensor(ZC[:, k, o], ZC[:, k, o], pcol[:, QNG + k:QNG + k + 1], RS[:, o], ALU.mult, ALU.mult).then_inc(*mark("qnorm", l, k))
            dve.wait_ge(*when("qnorm", l, 2))
            mean_square(("kvn", l), 256, slice(0, T))
            for k in range(2):
                V.scalar_tensor_tensor(ZC[:, 3 + k, :], ZC[:, 3 + k, :], pcol[:, KVG + k:KVG + k + 1], RS, ALU.mult, ALU.mult).then_inc(*mark("kvnorm", l, k))
            dve.wait_ge(*when("kvnorm", l, 1))
            rope(("krot", l), ZC[q32, 5, LAT], COSC, SINC, q32, "krope", (l,), 0)
            dve.wait_ge(*when("krope", l))
            V.tensor_copy(MK[q32, :, :], ZC[q32, 5:6, :].broadcast_to([32, 8, T])).then_inc(*mark("mk_rope", l))
            for h in range(8):
                rope(("mqrot", l, h), MQ[q32, h, LAT], COSC, SINC, q32, "mq_ready", (l, h), h)

            units = attention_units(l)

            def maxima(i):
                kind, h, q, nk = units[i]
                scale = DIFF_SCALE if kind == "diff" else MLA_SCALE
                for c in range(2 if kind == "diff" else 1):
                    dve.wait_ge(*full("sc", l, i, c))
                    step(V.reduce_max(smax[:, c, i:i + 1], bank("sc", l, i, c)[:, 0:P * nk], AX.X))
                    V.tensor_scalar(smax[:, c, i:i + 1], smax[:, c, i:i + 1], -scale, None, ALU.mult).then_inc(*mark("negmax", l, i, c))

            def normalised(i):
                kind, h, q, nk = units[i]
                n = P * nk
                nc_ = 2 if kind == "diff" else 1
                for c in range(nc_):
                    dve.wait_ge(*drained("sc", l, i, c))
                step(V.reciprocal(rsum[:, 0:nc_, i:i + 1], ssum[:, 0:nc_, i:i + 1]))
                if kind == "diff":
                    step(V.tensor_scalar(PR[:, i % 3, 1, 0:n], PR[:, i % 3, 1, 0:n], rsum[:, 1, i:i + 1], lam[:, 2:3], ALU.mult, ALU.mult))
                    V.scalar_tensor_tensor(PR[:, i % 3, 0, 0:n], PR[:, i % 3, 0, 0:n], rsum[:, 0, i:i + 1], PR[:, i % 3, 1, 0:n],
                                           ALU.mult, ALU.subtract).then_inc(*mark("probs", l, i))
                else:
                    V.tensor_scalar(PR[:, i % 3, 0, 0:n], PR[:, i % 3, 0, 0:n], rsum[:, 0, i:i + 1], None, ALU.mult).then_inc(*mark("probs", l, i))

            maxima(0)
            maxima(1)
            for i in range(len(units)):
                normalised(i)
                if i + 2 < len(units):
                    maxima(i + 2)
            for m in range(18, 21):
                weights_rest(b0 + m)

            for b in range(15):
                lo = l == 1 and (b < 4 or b == 14)
                ps = bank("za", l, b)
                dve.wait_ge(*when("zs_own", l, b))
                if lo:
                    z, s = ps[:, 0:HALF].unsqueeze(1), ZS[:, b, LAT].unsqueeze(1)
                else:
                    z, s = ps[:, :].rearrange("p (h t) -> p h t", h=2), ZS[:, b, :].rearrange("p (h t) -> p h t", h=2)
                step(V.scalar_tensor_tensor(s[:, :, 1:HALF], z[:, :, 0:HALF - 1], pcol[:, MU + b:MU + b + 1], s[:, :, 1:HALF], ALU.mult, ALU.add))
                V.scalar_tensor_tensor(s[:, :, 0:HALF - 1], z[:, :, 1:HALF], pcol[:, MU + 15 + b:MU + 16 + b], s[:, :, 0:HALF - 1],
                                       ALU.mult, ALU.add).then_inc(*drain("za", l, b))
                if b + 3 < 15:
                    weights_rest(b0 + 21 + b)
                if b in BN_AT:
                    h = BN_AT.index(b)
                    mean_square(("bn", l, h), P, o)
                    V.scalar_tensor_tensor(YB[:, h, o], YB[:, h, o], subg[:, 0:1], RS[:, o], ALU.mult, ALU.mult).then_inc(*mark("yb", l, h))
                    dve.wait_ge(*when("yb", l, h))
                if b + 2 in KK_AT:
                    p = KK_AT.index(b + 2)
                    dve.wait_ge(*drained("za", l, 4 + p))
                    V.tensor_scalar(KK[:, p, :], ZS[:, 4 + p, :], pcol[:, KKC + p:KKC + p + 1], None, ALU.mult).then_inc(*mark("kkraw", l, p))
                if b - 2 in KK_AT:
                    p = KK_AT.index(b - 2)
                    dve.wait_ge(*drained("kkn", l, p))
                    step(V.tensor_scalar(RK[:, p, :], RK[:, p, :], 1e-12, None, ALU.max))
                    step(V.reciprocal(RK[:, p, :], RK[:, p, :]))
                    V.tensor_tensor(KK[:, p, :], KK[:, p, :], RK[:, p, :], ALU.mult).then_inc(*mark("kk", l, p))
            groups, gate_half = gate_groups(l)

            def gates_rest(i):
                if i < len(groups):
                    for half in range(2):
                        weights_rest(gate_half + 2 * i + half)

            gates_rest(0)
            dve.wait_ge(*when("kk", l, 3))
            w65v = W65.rearrange("p (c t) -> p c t", t=C + 1)
            V.memset(w65v[:, :, 0:1], 0.0).then_inc(*mark("w65_zero", l))

            def scaled(i):
                d, p = i // 4, i % 4
                k, r, kk = ZS[:, 4 + p, :], ZS[:, p, :], KK[:, p, :]
                ar = AR[:, i % 2]
                e = E65.rearrange("p (c t) -> p c t", t=C + 1)
                dve.wait_ge(*drained("lora_w", l, i))
                if i:
                    dve.wait_ge(*when("bk", l, i - 1))
                V.tensor_tensor_scan(E65, cst[:, INSIDE:INSIDE + NCH * (C + 1)], W65, 0.0, ALU.mult, ALU.add).then_inc(*mark("scanned", l, i))
                dve.wait_ge(*drained("lora_a", l, i))
                if i:
                    dve.wait_ge(*when("bk", l, i - 1))
                step(V.tensor_scalar(TA, AI, pcol[:, KAC + p:KAC + p + 1], kaneg[:, p:p + 1], ALU.mult, ALU.add))
                step(V.tensor_tensor(TA, TA, k, ALU.mult))
                V.tensor_tensor(TB, kk, AI, ALU.mult).then_inc(*mark("b", l, i))
                if d == 0:
                    V.scalar_tensor_tensor(BV[:, p, o], TA[:, o], pcol[:, RKC + p:RKC + p + 1], r[:, o], ALU.mult, ALU.mult)
                else:
                    step(V.scalar_tensor_tensor(GT[:, o], TA[:, o], pcol[:, RKC + p:RKC + p + 1], r[:, o], ALU.mult, ALU.mult))
                    V.tensor_tensor(BV[:, p, o], BV[:, p, o], GT[:, o], ALU.add).then_inc(*mark("rkk", l, p))
                dve.wait_ge(*when("decayed", l, i))
                if i >= 2:
                    dve.wait_ge(*when(f"r_spilled{i % 2}", l, i - 2))
                V.tensor_copy(dend[:, i, :], e[:, :, C])
                for h in range(2):
                    cs = slice(4 * h, 4 * h + 4)
                    V.scalar_tensor_tensor(ar[:, cs, 0:C], directed(kk, d)[:, h], -1.0, e[:, cs, 0:C], ALU.mult, ALU.mult)
                    if l and h == 0:
                        ins = V.memset(ar[:, cs, C:P], 0.0)
                    else:
                        ins = V.tensor_tensor(ar[:, cs, C:P], directed(r, d)[:, h], e[:, cs, 1:C + 1], ALU.mult)
                ins.then_inc(*mark("ar", l, i))

            def scaled_back(i):
                d = i // 4
                r3 = RI.rearrange("p (c t) -> p c t", t=C)
                dve.wait_ge(*when("b", l, i))
                if i:
                    dve.wait_ge(*full("A", l, i - 1, 3))
                    dve.wait_ge(*when("bh", l, i - 1))
                else:
                    for c in range(4, NCH):
                        dve.wait_ge(*when(f"v_spilled{c % 4}", l, c))
                for h in range(2):
                    cs = slice(4 * h, 4 * h + 4)
                    V.tensor_tensor(BK[:, cs, 0:C], directed(TB, d)[:, h], r3[:, cs, :], ALU.mult)
                    ins = V.tensor_tensor(BK[:, cs, C:P], directed(TA, d)[:, h], r3[:, cs, :], ALU.mult)
                ins.then_inc(*mark("bk", l, i))

            def masked(i):
                for g in range(4):
                    dve.wait_ge(*full("A", l, i, g))
                    if i:
                        dve.wait_ge(*when(f"a_spilled{g}", l, i - 1))
                    V.tensor_tensor(AS[:, g], bank("A", l, i, g)[:, :].rearrange("p (c n) -> p c n", c=4),
                                    cst[:, MASK:MASK + P].unsqueeze(1).broadcast_to([P, 4, P]), ALU.mult).then_inc(*drain("A", l, i, g))

            def merged12(d):
                for g in range(2):
                    dve.wait_ge(*full("w12", l, d, g))
                    dve.wait_ge(*drained("g12", l, d, g))
                    V.tensor_tensor(GS[:, g, 0:no], bank("w12", l, d, g)[:, 0:no], GS[:, g, 0:no], ALU.mult).then_inc(*drain("w12", l, d, g))
                for g in range(2):
                    dve.wait_ge(*drained("w12", l, d, g))
                V.tensor_tensor(GS[:, 0, 0:no], GS[:, 0, 0:no], GS[:, 1, 0:no], ALU.add).then_inc(*mark("m12", l, d))

            scaled(0)
            scaled_back(0)
            for i in range(8):
                if i + 1 < 8:
                    scaled(i + 1)
                if i < 4:
                    merged12(i)
                if i + 1 < 8:
                    scaled_back(i + 1)
                masked(i)
            for p in range(4):
                dve.wait_ge(*full("bonus", l, p))
                V.tensor_tensor(BV[:, p, o], bank("bonus", l, p)[:, 0:no], ZS[:, 8 + p, o], ALU.mult).then_inc(*drain("bonus", l, p))

            pieces = (("weights", 5), ("merge", 4), ("weights", 6), ("merge", 5), ("weights", 7), ("merge", 6), ("merge", 7))
            at = (0, 0, 10, 14, 21, 25, 35) if l == 0 else (0, 0, 6, 10, 14, 18, 22)

            def beside_inverse(s):
                for (kind, d), when_due in zip(pieces, at):
                    if when_due == s and kind == "weights":
                        gates_rest(d + (4 if l == DEPTH - 1 else 0))
                    elif when_due == s:
                        merged12(d)

            beside_inverse(0)
            dve.wait_ge(*when("nb_in", l))
            for i in (6, 7):
                dve.wait_ge(*when(f"r_spilled{i % 2}", l, i))
            for s in range(1, CSPLIT - 1):
                n = CSPLIT - 1 - s
                tmp = NT[:, 0:s * n].rearrange("p (j t) -> p j t", t=n)
                step(V.tensor_tensor(tmp, NB[:, 0:s, s:s + 1].broadcast_to([P, s, n]), NB[:, s:s + 1, s + 1:CSPLIT].broadcast_to([P, s, n]), ALU.mult))
                V.tensor_tensor(NB[:, 0:s, s + 1:CSPLIT], NB[:, 0:s, s + 1:CSPLIT], tmp, ALU.add).then_inc(*mark("inverse_col", l, s + 1))
                dve.wait_ge(*when("inverse_col", l, s + 1))
                beside_inverse(s)
            dve.wait_ge(*when("inverse_right", l, LATE - 1))
            for s in range(LATE, C - 1):
                t0 = max(s + 1, CSPLIT)
                n = C - t0
                tmp = NT[:, 0:s * n].rearrange("p (j t) -> p j t", t=n)
                step(V.tensor_tensor(tmp, NB[:, 0:s, s:s + 1].broadcast_to([P, s, n]), NB[:, s:s + 1, t0:C].broadcast_to([P, s, n]), ALU.mult))
                step(V.tensor_tensor(NB[:, 0:s, t0:C], NB[:, 0:s, t0:C], tmp, ALU.add))
            V.memset(NB.rearrange("p s t -> p (s t)")[:, 0:C * C:C + 1], 1.0).then_inc(*mark("inverted", l))
            V.memset(S, 0.0).then_inc(*mark("state_zero", l))
            dve.wait_ge(*when("state_zero", l))
            for c in range(NCH):
                b = c % 2
                for g in range(2):
                    dve.wait_ge(*full("SA", l, c, g))
                    dve.wait_ge(*when(f"chunk_in{b}", l, c))
                    V.tensor_copy(cV[0:C, b, g, :], bank("SA", l, c, g)[0:C, :]).then_inc(*drain("SA", l, c, g))
                for g in range(2):
                    if c:
                        dve.wait_ge(*drained("S", l, c - 1, g))
                    dve.wait_ge(*full("S", l, c, g))
                    ps = bank("S", l, c, g)
                    for ii in range(4):
                        i = 4 * g + ii
                        for hh in range(2):
                            r = slice(C * hh, C * hh + C)
                            ins = V.scalar_tensor_tensor(S[r, i, r], S[r, i, r], dend[r, i, c:c + 1],
                                                         ps[r, P * ii + C * hh:P * ii + C * hh + C], ALU.mult, ALU.add)
                    ins.then_inc(*drain("S", l, c, g))
                if l < DEPTH - 1 and 3 <= c < 7:
                    weights_rest(split_at[(l, ("G0", c - 3), 0)])

            modulation_columns(l, 1)
            modulation_columns(l, 2)
            if l + 1 < DEPTH:
                modulation_columns(l + 1, 0)
            for p in range(4):
                if p == 0:
                    for g in range(2):
                        dve.wait_ge(*drained("Y", l, NCH - 1, g))
                V.tensor_tensor(Y[:, 0, p, o], Y[:, 0, p, o], Y[:, 1, p, o], ALU.add).then_inc(*mark("ysum", l, p))
            for p in range(4):
                dve.wait_ge(*full("gmean", l, p))
                V.scalar_tensor_tensor(Y[:, 0, p, o], bank("gmean", l, p)[:, 0:no], -1.0 / 64, Y[:, 0, p, o], ALU.mult, ALU.add).then_inc(*drain("gmean", l, p))
            for p in range(4):
                dve.wait_ge(*full("gvar", l, p))
                V.tensor_scalar(RO[1][:, p, o], bank("gvar", l, p)[:, 0:no], 1.0 / 64, GN_EPS, ALU.mult, ALU.add).then_inc(*drain("gvar", l, p))
            if l < DEPTH - 1:
                weights_rest(split_at[(l, ("G0", 4), 0)])
            for p in range(4):
                dve.wait_ge(*when("groot", l, p))
                step(V.reciprocal(RO[1][:, p, o], RO[1][:, p, o]))
                step(V.scalar_tensor_tensor(Y[:, 0, p, o], Y[:, 0, p, o], pcol[:, LNW + p:LNW + p + 1], RO[1][:, p, o], ALU.mult, ALU.mult))
                step(V.scalar_tensor_tensor(Y[:, 0, p, o], Y[:, 0, p, o], pcol[:, LNB + p:LNB + p + 1], BV[:, p, o], ALU.add, ALU.add))
                dve.wait_ge(*full("lora_g", l, p))
                V.tensor_tensor(YA[:, p, o], bank("lora_g", l, p)[:, 0:no], Y[:, 0, p, o], ALU.mult).then_inc(*drain("lora_g", l, p))
            def merge_rest(d):
                dve.wait_ge(*when("m_hi", l, d))
                V.tensor_tensor(m_lo[:, d, o], M[:, d, o], m_hi[:, d, o].bitcast(F32), ALU.subtract).then_inc(*mark("m_rest", l, d))

            o0 = split_at[(l, ("O", 0), 0)]
            dve.wait_ge(*when("m12_back", l))
            for d in range(8):
                if l < DEPTH - 1 and d + 5 < 8:
                    weights_rest(split_at[(l, ("G0", d + 5), 0)])
                dve.wait_ge(*full("w0", l, d))
                dve.wait_ge(*drained("g0", l, d))
                gate = GATE[:, d % 4, 0:no] if l < DEPTH - 1 else M[:, d, 0:no]
                V.tensor_tensor(gate, bank("w0", l, d)[:, 0:no], gate, ALU.mult).then_inc(*drain("w0", l, d))
                dve.wait_ge(*drained("w0", l, d))
                V.tensor_tensor(M[:, d, o], M[:, d, o], gate, ALU.add).then_inc(*mark("merged", l, d))
                if d:
                    merge_rest(d - 1)
                if d >= 6:
                    for m in range(2):
                        weights_rest(o0 + 2 * (d - 6) + m)
            merge_rest(7)
            dve.wait_ge(*when("x_back", l))
            for k in range(KT):
                dve.wait_ge(*full("wo", l, k))
                for s in sides(l):
                    tk = slice(HALF * s, HALF * s + HALF)
                    ins = V.scalar_tensor_tensor(X2[:, k, tk], bank("wo", l, k)[:, tk.start - o.start:tk.stop - o.start],
                                                 mods[:, 16 + k, s:s + 1], X2[:, k, tk], ALU.mult, ALU.add)
                ins.then_inc(*drain("wo", l, k))
                if k < 4:
                    weights_rest(o0 + k + 4)
            m0 = split_at[(l, ("FG", 0), 0)]
            for m in range(m0, m0 + 4):
                weights_rest(m)
            mean_square(("n2", l), D, o)

            modulated("h2", X2, 1, 24, sides(l))

            def hidden_rest(f):
                dve.wait_ge(*when("f_hi", l, f))
                V.tensor_tensor(f_lo[:, f, o], f_raw[:, f, o], f_hi(f, o).bitcast(F32), ALU.subtract).then_inc(*mark("ffn_hidden", l, f))

            for f in range(FT):
                dve.wait_ge(*when("fsg", l, f))
                V.tensor_tensor(f_raw[:, f, o], bank("fg", l, f)[:, 0:no], f_raw[:, f, o], ALU.mult).then_inc(*drain("fg", l, f))
                weights_rest(m0 + 2 * f + 4)
                if f:
                    hidden_rest(f - 1)
                dve.wait_ge(*drained("fg", l, f))
                dve.wait_ge(*full("fu", l, f))
                V.tensor_tensor(f_raw[:, f, o], bank("fu", l, f)[:, 0:no], f_raw[:, f, o], ALU.mult).then_inc(*drain("fu", l, f))
                weights_rest(m0 + 2 * f + 1 + 4)
            hidden_rest(FT - 1)
            for k in range(KT):
                if k % 2 == 0:
                    m1 = m0 + 2 * FT + 4 + 3 * k
                    for m in range(m1, min(m1 + 6, m0 + 2 * FT + 24)):
                        weights_rest(m)
                dve.wait_ge(*full("fd", l, k))
                for s in sides(l):
                    tk = slice(HALF * s, HALF * s + HALF)
                    ins = V.scalar_tensor_tensor(X[:, k, tk], bank("fd", l, k)[:, tk.start - o.start:tk.stop - o.start],
                                                 mods[:, 40 + k, s:s + 1], X2[:, k, tk], ALU.mult, ALU.add)
                ins.then_inc(*drain("fd", l, k))
        mean_square(("nf",), D, LAT)
        for k in range(KT):
            V.scalar_tensor_tensor(H[:, k, LAT], X[:, k, LAT], par2[:, DEPTH - 1, FING + k:FING + k + 1], RS[:, LAT], ALU.mult, ALU.mult).then_inc(*mark("final", k))


_NAMES = ['x', 'c', 'ctx', 'c_ctx', 'ada_w', 'ada_b', 'norm1_g', 'norm2_g', 'w_in', 'rwkv_shift_mu', 'rwkv_w0',
          'rwkv_w2', 'rwkv_a0', 'rwkv_a2', 'rwkv_g2', 'rwkv_k_k', 'rwkv_k_a', 'rwkv_r_k', 'rwkv_ln_w', 'rwkv_ln_b',
          'diff_lambda', 'diff_subln_g', 'mla_q_norm_g', 'mla_kv_norm_g', 'mla_w_uq', 'mla_w_uk', 'mla_w_uv',
          'w_branch', 'w_out', 'ffn_w_gate', 'ffn_w_up', 'ffn_w_down', 'final_norm_g']


def program(new_bass, shapes):
    plan = None
    for _ in range(2):
        nc = new_bass()
        plan = Plan(plan)
        w = {n: nc.dram_tensor(f"in_{n}", s, F32, kind="ExternalInput").ap() for n, s in shapes.items()}
        tab = nc.dram_tensor("in_tables", (P, NTAB), F32, kind="ExternalInput").ap()
        out = nc.dram_tensor("out_0", (1, HALF, D), F32, kind="ExternalOutput").ap()
        with ExitStack() as ctx:
            build(nc, w, tab, out, plan, ctx)
    return nc


def kernel(**inputs):
    import concourse.bacc as bacc
    from concourse.bass_utils import run_bass_kernel_spmd

    arrays = {f"in_{n}": np.ascontiguousarray(inputs[n]) for n in _NAMES}
    nc = program(lambda: bacc.Bacc("TRN2", target_bir_lowering=False, num_devices=1),
                 {n: tuple(inputs[n].shape) for n in _NAMES})
    arrays["in_tables"] = tables()
    return run_bass_kernel_spmd(nc, [arrays], core_ids=[0]).results[0]["out_0"]
```
